# Optimizing a Trainium2 kernel written in Bass

```python
import math
import jax
import jax.numpy as jnp
from jax import lax
import numpy as np

D_MODEL = 1024
BATCH = 1
SEQ = 512
DEPTH = 1
DEC_BATCH = 1
DEC_SEQ = 64
PAST_LEN = 128

CHUNK = 64
Q_BLOCK = 128
ROPE_THETA = 500000.0
EPS = 1e-6
H_A = 8
Q_LORA = 384
KV_LORA = 256
QK_NOPE = 64
QK_ROPE = 32
V_A = 128
MLA_SCALE = 1.0 / math.sqrt(QK_NOPE + QK_ROPE)
H_B = 8
D_B = 64
V_B = 2 * D_B
ROT_B = D_B // 4
DIFF_SCALE = 1.0 / math.sqrt(D_B)
N_GROUPS = 4
EXP_PER_GROUP = 8
N_EXPERTS = N_GROUPS * EXP_PER_GROUP
TOP_K_IN_GROUP = 2
D_EXPERT = 256
D_PLE = 256
IN_SIZES = (Q_LORA, KV_LORA, QK_ROPE, H_B * 2 * D_B, H_B * 2 * D_B, H_B * V_B, D_MODEL, D_MODEL)
IN_COLS = sum(IN_SIZES)
IN_OFFSETS = tuple(sum(IN_SIZES[:i + 1]) for i in range(len(IN_SIZES) - 1))

kernel_name = 'hybrid_mla_diffattn_hmoe_stream_step'

def _rms(x, g):
    xf = x.astype(jnp.float32)
    y = xf * lax.rsqrt(jnp.mean(xf * xf, axis=-1, keepdims=True) + EPS)
    return (y * g.astype(jnp.float32)).astype(x.dtype)

def _rope(x, pos):
    r = x.shape[-1]
    half = r // 2
    inv = ROPE_THETA ** (-jnp.arange(half, dtype=jnp.float32) * (2.0 / r))
    ang = pos.astype(jnp.float32)[:, None] * inv[None, :]
    ang = ang.reshape((1, pos.shape[0]) + (1,) * (x.ndim - 3) + (half,))
    c, s = jnp.cos(ang), jnp.sin(ang)
    xf = x.astype(jnp.float32)
    x1, x2 = xf[..., :half], xf[..., half:]
    return jnp.concatenate([x1 * c - x2 * s, x2 * c + x1 * s], axis=-1).astype(x.dtype)

def _partial_rope(x, pos, rot):
    return jnp.concatenate([_rope(x[..., :rot], pos), x[..., rot:]], axis=-1)

def _chunk_mask(q_pos, k_pos):
    return (k_pos[None, :] // CHUNK) <= (q_pos[:, None] // CHUNK)

def _over_query_blocks(fn, qs, q_pos):
    sq = q_pos.shape[0]
    if sq <= Q_BLOCK or sq % Q_BLOCK != 0:
        return fn(qs, q_pos)
    nb = sq // Q_BLOCK
    qs_b = tuple(jnp.moveaxis(q.reshape((q.shape[0], nb, Q_BLOCK) + q.shape[2:]), 1, 0) for q in qs)
    out = lax.map(lambda a: fn(a[0], a[1]), (qs_b, q_pos.reshape(nb, Q_BLOCK)))
    out = jnp.moveaxis(out, 0, 1)
    return out.reshape((out.shape[0], sq) + out.shape[3:])

def _hier_moe(x, w_rg, b_rg, w_re, b_re, w_ei, w_eo):
    n = x.shape[0]
    p_grp = jax.nn.softmax((x @ w_rg).astype(jnp.float32) + b_rg.astype(jnp.float32), axis=-1)
    p_top, g_sel = lax.top_k(p_grp, 1)
    le = ((x @ w_re).astype(jnp.float32) + b_re.astype(jnp.float32)).reshape(n, N_GROUPS, EXP_PER_GROUP)
    le = jnp.take_along_axis(le, g_sel[:, :, None], axis=1)[:, 0]
    v_top, i_top = lax.top_k(le, TOP_K_IN_GROUP)
    w_top = jax.nn.softmax(v_top, axis=-1) * p_top
    e_id = g_sel * EXP_PER_GROUP + i_top
    gate = jnp.sum(jax.nn.one_hot(e_id, N_EXPERTS, dtype=jnp.float32) * w_top[..., None], axis=1).astype(x.dtype)
    y = jnp.zeros_like(x)
    for e in range(N_EXPERTS):
        a, b = jnp.split(x @ w_ei[e], 2, axis=-1)
        y = y + gate[:, e:e + 1] * ((jax.nn.silu(a) * b) @ w_eo[e])
    return y

def _layer(x, pe, pos, past, w, lam_init):
    b, s, _ = x.shape
    xn = _rms(x, w['g_mix'])
    z = xn @ w['w_in']
    q_lat, c_kv, kr_raw, dq, dk, dv, ga, gb = jnp.split(z, IN_OFFSETS, axis=-1)

    q = (_rms(q_lat, w['g_q_lat']) @ w['w_uq']).reshape(b, s, H_A, QK_NOPE + QK_ROPE)
    q_nope = _rms(q[..., :QK_NOPE], w['g_mla_qn'])
    q_rope = _rope(_rms(q[..., QK_NOPE:], w['g_mla_qr']), pos)
    ckv = _rms(c_kv, w['g_kv_lat'])
    krope = _rope(_rms(kr_raw, w['g_mla_kr']), pos)

    dq = _partial_rope(_rms(dq.reshape(b, s, H_B, 2, D_B), w['g_diff_q']), pos, ROT_B)
    dk = _partial_rope(_rms(dk.reshape(b, s, H_B, 2, D_B), w['g_diff_k']), pos, ROT_B)
    dv = dv.reshape(b, s, H_B, V_B)

    if past is None:
        ckv_all, kr_all, dk_all, dv_all, k_pos = ckv, krope, dk, dv, pos
    else:
        ckv_p, kr_p, dk_p, dv_p = past
        ckv_all = jnp.concatenate([ckv_p, ckv], axis=1)
        kr_all = jnp.concatenate([kr_p, krope], axis=1)
        dk_all = jnp.concatenate([dk_p, dk], axis=1)
        dv_all = jnp.concatenate([dv_p, dv], axis=1)
        k_pos = jnp.concatenate([jnp.arange(ckv_p.shape[1], dtype=jnp.int32), pos])

    k_nope = _rms((ckv_all @ w['w_uk']).reshape(b, -1, H_A, QK_NOPE), w['g_mla_kn'])
    v_a = (ckv_all @ w['w_uv']).reshape(b, -1, H_A, V_A)

    def mla_fn(qs, qp):
        qn, qr = qs
        sc = (jnp.einsum('bqhd,bkhd->bhqk', qn, k_nope)
              + jnp.einsum('bqhr,bkr->bhqk', qr, kr_all)).astype(jnp.float32) * MLA_SCALE
        sc = jnp.where(_chunk_mask(qp, k_pos), sc, -jnp.inf)
        pr = jax.nn.softmax(sc, axis=-1).astype(v_a.dtype)
        return jnp.einsum('bhqk,bkhd->bqhd', pr, v_a)

    o_a = _over_query_blocks(mla_fn, (q_nope, q_rope), pos).reshape(b, s, H_A * V_A)

    lam = (jnp.exp(jnp.sum(w['lambda_q1'].astype(jnp.float32) * w['lambda_k1'].astype(jnp.float32)))
           - jnp.exp(jnp.sum(w['lambda_q2'].astype(jnp.float32) * w['lambda_k2'].astype(jnp.float32)))
           + lam_init)

    def diff_fn(qs, qp):
        (qb,) = qs
        sc = jnp.einsum('bqhcd,bkhcd->bchqk', qb, dk_all).astype(jnp.float32) * DIFF_SCALE
        sc = jnp.where(_chunk_mask(qp, k_pos), sc, -jnp.inf)
        pr = jax.nn.softmax(sc, axis=-1)
        att = (pr[:, 0] - lam * pr[:, 1]).astype(dv_all.dtype)
        return jnp.einsum('bhqk,bkhd->bqhd', att, dv_all)

    o_b = _over_query_blocks(diff_fn, (dq,), pos)
    o_b = (_rms(o_b, w['g_diff_sub']) * (1.0 - lam_init)).reshape(b, s, H_B * V_B)

    merged = jax.nn.sigmoid(ga) * o_a + jax.nn.sigmoid(gb) * o_b
    h = x + merged @ w['w_out']

    hn = _rms(h, w['g_ffn']).reshape(b * s, D_MODEL)
    h = h + _hier_moe(hn, w['w_router_grp'], w['b_router_grp'], w['w_router_exp'], w['b_router_exp'],
                      w['w_exp_in'], w['w_exp_out']).reshape(b, s, D_MODEL)

    h = h + jax.nn.sigmoid(_rms(h, w['g_ple']) @ w['w_ple_gate']) * (pe @ w['w_ple_proj'])
    return h, (ckv, krope, dk, dv)

def setup_inputs(seed: int = 0) -> dict:
    key = jax.random.key(seed)
    ks = iter(jax.random.split(key, 64))
    f32 = jnp.float32

    def nrm(shape, fan_in=None, scale=None):
        sc = scale if scale is not None else fan_in ** -0.5
        return jax.random.normal(next(ks), shape, f32) * sc

    def gain(shape):
        return 1.0 + 0.02 * jax.random.normal(next(ks), shape, f32)

    L = DEPTH
    return {
        'x_prompt': nrm((BATCH, SEQ, D_MODEL), scale=1.0),
        'x_sample': nrm((DEC_BATCH, DEC_SEQ, D_MODEL), scale=1.0),
        'p_prompt': nrm((L, BATCH, SEQ, D_PLE), scale=1.0),
        'p_sample': nrm((L, DEC_BATCH, DEC_SEQ, D_PLE), scale=1.0),
        'cache_mla_ckv': nrm((L, DEC_BATCH, PAST_LEN, KV_LORA), scale=1.0),
        'cache_mla_krope': nrm((L, DEC_BATCH, PAST_LEN, QK_ROPE), scale=1.0),
        'cache_diff_k': nrm((L, DEC_BATCH, PAST_LEN, H_B, 2, D_B), scale=1.0),
        'cache_diff_v': nrm((L, DEC_BATCH, PAST_LEN, H_B, V_B), scale=1.0),
        'g_mix': gain((L, D_MODEL)),
        'w_in': nrm((L, D_MODEL, IN_COLS), D_MODEL),
        'g_q_lat': gain((L, Q_LORA)),
        'w_uq': nrm((L, Q_LORA, H_A * (QK_NOPE + QK_ROPE)), Q_LORA),
        'g_kv_lat': gain((L, KV_LORA)),
        'w_uk': nrm((L, KV_LORA, H_A * QK_NOPE), KV_LORA),
        'w_uv': nrm((L, KV_LORA, H_A * V_A), KV_LORA),
        'g_mla_qn': gain((L, QK_NOPE)),
        'g_mla_qr': gain((L, QK_ROPE)),
        'g_mla_kn': gain((L, QK_NOPE)),
        'g_mla_kr': gain((L, QK_ROPE)),
        'g_diff_q': gain((L, D_B)),
        'g_diff_k': gain((L, D_B)),
        'lambda_q1': nrm((L, D_B), scale=0.1),
        'lambda_k1': nrm((L, D_B), scale=0.1),
        'lambda_q2': nrm((L, D_B), scale=0.1),
        'lambda_k2': nrm((L, D_B), scale=0.1),
        'g_diff_sub': gain((L, V_B)),
        'w_out': nrm((L, D_MODEL, D_MODEL), D_MODEL),
        'g_ffn': gain((L, D_MODEL)),
        'w_router_grp': nrm((L, D_MODEL, N_GROUPS), D_MODEL),
        'b_router_grp': nrm((L, N_GROUPS), scale=0.01),
        'w_router_exp': nrm((L, D_MODEL, N_EXPERTS), D_MODEL),
        'b_router_exp': nrm((L, N_EXPERTS), scale=0.01),
        'w_exp_in': nrm((L, N_EXPERTS, D_MODEL, 2 * D_EXPERT), D_MODEL),
        'w_exp_out': nrm((L, N_EXPERTS, D_EXPERT, D_MODEL), D_EXPERT),
        'g_ple': gain((L, D_MODEL)),
        'w_ple_gate': nrm((L, D_MODEL, D_MODEL), D_MODEL),
        'w_ple_proj': nrm((L, D_PLE, D_MODEL), D_PLE),
    }

def reference(x_prompt, x_sample, p_prompt, p_sample, cache_mla_ckv, cache_mla_krope, cache_diff_k, cache_diff_v,
              g_mix, w_in, g_q_lat, w_uq, g_kv_lat, w_uk, w_uv, g_mla_qn, g_mla_qr, g_mla_kn, g_mla_kr,
              g_diff_q, g_diff_k, lambda_q1, lambda_k1, lambda_q2, lambda_k2, g_diff_sub, w_out,
              g_ffn, w_router_grp, b_router_grp, w_router_exp, b_router_exp, w_exp_in, w_exp_out,
              g_ple, w_ple_gate, w_ple_proj):
    pos_p = jnp.arange(x_prompt.shape[1], dtype=jnp.int32)
    pos_s = cache_mla_ckv.shape[2] + jnp.arange(x_sample.shape[1], dtype=jnp.int32)
    hp, hs = x_prompt, x_sample
    ckv_p, kr_p, dk_p, dv_p = [], [], [], []
    ckv_s, kr_s, dk_s, dv_s = [], [], [], []
    for l in range(DEPTH):
        w = {
            'g_mix': g_mix[l], 'w_in': w_in[l], 'g_q_lat': g_q_lat[l], 'w_uq': w_uq[l],
            'g_kv_lat': g_kv_lat[l], 'w_uk': w_uk[l], 'w_uv': w_uv[l],
            'g_mla_qn': g_mla_qn[l], 'g_mla_qr': g_mla_qr[l], 'g_mla_kn': g_mla_kn[l], 'g_mla_kr': g_mla_kr[l],
            'g_diff_q': g_diff_q[l], 'g_diff_k': g_diff_k[l],
            'lambda_q1': lambda_q1[l], 'lambda_k1': lambda_k1[l], 'lambda_q2': lambda_q2[l], 'lambda_k2': lambda_k2[l],
            'g_diff_sub': g_diff_sub[l], 'w_out': w_out[l], 'g_ffn': g_ffn[l],
            'w_router_grp': w_router_grp[l], 'b_router_grp': b_router_grp[l],
            'w_router_exp': w_router_exp[l], 'b_router_exp': b_router_exp[l],
            'w_exp_in': w_exp_in[l], 'w_exp_out': w_exp_out[l],
            'g_ple': g_ple[l], 'w_ple_gate': w_ple_gate[l], 'w_ple_proj': w_ple_proj[l],
        }
        lam_init = 0.8 - 0.6 * math.exp(-0.3 * l)
        hp, st_p = _layer(hp, p_prompt[l], pos_p, None, w, lam_init)
        hs, st_s = _layer(hs, p_sample[l], pos_s,
                          (cache_mla_ckv[l], cache_mla_krope[l], cache_diff_k[l], cache_diff_v[l]), w, lam_init)
        ckv_p.append(st_p[0]); kr_p.append(st_p[1]); dk_p.append(st_p[2]); dv_p.append(st_p[3])
        ckv_s.append(st_s[0]); kr_s.append(st_s[1]); dk_s.append(st_s[2]); dv_s.append(st_s[3])
    return (hp, hs,
            jnp.stack(ckv_p), jnp.stack(kr_p), jnp.stack(dk_p), jnp.stack(dv_p),
            jnp.stack(ckv_s), jnp.stack(kr_s), jnp.stack(dk_s), jnp.stack(dv_s))


_drawn_inputs = setup_inputs


def setup_inputs(seed=0):
    import zlib

    import numpy as np

    out = dict(_drawn_inputs(seed))
    spreads = {}
    factors = {'g_q_lat': 8.0,
     'g_kv_lat': 2.98,
     'g_mla_qn': 8.0,
     'g_mla_qr': 36.485,
     'g_mla_kn': 8.0,
     'g_diff_q': 3.48,
     'g_diff_k': 2.935,
     'lambda_q1': 3.093,
     'lambda_k1': 3.521,
     'g_diff_sub': 11.605,
     'b_router_exp': 7.807,
     'g_ple': 64.0,
     'cache_diff_k': 8.0,
     'cache_diff_v': 8.0,
     'g_ffn': 3.65,
     'b_router_grp': 4.555}
    for name, (base, spread) in spreads.items():
        noise = np.random.default_rng([zlib.crc32(name.encode()), seed]).standard_normal(out[name].shape)
        drawn = base * np.exp(spread * noise) if base else spread * noise
        out[name] = jnp.asarray(drawn.astype(out[name].dtype))
    for name, factor in factors.items():
        out[name] = (out[name] * factor).astype(out[name].dtype)
    return out
```

```python
import math
from contextlib import ExitStack

import numpy as np
import concourse.bass as bass
from concourse import mybir

F32 = mybir.dt.float32
F32R = mybir.dt.float32r
I32 = mybir.dt.int32
U32 = mybir.dt.uint32
ACT = mybir.ActivationFunctionType
ALU = mybir.AluOpType
AX = mybir.AxisListType

P = 128
D = 1024
SEQ, DEC, PAST = 512, 64, 128
CHUNK = 64
PT = SEQ // P
TILES = PT + 1
ROWS = [P] * PT + [DEC]
TOK = TILES * P
CACHE = TILES
KEYS = SEQ + PAST + DEC
KCOL = [t * P for t in range(PT)] + [SEQ + PAST, SEQ]
EPS = 1e-6
H = 8
QL, KVL, NOPE, RD = 384, 256, 64, 32
HD = NOPE + RD
MLA_SCALE = 1.0 / math.sqrt(HD)
DB = 64
VB = 128
ROT = DB // 4
DIFF_SCALE = 1.0 / math.sqrt(DB)
LAM_INIT = 0.8 - 0.6 * math.exp(-0.3 * 0)
NG, EPG = 4, 8
NE = NG * EPG
DE = 256
DP = 256
NBLK = NE + (2 * (SEQ + DEC) - NE) // P
REAL = SEQ + DEC
NASSIGN = 2 * REAL
BIG = 1e30
ROPE_THETA = 500000.0


class Item:

    def __init__(self, name, kind, src, col, width, kt, tiles, lhs, split, half=0):
        self.name, self.kind, self.src, self.col, self.width = name, kind, src, col, width
        self.kt, self.tiles, self.lhs, self.split, self.half = kt, tiles, lhs, split, half


def plan():
    first = [Item("q_lat", "norm", "w_in", 0, QL, 8, TILES, "act", True),
             Item("ckv", "norm", "w_in", QL, KVL + RD, 8, TILES, "act", True)]
    at = QL + KVL + RD
    for name, kind in (("dq", "norm"), ("dk", "norm"), ("dv", "store"), ("ga", "gate"), ("gb", "gate")):
        for half in range(2):
            first.append(Item(name, kind, "w_in", at, 512, 8, TILES, "act", True, half))
            at += 512
    latent = [Item("uq", "norm", "w_uq", 384 * half, 384, 3, TILES, "q_lat", False, half) for half in range(2)]
    latent += [Item("uk", "norm", "w_uk", 0, 512, 2, TILES + 1, "ckv", False)]
    latent += [Item("uv", "store", "w_uv", 512 * half, 512, 2, TILES + 1, "ckv", False, half) for half in range(2)]
    out = [Item("out", "residual", "w_out", 512 * half, 512, 8, TILES, "act", True, half) for half in range(2)]
    ple = [Item("proj", "store", "w_ple_proj", 512 * half, 512, 2, TILES, "pe", True, half) for half in range(2)]
    ple += [Item("pgate", "ple", "w_ple_gate", 512 * half, 512, 8, TILES, "act", True, half) for half in range(2)]
    return first, latent, out, ple


def number(keys):
    return {k: i for i, k in enumerate(keys)}


def trunk(nc, a, o):
    first, latent, outp, ple = plan()
    phases = [first, latent, outp, ple]
    items = [c for ph in phases for c in ph]
    start = {id(ph): sum(len(x) for x in phases[:i]) for i, ph in enumerate(phases)}

    units = number([(i, t) for i, c in enumerate(items) for t in range(c.tiles)])
    granules = number([(i, g) for i, c in enumerate(items) if c.split for g in range(c.kt // 2)])
    normed = number([(i, t) for i, c in enumerate(items) if c.kind == "norm" for t in range(c.tiles)])
    normitems = number([i for i, c in enumerate(items) if c.kind == "norm"])
    RAW, RING = 3, 2
    EG, ERING = 12, 6
    PAIRS = (NBLK + 1) // 2

    def subs(i):
        c = items[i]
        return 2 if c.name == "uk" else 1 if c.kind == "norm" else 0

    tgroups = [("x", t, s) for t in range(TILES) for s in range(2)]
    tgroups += [("cache_k", 0, 0), ("cache_k", 0, 1), ("cache_ckv", 0, 0)]
    tgroups += [(i, t, s) for i in range(len(first)) for t in range(items[i].tiles) for s in range(subs(i))]
    tgroups += [("attn_b", n, 0) for n in range(H * TILES)]
    tgroups += [(i, t, s) for i in range(len(first), len(first) + len(latent))
                for t in range(items[i].tiles) for s in range(subs(i))]
    tgroups += [("attn_a", n, 0) for n in range(H * TILES)]
    tgroups += [("merged", t, s) for t in range(TILES) for s in range(2)]
    tgroups += [("hn", t, s) for t in range(TILES) for s in range(2)]
    tgroups += [("pe", t, 0) for t in range(TILES)]
    tgroups += [("hp", t, s) for t in range(TILES) for s in range(2)]
    tg = number(tgroups)

    with ExitStack() as ctx:
        def sb(name, shape, dt=F32, c=ctx):
            return c.enter_context(nc.sbuf_tensor(name, shape, dt))

        def sem(name):
            return ctx.enter_context(nc.semaphore(name))

        def dram(name, shape, dt=F32):
            return nc.dram_tensor(name, shape, dt, kind="Internal").ap()

        acc = ctx.enter_context(nc.psum_tensor("acc", [P, 6, 512], F32))
        tp = ctx.enter_context(nc.psum_tensor("tp", [P, 2, 512], F32))

        va_rows = dram("va_rows", [TOK + P, D])
        hn_rows = dram("hn_rows", [REAL, D])
        y_rows = dram("y_rows", [NASSIGN, D])

        ident = sb("ident", [P, P])
        small = sb("small", [P, 512])
        raw = sb("raw", [P, RAW, 2, 512])
        whi = sb("whi", [P, RING, 2, 512], F32R)
        wlo = sb("wlo", [P, RING, 2, 512], F32R)
        grow = sb("grow", [P, D])
        neghalf = sb("neghalf", [P, 64])

        mask = sb("mask", [1, P + 64])
        rope = sb("rope", [P, TILES, 96])
        zs = sb("zs", [P, 6, 512])
        sq = sb("sq", [P, 512])
        rot = sb("rot", [P, 2, 128])

        early = ExitStack()
        gates = sb("gates", [P, TILES, 2 * D], c=early)
        q_latT = sb("q_latT", [P, 3, TOK], c=early)
        ckvT = sb("ckvT", [P, 2, TOK + P], c=early)
        krope = sb("krope", [P, 6, RD], c=early)
        qT = sb("qT", [P, H, SEQ + DEC], c=early)
        kT = sb("kT", [P, H, KEYS], c=early)
        vh = sb("vh", [P, 2, 6, VB], c=early)
        gq_lat = sb("gq_lat", [P, QL], c=early)
        gkv = sb("gkv", [P, KVL + RD], c=early)
        gvec = sb("gvec", [P, 6, P], c=early)
        halves = ExitStack()
        lhi = sb("lhi", [P, 8, TOK], F32R, c=halves)
        llo = sb("llo", [P, 8, TOK], F32R, c=halves)
        halves.close()
        inner = ExitStack()
        w_uq = sb("w_uq", [P, 3, 768], c=inner)
        w_uk = sb("w_uk", [P, 2, 512], c=inner)
        w_uv = sb("w_uv", [P, 2, 1024], c=inner)
        pr = sb("pr", [P, 2, 2, 512], c=inner)
        prT = sb("prT", [P, 2, 4, P], c=inner)
        inner.close()
        halves2 = ExitStack()
        lhi2 = sb("lhi2", [P, 8, TOK], F32R, c=halves2)
        llo2 = sb("llo2", [P, 8, TOK], F32R, c=halves2)
        halves2.close()
        early.close()
        h = sb("h", [P, TILES, D])
        src_row = sb("src_row", [P, NBLK + 2], I32)
        dst_row = sb("dst_row", [P, NBLK + 2], I32)
        gate_of = sb("gate_of", [P, NBLK + 2])
        expert_of = sb("expert_of", [1, NBLK + 2], I32)
        n_blocks = sb("n_blocks", [1, 2], I32)
        row_in = sb("row_in", [P, 2, 1], I32)
        row_out = sb("row_out", [P, 2, 1], I32)
        gate_in = sb("gate_in", [P, 2, 1])
        raw_e = sb("raw_e", [P, EG, D])
        route = ExitStack()
        xn = sb("xn", [P, 2, D], c=route)
        xnT = sb("xnT", [P, 2, 8, P], c=route)
        w_r = sb("w_r", [P, 8, NG + NE], c=route)
        b_r = sb("b_r", [P, NG + NE], c=route)
        iota = sb("iota", [P, 320], c=route)
        token = sb("token", [P, TILES, 3], c=route)
        before = sb("before", [P, P], c=route)
        ones = sb("ones", [P, P], c=route)
        rt = sb("rt", [P, 3008], c=route)
        route.close()
        moe = ExitStack()
        ehi = sb("ehi", [P, ERING, D], F32R, c=moe)
        elo = sb("elo", [P, ERING, D], F32R, c=moe)
        xg = sb("xg", [P, 2, D], c=moe)
        xhi = sb("xhi", [P, 2, 8, P], F32R, c=moe)
        xlo = sb("xlo", [P, 2, 8, P], F32R, c=moe)
        gg = sb("gg", [P, 2, DE], c=moe)
        ghi = sb("ghi", [P, 2, 2, P], F32R, c=moe)
        glo = sb("glo", [P, 2, 2, P], F32R, c=moe)
        ye = zs[:, 0:4, :].rearrange("p (b a) n -> p b (a n)", b=2)
        moe.close()
        tail = ExitStack()
        ptok = sb("ptok", [P, TILES, DP], c=tail)
        phi = sb("phi", [P, 2, TOK], F32R, c=tail)
        plo = sb("plo", [P, 2, TOK], F32R, c=tail)
        ysum = raw_e[:, 0:4, :].rearrange("p (b j) n -> p b j n", b=2)
        hp = raw_e[:, 4:6, :]
        pj = raw_e[:, 6:11, :]
        grow2 = raw_e[:, 11, :]
        tail.close()

        def part(at, n):
            return small[:, at:at + n]

        ss_z = [part(0, 48), part(48, 48)]
        r_z = [part(96, 48), part(144, 48)]
        ss_x, r_x = part(192, 5), part(200, 5)
        ss_o, r_o = part(208, 40), part(248, 40)
        negmax, sums, rsum = part(288, 4), part(292, 4), part(296, 8)
        lamv = part(304, 8)
        pair = part(312, 2)

        ld_const = sem("ld_const")
        ld_x = [sem(f"ld_x{t}") for t in range(TILES)]
        ld_raw = [sem(f"ld_raw{s}") for s in range(RAW)]
        ld_v = [sem(f"ld_v{s}") for s in range(2)]
        ld_wu = sem("ld_wu")
        zeroed = sem("zeroed")
        hi_done, lo_done, w_used = sem("hi_done"), sem("lo_done"), sem("w_used")
        z_done, z_copied = sem("z_done"), sem("z_copied")
        sq_done, ss_done, rstd_done, y_done = sem("sq_done"), sem("ss_done"), sem("rstd_done"), sem("y_done")
        t_done, t_copied, hi_copied, pt_copied = sem("t_done"), sem("t_copied"), sem("hi_copied"), sem("pt_copied")
        x_sq, x_rstd, xn_done = sem("x_sq"), sem("x_rstd"), sem("xn_done")
        outz = [sem(f"outz{t}") for t in range(6)]
        lam_dots, lam_exp, lam_done = sem("lam_dots"), sem("lam_exp"), sem("lam_done")
        s_done = {p: sem(f"s_done_{p}") for p in "ba"}
        nm_done = {p: sem(f"nm_done_{p}") for p in "ba"}
        exp_done = {p: sem(f"exp_done_{p}") for p in "ba"}
        pv_done = {p: sem(f"pv_done_{p}") for p in "ba"}
        o_done = {p: sem(f"o_done_{p}") for p in "ba"}
        comb_done = {p: sem(f"comb_done_{p}") for p in "ba"}
        sqo_done, ro_done = sem("sqo_done"), sem("ro_done")
        merged_done = sem("merged_done")
        ld_h = sem("ld_h")
        dve_own, act_own, pool_own = sem("dve_own"), sem("act_own"), sem("pool_own")

        copied = number([k for k in tgroups if k[0] not in ("attn_b", "attn_a")])
        pt = number([k for k in tgroups if k[0] in ("attn_b", "attn_a")])

        def wait_group_copied(eng, key):
            if key in copied:
                eng.wait_ge(t_copied, copied[key] + 1)
            else:
                eng.wait_ge(pt_copied, pt[key] + 1)

        def wait_bank_for(eng, key):
            if tg[key] >= 2:
                wait_group_copied(eng, tgroups[tg[key] - 2])

        def dmas_of(i):
            return {"ckv": 2, "dk": 1, "dv": 1, "uv": 1}.get(items[i].name, 0)

        def out_count(i, t):
            return sum(dmas_of(n) for n in range(i + 1) if items[n].tiles > t)

        def uses_zs(i):
            return items[i].kind in ("norm", "residual", "ple") or items[i].name in ("dv", "uv")

        def wait_slot_free(eng, i, t):
            before = [n for n in range(i) if uses_zs(n) and items[n].tiles > t]
            if not before:
                return
            n = before[-1]
            c = items[n]
            if c.kind == "norm" and c.name != "uk":
                eng.wait_ge(t_done, tg[(n, t, subs(n) - 1)] + 1)
            if c.name == "uk":
                eng.wait_ge(y_done, y_index[(n, t)] + 1)
            if c.kind in ("residual", "ple"):
                eng.wait_ge(y_done, y_index[(n, t)] + 1)
            if out_count(n, t):
                eng.wait_ge(outz[t], 16 * out_count(n, t))

        y_norm = number([(i, t) for i, c in enumerate(items) if c.kind == "norm" for t in range(c.tiles)])

        def y_norm_of_phase(ph):
            return sum(c.tiles for x in phases[:phases.index(ph) + 1] for c in x if c.kind == "norm")

        hi_index = number([k for k in tgroups if k[0] in ("x", "merged", "pe", "hp")])
        y_index = number([(i, t) for i, c in enumerate(items) if c.kind in ("norm", "residual", "ple")
                          for t in range(c.tiles)])

        def groups(i):
            return {"q_lat": [(0, 1, QL, QL, 1.0)],
                    "ckv": [(0, 1, KVL, KVL, 1.0), (KVL, 1, RD, RD, 1.0)],
                    "dq": [(0, 8, DB, DB, DIFF_SCALE ** 2)],
                    "dk": [(0, 8, DB, DB, 1.0)],
                    "uq": [(0, 4, NOPE, HD, 1.0 / HD), (NOPE, 4, RD, HD, 1.0 / HD)],
                    "uk": [(0, 8, NOPE, NOPE, 1.0)]}[items[i].name]

        def grouped(tile, g):
            off, n, size, stride, _ = g
            if n == 1:
                return tile[:, off:off + size].unsqueeze(1)
            return tile[:, 0:n * stride].rearrange("p (n s) -> p n s", s=stride)[:, :, off % stride:off % stride + size]

        inner_granules = number([k for k in granules if k[1] < items[k[0]].kt // 2 - 1])
        granule_list = list(granules)

        def wait_ring_free(eng, n):
            if n < RING:
                return
            i, g = granule_list[n - RING]
            if (i, g) in inner_granules:
                eng.wait_ge(w_used, inner_granules[(i, g)] + 1)
            else:
                eng.wait_ge(z_done, units[(i, items[i].tiles - 1)] + 1)

        def phase_items(ph):
            return range(start[id(ph)], start[id(ph)] + len(ph))

        ds = bass.ds
        ss_h, r_h = part(320, 5), part(328, 5)
        ss_f, r_f = part(336, 5), part(344, 5)
        h_sq, h_rstd, hn_done, hn_sent = sem("h_sq"), sem("h_rstd"), sem("hn_done"), [sem(f"hn_sent{j}") for j in range(2)]
        ld_g, ld_late = sem("ld_g"), sem("ld_late")
        ones_set = sem("ones_set")
        logits_done, grp_shift, grp_exp, exp2_in, exp2_out = (
            sem("logits_done"), sem("grp_shift"), sem("grp_exp"), sem("exp2_in"), sem("exp2_out"))
        hot_done, rank_done, plan_in, plan_done, routed = (
            sem("hot_done"), sem("rank_done"), sem("plan_in"), sem("plan_done"), sem("routed"))
        ld_e = [sem(f"ld_e{j}") for j in range(EG)]
        ld_xg = [sem(f"ld_xg{j}") for j in range(2)]
        hi_e, lo_e, used_e, t_e, thi_e, tlo_e = (sem("hi_e"), sem("lo_e"), sem("used_e"), sem("t_e"), sem("thi_e"),
                                                 sem("tlo_e"))
        silu_e, g_e, ya_e, yd_e, sent_e = (sem("silu_e"), sem("g_e"), sem("ya_e"), sem("yd_e"),
                                           [sem(f"sent_e{j}") for j in range(2)])
        gate_e, own_e = sem("gate_e"), sem("own_e")
        left_e = sem("left_e")
        pool_steps = sem("pool_steps")
        moe_done = sem("moe_done")
        ld_y, y_added, f_sq, f_rstd, fn_done, ld_p = (
            [sem(f"ld_y{j}") for j in range(2)], sem("y_added"), sem("f_sq"), sem("f_rstd"), sem("fn_done"), sem("ld_p"))
        st_y = sem("st_y")
        ORDER = [(0, g) for g in range(4)] + [(1, g) for g in range(4)] + [(0, 4), (0, 5), (1, 4), (1, 5)]
        residual_last = start[id(outp)] + 1
        ple_first = start[id(ple)]

        def late_sync(sp):
            for dst, src in ((w_r[:, :, 0:NG], a["w_rg"].rearrange("(k p) n -> p k n", p=P)),
                             (w_r[:, :, NG:NG + NE], a["w_re"].rearrange("(k p) n -> p k n", p=P)),
                             (b_r[:, 0:NG], a["b_rg"].partition_broadcast(P)),
                             (b_r[:, NG:NG + NE], a["b_re"].partition_broadcast(P)),
                             (iota[:, :], a["c_iota"].partition_broadcast(P)),
                             (token[:, :, :], a["c_token"].rearrange("(t p) n -> p t n", p=P)),
                             (before[:, :], a["c_before"])):
                sp.dma_start(dst, src).then_inc(ld_late, 16)
            every = [(i, g) for i in phase_items(ple) for g in range(items[i].kt // 2)]
            for i, g in every[:RAW]:
                load_granule(sp, i, g)
            sp.wait_ge(routed, 1)
            n = sp.value_load(n_blocks[0:1, 0:1], min_val=1, max_val=NBLK)
            with sp.Fori(0, PAIRS) as i:
                with sp.If(i * 2 < n):
                    e = [sp.value_load(expert_of[0:1, ds(i * 2 + j, 1)], min_val=0, max_val=NE - 1) for j in range(2)]
                    for q, (b, g) in enumerate(ORDER):
                        if g < 4:
                            src = a["w_ei"][ds(e[b] * D + 2 * g * P, 2 * P), :].rearrange("(k p) n -> p k n", p=P)
                            dst = raw_e[:, q, :].rearrange("p (k n) -> p k n", k=2)
                        else:
                            src = a["w_eo"][ds(e[b] * DE + (g - 4) * P, P), :]
                            dst = raw_e[:, q, :]
                        sp.wait_ge(lo_e, i * EG + (q + 1))
                        sp.dma_start(dst, src).then_inc(ld_e[q], 16)
            sp.wait_ge(moe_done, 1)
            sp.dma_start(grow2, a["g_ple"].partition_broadcast(P)).then_inc(ld_g, 16)
            for t in range(TILES):
                if t >= 2:
                    sp.wait_ge(y_added, t - 1)
                sp.dma_start(ysum[0:ROWS[t], t % 2, :, :],
                             y_rows.rearrange("(j n) d -> n j d", j=2)[t * P:t * P + ROWS[t], :, :]
                             ).then_inc(ld_y[t % 2], 16)
                sp.dma_start(ptok[0:ROWS[t], t, :], a["p"][t * P:t * P + ROWS[t], :]).then_inc(ld_p, 16)
            for i, g in every[RAW:]:
                load_granule(sp, i, g)

        def late_tensor(pe, turn, run):
            for t in range(TILES):
                pe.wait_ge(hn_done, t + 1)
                for s in range(2):
                    turn(("hn", t, s), [xn[:, t % 2, j * P:j * P + P] for j in range(4 * s, 4 * s + 4)])
                if t == 0:
                    pe.wait_ge(ld_late, 16 * 7)
                    pe.wait_ge(z_copied, units[(residual_last, TILES - 1)] + 1)
                pe.wait_ge(t_copied, copied[("hn", t, 1)] + 1)
                for k in range(8):
                    mm = pe.matmul(acc[:, t, 0:NG + NE], xnT[:, t % 2, k, :], w_r[:, k, :], start=(k == 0),
                                   stop=(k == 7))
                mm.then_inc(logits_done, 1)
            pe.wait_ge(hot_done, 1)
            pe.wait_ge(ones_set, 1)
            for t in range(TILES):
                for u in range(t + 1):
                    pe.matmul(acc[:, t, 0:NE], (before if u == t else ones)[:, :], R["hot"][:, u, :],
                              start=(u == 0), stop=(u == t))
            for u in range(TILES):
                mm = pe.matmul(acc[:, 5, 0:NE], ones[:, :], R["hot"][:, u, :], start=(u == 0), stop=(u == TILES - 1))
            mm.then_inc(rank_done, 1)
            pe.wait_ge(plan_in, 1)
            for n in range(2 * TILES):
                mm = pe.matmul(acc[:, 0, 0:3 * NBLK], R["in_block"][:, n, :], R["what"][:, n, :], start=(n == 0),
                               stop=(n == 2 * TILES - 1))
            mm.then_inc(plan_done, 1)

            pe.wait_ge(routed, 1)
            pe.sem_inc(used_e, ERING)
            pe.sem_inc(t_e, 6)
            n = pe.value_load(n_blocks[0:1, 0:1], min_val=1, max_val=NBLK)
            with pe.Fori(0, PAIRS) as i:
                with pe.If(i * 2 < n):
                    for b in range(2):
                        pe.wait_ge(ld_xg[b], i * 16 + 16)
                        for s in range(2):
                            pe.wait_ge(tlo_e, i * 6 + (2 * b + s + 1))
                            for j in range(4):
                                k = 4 * s + j
                                tr = pe.transpose(tp[:, s, j * P:j * P + P], xg[:, b, k * P:k * P + P], ident[:, :])
                            tr.then_inc(t_e, 1)

                    def product(q, out, lhs, n0, n1, first_, last_):
                        for x, w in ((0, 0), (0, 1), (1, 0)):
                            mm = pe.matmul(out, lhs[x], (ehi, elo)[w][:, q % ERING, n0:n1],
                                           start=(first_ and x + w == 0), stop=(last_ and x == 1))
                        return mm

                    for b in range(2):
                        pe.wait_ge(tlo_e, i * 6 + (2 * b + 4))
                        pe.wait_ge(g_e, i * 2 + (b + 1))
                        for g in range(4):
                            q = 4 * b + g
                            pe.wait_ge(lo_e, i * EG + (q + 1 + EG))
                            for k in range(2):
                                kk = 2 * g + k
                                mm = product(q, acc[:, b, :], (xhi[:, b, kk, :], xlo[:, b, kk, :]), 512 * k,
                                             512 * k + 512, kk == 0, kk == 7)
                            mm.then_inc(used_e, 1)
                    for b in range(2):
                        pe.wait_ge(g_e, i * 2 + (b + 3))
                        pe.wait_ge(tlo_e, i * 6 + (b + 5))
                        for j in range(2):
                            tr = pe.transpose(tp[:, b, j * P:j * P + P], gg[:, b, j * P:j * P + P], ident[:, :])
                        tr.then_inc(t_e, 1)
                        pe.wait_ge(tlo_e, i * 6 + (b + 7))
                        pe.wait_ge(ya_e, i * 2 + (b + 1))
                        pe.wait_ge(yd_e, i * 2 + (b + 1))
                        for k in range(2):
                            q = 8 + 2 * b + k
                            pe.wait_ge(lo_e, i * EG + (q + 1 + EG))
                            for half in range(2):
                                mm = product(q, acc[:, 2 + 2 * b + half, :], (ghi[:, b, k, :], glo[:, b, k, :]),
                                             512 * half, 512 * half + 512, k == 0, k == 1)
                            mm.then_inc(used_e, 1)

            pe.wait_ge(moe_done, 1)
            pe.wait_ge(ld_p, 16 * TILES)
            pe.wait_ge(zeroed, 3)
            for t in range(TILES):
                turn(("pe", t, 0), [ptok[:, t, j * P:j * P + P] for j in range(2)])
            for t in range(TILES):
                pe.wait_ge(fn_done, t + 1)
                for s in range(2):
                    turn(("hp", t, s), [hp[:, t % 2, j * P:j * P + P] for j in range(4 * s, 4 * s + 4)])
            run(ple)

        def squares_of_h(act, after, done, dst):
            for t in range(TILES):
                after(t)
                if t:
                    act.wait_ge(done, t)
                act.activation(zs[:, 4:6, :].rearrange("p a b -> p (a b)"), h[:, t, :], ACT.Square,
                               accum_out=dst[:, t:t + 1]).then_inc(done, 1)

        def late_scalar(act, link, halve_hi, run):
            squares_of_h(act, lambda t: act.wait_ge(y_done, y_index[(residual_last, TILES - 1)] + 1), h_sq, ss_h)
            act.wait_ge(grp_shift, 1)
            act.activation(R["e_grp"], R["shifted"], ACT.Exp).then_inc(grp_exp, 1)
            act.wait_ge(exp2_in, 1)
            act.activation(R["e2"], R["d2"], ACT.Exp).then_inc(exp2_out, 1)

            act.wait_ge(routed, 1)
            act.wait_ge(h_sq, TILES)
            n = act.value_load(n_blocks[0:1, 0:1], min_val=1, max_val=NBLK)
            with act.Fori(0, PAIRS) as i:
                with act.If(i * 2 < n):
                    def split(q):
                        act.wait_ge(ld_e[q], i * 16 + 16)
                        act.wait_ge(used_e, i * EG + (q + 1))
                        act.activation(ehi[:, q % ERING, :], raw_e[:, q, :], ACT.Copy).then_inc(hi_e, 1)

                    def turned(b, s):
                        act.wait_ge(t_e, i * 6 + (2 * b + s + 7))
                        act.activation(xhi[:, b, 4 * s:4 * s + 4, :],
                                       tp[:, s, :].rearrange("p (k r) -> p k r", r=P), ACT.Copy).then_inc(thi_e, 1)

                    def silu(b):
                        act.wait_ge(used_e, i * EG + (4 * b + 4 + ERING))
                        act.activation(gg[:, b, :], acc[:, b, 0:DE], ACT.Silu).then_inc(silu_e, 1)

                    def turned_g(b):
                        act.wait_ge(t_e, i * 6 + (b + 11))
                        act.activation(ghi[:, b, :, :], tp[:, b, 0:DE].rearrange("p (k r) -> p k r", r=P),
                                       ACT.Copy).then_inc(thi_e, 1)

                    def result(b):
                        act.wait_ge(used_e, i * EG + (2 * b + 10 + ERING))
                        act.wait_ge(gate_e, i * 2 + (b + 1))
                        act.wait_ge(left_e, i * 2 + (b + 1))
                        act.activation(ye[:, b, 0:512], acc[:, 2 + 2 * b, :], ACT.Copy,
                                       scale=gate_in[:, b, :]).then_inc(ya_e, 1)

                    split(0)
                    turned(0, 0)
                    turned(0, 1)
                    split(1)
                    turned(1, 0)
                    turned(1, 1)
                    for q in range(2, 9):
                        split(q)
                    silu(0)
                    for q in range(9, 12):
                        split(q)
                    silu(1)
                    turned_g(0)
                    result(0)
                    turned_g(1)
                    result(1)

            squares_of_h(act, lambda t: act.wait_ge(y_added, t + 1), f_sq, ss_f)
            for t in range(TILES):
                halve_hi("pe", 0, t, 2, phi)
            for t in range(TILES):
                for s in range(2):
                    halve_hi("hp", s, t, 4, lhi2)
            run(ple)

        R, at = {}, 0
        for name, shape in (("lg", (TILES, 8)), ("m8", (TILES, 8)), ("le", (TILES, NE)), ("v8", (TILES, 8)),
                            ("shifted", (TILES, NG)), ("e_grp", (TILES, NG)), ("pen", (TILES, NG)),
                            ("gsum", (TILES,)), ("gidx", (TILES,)), ("d2", (TILES,)), ("e2", (TILES,)),
                            ("idx", (2, TILES)), ("w", (2, TILES)), ("hot1", (2, TILES, NE)), ("hot", (TILES, NE)),
                            ("cnt", (NE,)), ("cum", (NE,)), ("startof", (NE,)), ("slot", (2 * TILES,)),
                            ("nge", (2 * TILES,))):
            n = int(np.prod(shape))
            v = rt[:, at:at + n]
            names = "abc"[:len(shape)]
            if len(shape) > 1:
                v = v.rearrange(f"p ({' '.join(names)}) -> p {' '.join(names)}", **dict(zip(names, shape)))
            R[name] = v
            at += n
        R["i8"] = rt[:, at:at + 8 * TILES].bitcast(U32).rearrange("p (a b) -> p a b", b=8)
        at += 8 * TILES
        base = at
        R["slotbase"] = rt[:, at:at + TILES * NE].rearrange("p (a b) -> p a b", b=NE)
        big = xn[:, :, :].rearrange("p a b -> p (a b)")
        R["in_block"] = big[:, 0:2 * TILES * P].rearrange("p (a b) -> p a b", b=P)
        R["ge"] = big[:, 1280:1280 + 10 * (NBLK + 1)].rearrange("p (a b) -> p a b", b=NBLK + 1)
        bigT = xnT[:, :, :, :].rearrange("p a b c -> p (a b c)")
        R["what"] = bigT[:, 0:10 * 3 * NBLK].rearrange("p (a b) -> p a b", b=3 * NBLK)
        at = base + TILES * NE
        R["oh_blk"] = rt[:, at:at + 10 * NBLK].rearrange("p (a b) -> p a b", b=NBLK)
        at += 10 * NBLK
        R["pl"] = rt[:, at:at + 3 * NBLK].rearrange("p (a b) -> p a b", b=NBLK)
        at += 3 * NBLK
        R["tmp"] = rt[:, at:at + NBLK * NE // 2]
        at += NBLK * NE // 2
        assert at <= 3008, at
        assert 1280 + 10 * (NBLK + 1) <= 2 * D

        def late_vector(dve, link, halve_lo, run):
            io128, io_blk, io_e = iota[:, 0:P], iota[:, P:P + NBLK + 1], iota[:, 192:192 + NE]
            dve.wait_ge(ld_g, 16)
            dve.wait_ge(h_rstd, 1)

            def copy_hn(t):
                for s in range(2):
                    dve.wait_ge(t_done, tg[("hn", t, s)] + 1)
                    if t >= 2:
                        dve.wait_ge(logits_done, t - 1)
                    dve.tensor_copy(xnT[:, t % 2, 4 * s:4 * s + 4, :],
                                    tp[:, tg[("hn", t, s)] % 2, :].rearrange("p (k r) -> p k r", r=P)
                                    ).then_inc(t_copied, 1)

            for t in range(TILES):
                if t >= 2:
                    dve.wait_ge(hn_sent[t % 2], 16 * (t // 2))
                dve.scalar_tensor_tensor(xn[:, t % 2, :], h[:, t, :], r_h[:, t:t + 1], grow[:, :], ALU.mult,
                                         ALU.mult).then_inc(hn_done, 1)
                if t >= 1:
                    copy_hn(t - 1)
            copy_hn(TILES - 1)
            dve.wait_ge(ld_late, 16 * 7)
            for j in range(2):
                dve.wait_ge(hn_sent[j], 16 * ((TILES - j + 1) // 2))
            dve.wait_ge(logits_done, TILES)
            lgt = acc[:, 0:TILES, 0:NG + NE]
            dve.memset(R["lg"], -3e38)
            link(dve.tensor_tensor(R["le"], lgt[:, :, NG:NG + NE],
                                   b_r[:, NG:NG + NE].unsqueeze(1).broadcast_to([P, TILES, NE]), ALU.add))
            link(dve.tensor_tensor(R["lg"][:, :, 0:NG], lgt[:, :, 0:NG],
                                   b_r[:, 0:NG].unsqueeze(1).broadcast_to([P, TILES, NG]), ALU.add))
            for t in range(TILES):
                ins = dve.max(R["m8"][:, t, :], R["lg"][:, t, :])
            link(ins)
            dve.tensor_tensor(R["shifted"], R["lg"][:, :, 0:NG], R["m8"][:, :, 0:1].broadcast_to([P, TILES, NG]),
                              ALU.subtract).then_inc(grp_shift, 1)
            for t in range(TILES):
                ins = dve.max_index(R["i8"][:, t, :], R["m8"][:, t, :], R["lg"][:, t, :])
            link(ins)
            link(dve.tensor_copy(R["gidx"], R["i8"][:, :, 0]))
            link(dve.tensor_tensor(R["pen"], R["gidx"].unsqueeze(2).broadcast_to([P, TILES, NG]),
                                   io_e[:, 0:NG].unsqueeze(1).broadcast_to([P, TILES, NG]), ALU.is_equal))
            link(dve.tensor_scalar(R["pen"], R["pen"], -1.0, BIG, ALU.add, ALU.mult))
            le3 = R["le"].rearrange("p t (g e) -> p (t g) e", e=EPG)
            link(dve.tensor_tensor(le3, le3, R["pen"].rearrange("p t g -> p (t g)").unsqueeze(2).broadcast_to(
                [P, TILES * NG, EPG]), ALU.add))
            for t in range(TILES):
                ins = dve.max(R["v8"][:, t, :], R["le"][:, t, :])
            link(ins)
            dve.tensor_tensor(R["d2"], R["v8"][:, :, 1], R["v8"][:, :, 0], ALU.subtract).then_inc(exp2_in, 1)
            for t in range(TILES):
                ins = dve.max_index(R["i8"][:, t, :], R["v8"][:, t, :], R["le"][:, t, :])
            link(ins)
            for j in range(2):
                ins = dve.tensor_copy(R["idx"][:, j, :], R["i8"][:, :, j])
            link(ins)
            for j in range(2):
                ins = dve.tensor_tensor(R["hot1"][:, j, :, :],
                                        R["idx"][:, j, :].unsqueeze(2).broadcast_to([P, TILES, NE]),
                                        io_e.unsqueeze(1).broadcast_to([P, TILES, NE]), ALU.is_equal)
            link(ins)
            for j in range(2):
                ins = dve.tensor_tensor(R["hot1"][:, j, :, :], R["hot1"][:, j, :, :],
                                        token[:, :, 1:2].broadcast_to([P, TILES, NE]), ALU.mult)
            link(ins)
            dve.tensor_tensor(R["hot"], R["hot1"][:, 0, :, :], R["hot1"][:, 1, :, :], ALU.add).then_inc(hot_done, 1)
            dve.wait_ge(grp_exp, 1)
            link(dve.tensor_reduce(R["gsum"], R["e_grp"], AX.X, ALU.add))
            link(dve.reciprocal(R["gsum"], R["gsum"]))
            dve.wait_ge(exp2_out, 1)
            link(dve.tensor_scalar(R["d2"], R["e2"], 1.0, None, ALU.add))
            link(dve.reciprocal(R["d2"], R["d2"]))
            link(dve.tensor_tensor(R["w"][:, 0, :], R["d2"], R["gsum"], ALU.mult))
            dve.tensor_tensor(R["w"][:, 1, :], R["w"][:, 0, :], R["e2"], ALU.mult)
            dve.wait_ge(rank_done, 1)
            link(dve.tensor_scalar(R["cnt"], acc[:, 5, 0:NE], 0.0, None, ALU.is_gt))
            for m in range(1, -(-(SEQ + DEC) // P)):
                link(dve.scalar_tensor_tensor(R["cnt"], acc[:, 5, 0:NE], float(P * m), R["cnt"], ALU.is_gt, ALU.add))
            link(dve.tensor_tensor_scan(R["cum"], ones[:, 0:NE], R["cnt"], 0.0, ALU.mult, ALU.add))
            link(dve.tensor_tensor(R["startof"], R["cum"], R["cnt"], ALU.subtract))
            link(dve.tensor_scalar(R["startof"], R["startof"], float(P), None, ALU.mult))
            link(dve.tensor_tensor(R["slotbase"], acc[:, 0:TILES, 0:NE],
                                   R["startof"].unsqueeze(1).broadcast_to([P, TILES, NE]), ALU.add))
            for j in range(2):
                ins = dve.tensor_tensor(R["hot1"][:, j, :, :], R["hot1"][:, j, :, :], R["slotbase"], ALU.mult)
            link(ins)
            for j in range(2):
                ins = dve.tensor_reduce(R["slot"][:, j * TILES:j * TILES + TILES], R["hot1"][:, j, :, :], AX.X,
                                        ALU.add)
            link(ins)
            for j in range(2):
                ins = dve.tensor_tensor(R["slot"][:, j * TILES:j * TILES + TILES],
                                        R["slot"][:, j * TILES:j * TILES + TILES], token[:, :, 2], ALU.add)
            link(ins)
            n2 = 2 * TILES
            link(dve.tensor_tensor(R["ge"], io_blk.unsqueeze(1).broadcast_to([P, n2, NBLK + 1]),
                                   R["slot"].unsqueeze(2).broadcast_to([P, n2, NBLK + 1]), ALU.is_le))
            dve.tensor_tensor(R["oh_blk"], R["ge"][:, :, 0:NBLK], R["ge"][:, :, 1:NBLK + 1], ALU.subtract)
            link(dve.tensor_reduce(R["nge"], R["ge"], AX.X, ALU.add))
            link(dve.scalar_tensor_tensor(R["slot"], R["nge"], -float(P), R["slot"], ALU.mult, ALU.add))
            link(dve.tensor_scalar(R["slot"], R["slot"], float(P), None, ALU.add))
            dve.tensor_tensor(R["in_block"], R["slot"].unsqueeze(2).broadcast_to([P, n2, P]),
                              io128.unsqueeze(1).broadcast_to([P, n2, P]), ALU.is_equal)
            for j in range(2):
                ohb = R["oh_blk"][:, j * TILES:j * TILES + TILES, :]
                what = R["what"][:, j * TILES:j * TILES + TILES, :]
                tok = token[:, :, 0:1].broadcast_to([P, TILES, NBLK])
                link(dve.tensor_tensor(what[:, :, 0:NBLK], ohb, tok, ALU.mult))
                dve.scalar_tensor_tensor(what[:, :, NBLK:2 * NBLK], ohb, float(REAL * j), what[:, :, 0:NBLK],
                                         ALU.mult, ALU.add)
                ins = dve.tensor_tensor(what[:, :, 2 * NBLK:3 * NBLK], ohb,
                                        R["w"][:, j, :].unsqueeze(2).broadcast_to([P, TILES, NBLK]), ALU.mult)
            ins.then_inc(plan_in, 1)
            for half in range(2):
                nb = NBLK // 2
                cmp_ = R["tmp"].rearrange("p (b e) -> p b e", e=NE)
                link(dve.scalar_tensor_tensor(cmp_, R["cum"].unsqueeze(1).broadcast_to([P, nb, NE]), float(P),
                                              io_blk[:, half * nb:half * nb + nb].unsqueeze(2).broadcast_to(
                                                  [P, nb, NE]), ALU.mult, ALU.is_le))
                link(dve.tensor_reduce(R["ge"][:, 0, half * nb:half * nb + nb], cmp_, AX.X, ALU.add))
            link(dve.tensor_scalar(R["ge"][:, 0, 0:NBLK], R["ge"][:, 0, 0:NBLK], float(NE - 1), None, ALU.min))
            link(dve.tensor_copy(expert_of[:, 0:NBLK], R["ge"][0:1, 0, 0:NBLK]))
            dve.tensor_copy(n_blocks[:, 0:1], R["cum"][0:1, NE - 1:NE])
            dve.wait_ge(plan_done, 1)
            pl3 = acc[:, 0, 0:3 * NBLK].rearrange("p (a b) -> p a b", b=NBLK)
            dve.tensor_scalar(R["pl"][:, 0, :], pl3[:, 0, :], -1.0, 0.0, ALU.add, ALU.max)
            link(dve.tensor_scalar(R["pl"][:, 1, :], pl3[:, 1, :], 0.0, 4.0 * NASSIGN, ALU.is_equal, ALU.mult))
            link(dve.tensor_tensor(R["pl"][:, 1, :], pl3[:, 1, :], R["pl"][:, 1, :], ALU.add))
            link(dve.tensor_scalar(R["pl"][:, 1, :], R["pl"][:, 1, :], -1.0, None, ALU.add))
            dve.tensor_copy(gate_of[:, 0:NBLK], pl3[:, 2, :])
            dve.tensor_copy(src_row[:, 0:NBLK], R["pl"][:, 0, :])
            dve.tensor_copy(dst_row[:, 0:NBLK], R["pl"][:, 1, :])
            link(dve.memset(src_row[:, NBLK:NBLK + 2], 0))
            dve.sem_inc(lo_e, EG)
            dve.sem_inc(tlo_e, 2)
            dve.sem_inc(g_e, 2)
            dve.sem_inc(ya_e, 2)
            dve.sem_inc(yd_e, 2)
            dve.sem_inc(routed, 1)

            n = dve.value_load(n_blocks[0:1, 0:1], min_val=1, max_val=NBLK)
            with dve.Fori(0, PAIRS) as i:
                with dve.If(i * 2 < n):
                    def split(q):
                        dve.wait_ge(hi_e, i * EG + (q + 1))
                        dve.tensor_tensor(elo[:, q % ERING, :], raw_e[:, q, :], ehi[:, q % ERING, :].bitcast(F32),
                                          ALU.subtract).then_inc(lo_e, 1)

                    def turned(b, s):
                        dve.wait_ge(thi_e, i * 6 + (2 * b + s + 1))
                        dve.tensor_tensor(xlo[:, b, 4 * s:4 * s + 4, :], tp[:, s, :].rearrange("p (k r) -> p k r", r=P),
                                          xhi[:, b, 4 * s:4 * s + 4, :].bitcast(F32), ALU.subtract).then_inc(tlo_e, 1)

                    def product(b):
                        dve.wait_ge(silu_e, i * 2 + (b + 1))
                        dve.tensor_tensor(gg[:, b, :], acc[:, b, DE:2 * DE], gg[:, b, :], ALU.mult).then_inc(g_e, 1)

                    def turned_g(b):
                        dve.wait_ge(thi_e, i * 6 + (b + 5))
                        dve.tensor_tensor(glo[:, b, :, :], tp[:, b, 0:DE].rearrange("p (k r) -> p k r", r=P),
                                          ghi[:, b, :, :].bitcast(F32), ALU.subtract).then_inc(tlo_e, 1)

                    def result(b):
                        dve.wait_ge(used_e, i * EG + (2 * b + 10 + ERING))
                        dve.wait_ge(left_e, i * 2 + (b + 1))
                        dve.tensor_scalar(ye[:, b, 512:D], acc[:, 3 + 2 * b, :], gate_in[:, b, :], None,
                                          ALU.mult).then_inc(yd_e, 1)

                    for b in range(2):
                        dve.wait_ge(ya_e, i * 2 + (b + 1))
                        dve.wait_ge(yd_e, i * 2 + (b + 1))
                        dve.tensor_copy(gate_in[:, b, :], gate_of[:, ds(i * 2 + b, 1)]).then_inc(gate_e, 1)
                    split(0)
                    turned(0, 0)
                    turned(0, 1)
                    split(1)
                    turned(1, 0)
                    turned(1, 1)
                    for q in range(2, 9):
                        split(q)
                    product(0)
                    for q in range(9, 12):
                        split(q)
                    product(1)
                    turned_g(0)
                    dve.wait_ge(gate_e, i * 2 + 2)
                    result(0)
                    turned_g(1)
                    result(1)

            for t in range(TILES):
                rows = ROWS[t]
                dve.wait_ge(ld_y[t % 2], 16 * (t // 2 + 1))
                link(dve.tensor_tensor(h[0:rows, t, :], h[0:rows, t, :], ysum[0:rows, t % 2, 0, :], ALU.add))
                dve.tensor_tensor(h[0:rows, t, :], h[0:rows, t, :], ysum[0:rows, t % 2, 1, :],
                                  ALU.add).then_inc(y_added, 1)
            for t in range(TILES):
                halve_lo("pe", 0, t, 2, phi, plo)
            dve.wait_ge(ld_g, 32)
            dve.wait_ge(f_rstd, 1)
            for t in range(TILES):
                if t >= 2:
                    dve.wait_ge(t_done, tg[("hp", t - 2, 1)] + 1)
                dve.scalar_tensor_tensor(hp[:, t % 2, :], h[:, t, :], r_f[:, t:t + 1], grow2, ALU.mult,
                                         ALU.mult).then_inc(fn_done, 1)
                if t >= 1:
                    for s in range(2):
                        halve_lo("hp", s, t - 1, 4, lhi2, llo2)
            for s in range(2):
                halve_lo("hp", s, TILES - 1, 4, lhi2, llo2)
            run(ple)

        def late_gpsimd(pool, link, inverse_rms):
            pool.memset(ones[:, :], 1.0).then_inc(ones_set, 1)
            pool.wait_ge(h_sq, TILES)
            inverse_rms(r_h, ss_h, TILES, D).then_inc(h_rstd, 1)
            for t in range(TILES):
                pool.wait_ge(hn_done, t + 1)
                pool.dma_start(hn_rows[t * P:t * P + ROWS[t], :], xn[0:ROWS[t], t % 2, :]).then_inc(hn_sent[t % 2], 16)
            for j in range(2):
                pool.wait_ge(hn_sent[j], 16 * ((TILES - j + 1) // 2))
            pool.sem_inc(left_e, 2)

            pool.wait_ge(routed, 1)
            n = pool.value_load(n_blocks[0:1, 0:1], min_val=1, max_val=NBLK)
            for b in range(2):
                pool.tensor_copy(row_in[:, b, :], src_row[:, b:b + 1]).then_inc(own_e, 1)
            pool.wait_ge(own_e, 2)
            for b in range(2):
                pool.indirect_dma_start(xg[:, b, :], None, hn_rows,
                                        bass.IndirectOffsetOnAxis(ap=row_in[:, b, :], axis=0)).then_inc(ld_xg[b], 16)
            with pool.Fori(0, PAIRS) as i:
                with pool.If(i * 2 < n):
                    for b in range(2):
                        pool.wait_ge(t_e, i * 6 + (2 * b + 8))
                        pool.wait_ge(ld_xg[b], i * 16 + 16)
                        pool.sem_inc(pool_steps, 1)
                        pool.tensor_copy(row_in[:, b, :], src_row[:, ds(i * 2 + (2 + b), 1)]).then_inc(own_e, 1)
                        pool.wait_ge(own_e, i * 4 + (b + 3))
                        pool.sem_inc(pool_steps, 1)
                        pool.indirect_dma_start(xg[:, b, :], None, hn_rows,
                                                bass.IndirectOffsetOnAxis(ap=row_in[:, b, :], axis=0)
                                                ).then_inc(ld_xg[b], 16)
                    for b in range(2):
                        pool.tensor_copy(row_out[:, b, :], dst_row[:, ds(i * 2 + b, 1)]).then_inc(own_e, 1)
                        pool.wait_ge(own_e, i * 4 + (b + 5))
                        pool.wait_ge(ya_e, i * 2 + (b + 3))
                        pool.wait_ge(yd_e, i * 2 + (b + 3))
                        pool.sem_inc(pool_steps, 1)
                        pool.indirect_dma_start(y_rows, bass.IndirectOffsetOnAxis(ap=row_out[:, b, :], axis=0),
                                                ye[:, b, :], None, bounds_check=NASSIGN - 1,
                                                oob_is_err=False).then_inc(sent_e[b], 16)
                    for b in range(2):
                        pool.wait_ge(sent_e[b], i * 16 + 16)
                        pool.sem_inc(left_e, 1)
            steps = (n + 1) // 2
            for b in range(2):
                pool.wait_ge(sent_e[b], steps * 16)
                pool.wait_ge(ld_xg[b], steps * 16 + 16)
            pool.sem_inc(moe_done, 1)
            pool.memset(ptok[DEC:P, PT, :], 0.0).then_inc(zeroed, 1)
            pool.wait_ge(zeroed, 3)
            pool.wait_ge(f_sq, TILES)
            inverse_rms(r_f, ss_f, TILES, D).then_inc(f_rstd, 1)
            for t in range(TILES):
                pool.wait_ge(y_done, y_index[(ple_first + 3, t)] + 1)
                dst = o["y_p"][t * P:t * P + P, :] if t < PT else o["y_s"]
                pool.dma_start(dst, h[0:ROWS[t], t, :]).then_inc(st_y, 16)
            pool.wait_ge(st_y, 16 * TILES)

        block = ctx.enter_context(nc.Block())
        last_first = len(first) - 1
        NCONST = 20
        gv = {"mla_qn": 0, "mla_qr": 1, "mla_kn": 2, "diff_q": 3, "diff_k": 4, "diff_sub": 5}

        def load_granule(sp, i, g):
            c, n = items[i], granules[(i, g)]
            if n >= RAW:
                sp.wait_ge(lo_done, n - RAW + 1)
            src = a[c.src].rearrange("(k p) n -> p k n", p=P)[:, 2 * g:2 * g + 2, c.col:c.col + c.width]
            sp.dma_start(raw[:, n % RAW, :, 0:c.width], src).then_inc(ld_raw[n % RAW], 16)

        @block.sync
        def _(sp):
            for t in range(TILES):
                sp.dma_start(gates[0:ROWS[t], t, 0:D], a["x"][t * P:t * P + ROWS[t], :]).then_inc(ld_x[t], 16)
            load_granule(sp, 0, 0)
            sp.dma_start(ident[:, :], a["c_ident"]).then_inc(ld_const, 16)
            sp.dma_start(grow[:, :], a["g_mix"].partition_broadcast(P)).then_inc(ld_const, 16)
            sp.dma_start(rope[:, :, :], a["c_rope"].rearrange("(t p) n -> p t n", p=P)).then_inc(ld_const, 16)
            sp.dma_start(mask[:, :], a["c_mask"]).then_inc(ld_const, 16)
            sp.dma_start(gq_lat[:, :], a["g_q_lat"].partition_broadcast(P)).then_inc(ld_const, 16)
            sp.dma_start(gkv[:, 0:KVL], a["g_kv_lat"].partition_broadcast(P)).then_inc(ld_const, 16)
            sp.dma_start(gkv[:, KVL:KVL + RD], a["g_mla_kr"].partition_broadcast(P)).then_inc(ld_const, 16)
            for name, j in gv.items():
                g = a["g_" + name]
                sp.dma_start(gvec[:, j, 0:g.shape[-1]], g.partition_broadcast(P)).then_inc(ld_const, 16)
            for j, name in enumerate(("lambda_q1", "lambda_k1", "lambda_q2", "lambda_k2")):
                sp.dma_start(zs[:, 5, 64 * j:64 * j + 64], a[name].partition_broadcast(P)).then_inc(ld_const, 16)
            sp.dma_start(gates[:, 0, D:2 * D], a["cache_k"]).then_inc(ld_const, 16)
            sp.dma_start(gates[:, 1, D:D + KVL], a["cache_ckv"]).then_inc(ld_const, 16)
            sp.dma_start(krope[:, CACHE, :], a["cache_krope"]).then_inc(ld_const, 16)
            every = [(i, g) for i in range(len(first)) for g in range(items[i].kt // 2)][1:]
            for n, (i, g) in enumerate(every):
                load_granule(sp, i, g)
                if n == 3:
                    sp.wait_ge(xn_done, TILES)
                    sp.dma_start(grow[:, :], a["g_ffn"].partition_broadcast(P)).then_inc(ld_g, 16)
            o_first = start[id(outp)]
            rest = [(i, g) for i in range(o_first, o_first + 2) for g in range(4)]
            for i, g in rest[:RAW]:
                load_granule(sp, i, g)
            sp.wait_ge(z_done, units[(last_first, TILES - 1)] + 1)
            sp.dma_start(w_uq[:, :, :], a["w_uq"].rearrange("(k p) n -> p k n", p=P)).then_inc(ld_wu, 16)
            sp.dma_start(w_uk[:, :, :], a["w_uk"].rearrange("(k p) n -> p k n", p=P)).then_inc(ld_wu, 16)
            sp.dma_start(w_uv[:, :, :], a["w_uv"].rearrange("(k p) n -> p k n", p=P)).then_inc(ld_wu, 16)
            for t in range(TILES):
                sp.wait_ge(outz[t], 16 * out_count(last_first, t))
            for hd in range(H):
                cols = slice(hd * VB, hd * VB + VB)
                if hd >= 2:
                    sp.wait_ge(pv_done["b"], TILES * (hd - 1))
                s = ld_v[hd % 2]
                sp.dma_start(vh[:, hd % 2, 0:PT, :],
                             o["dv_p"].rearrange("(t p) n -> p t n", p=P)[:, :, cols]).then_inc(s, 16)
                sp.dma_start(vh[0:DEC, hd % 2, PT, :], o["dv_s"][:, cols]).then_inc(s, 16)
                sp.dma_start(vh[:, hd % 2, CACHE, :], a["cache_v"][:, cols]).then_inc(s, 16)
            last_latent = start[id(outp)] - 1
            for t in range(TILES + 1):
                sp.wait_ge(outz[t], 16 * out_count(last_latent, t))
            for hd in range(H):
                cols = slice(hd * VB, hd * VB + VB)
                if hd >= 2:
                    sp.wait_ge(pv_done["a"], TILES * (hd - 1))
                else:
                    sp.wait_ge(pv_done["b"], TILES * H)
                sp.dma_start(vh[:, hd % 2, :, :],
                             va_rows.rearrange("(t p) n -> p t n", p=P)[:, :, cols]).then_inc(ld_v[hd % 2], 16)
            sp.wait_ge(t_copied, copied[("merged", TILES - 1, 1)] + 1)
            for t in range(TILES):
                sp.dma_start(h[0:ROWS[t], t, :], a["x"][t * P:t * P + ROWS[t], :]).then_inc(ld_h, 16)
            for i, g in rest[RAW:]:
                load_granule(sp, i, g)
            late_sync(sp)

        def key_tiles(t):
            if t < PT:
                return [(j, P, j * P) for j in range(t + 1)]
            return [(CACHE, PAST, SEQ), (PT, DEC, SEQ + PAST)]

        @block.tensor
        def _(pe):
            pe.wait_ge(ld_const, 16 * NCONST)

            def turn(key, blocks, rows=P, cols=P, pitch=P):
                wait_bank_for(pe, key)
                bank = tg[key] % 2
                for j, src in enumerate(blocks):
                    last = pe.transpose(tp[0:cols, bank, j * P:j * P + rows], src, ident[0:rows, 0:rows])
                last.then_inc(t_done, 1)

            def multiply(i):
                c = items[i]
                lo_name = {"act": {0: "x", 2: "merged", 3: "hp"}.get(
                    next(n for n, ph in enumerate(phases) if c in ph)), "pe": "pe"}.get(c.lhs)
                steps = c.kt // 2 if c.split else 1
                for g in range(steps):
                    if c.split:
                        pe.wait_ge(lo_done, granules[(i, g)] + 1)
                    for t in range(c.tiles):
                        bank = acc[:, t, 0:c.width]
                        rows = slice(t * P, t * P + P)
                        if g == 0:
                            if lo_name:
                                wait_group_copied(pe, (lo_name, t, 0 if lo_name == "pe" else 1))
                            before = [n for n in range(i) if items[n].tiles > t]
                            if before:
                                pe.wait_ge(z_copied, units[(before[-1], t)] + 1)
                        if c.split:
                            for k in range(2):
                                n = granules[(i, g)] % RING
                                kk = 2 * g + k
                                L, W = {"x": (lhi, llo), "pe": (phi, plo)}.get(lo_name, (lhi2, llo2)), (whi, wlo)
                                for x, w in ((0, 0), (0, 1), (1, 0)):
                                    mm = pe.matmul(bank, L[x][:, kk, rows], W[w][:, n, k, 0:c.width],
                                                   start=(kk == 0 and x + w == 0),
                                                   stop=(kk == c.kt - 1 and x == 1))
                        else:
                            L = {"q_lat": q_latT, "ckv": ckvT}[c.lhs]
                            W = {"w_uq": w_uq, "w_uk": w_uk, "w_uv": w_uv}[c.src]
                            for k in range(c.kt):
                                mm = pe.matmul(bank, L[:, k, rows], W[:, k, c.col:c.col + c.width],
                                               start=(k == 0), stop=(k == c.kt - 1))
                        if g == steps - 1:
                            mm.then_inc(z_done, 1)
                    if c.split and g < steps - 1:
                        mm.then_inc(w_used, 1)

            def transposes(i):
                c = items[i]
                if c.kind != "norm":
                    return
                for t in range(c.tiles):
                    pe.wait_ge(y_done, y_index[(i, t)] + 1)
                    z = zs[:, t, :]
                    if c.name == "uq":
                        turn((i, t, 0), [z[:, j * HD:j * HD + HD] for j in range(4)], cols=HD)
                    elif c.name == "uk":
                        kas = pr[:, t % 2, :, :].rearrange("p a b -> p (a b)")
                        for s in range(2):
                            turn((i, t, s), [kas[:, j * HD:j * HD + HD] for j in range(4 * s, 4 * s + 4)], cols=HD)
                    else:
                        n = {"q_lat": 3, "ckv": 2}.get(c.name, 4)
                        turn((i, t, 0), [z[:, j * P:j * P + P] for j in range(n)])

            def run(ph):
                ids = phase_items(ph)
                for i in ids:
                    multiply(i)
                    if i > ids[0]:
                        transposes(i - 1)
                transposes(ids[-1])

            def attention(ph, maps, dim):
                name = "attn_" + ph

                def scores(n):
                    hd, t = divmod(n, TILES)
                    kt_ = key_tiles(t)
                    k0, nk = kt_[0][2], sum(r for _, r, _ in kt_)
                    if n >= 2:
                        pe.wait_ge(exp_done[ph], maps * (n - 1))
                    for c in range(maps):
                        rows = slice(dim * c, dim * c + dim)
                        bank = 2 * (n % 2) + c
                        mm = pe.matmul(acc[0:ROWS[t], bank, 0:nk], qT[rows, hd, t * P:t * P + ROWS[t]],
                                       kT[rows, hd, k0:k0 + nk], start=True, stop=(t == PT))
                        if t < PT:
                            mm = pe.matmul(acc[:, bank, nk - CHUNK:nk], mask[:, 0:P], mask[:, P:P + CHUNK],
                                           start=False, stop=True)
                    mm.then_inc(s_done[ph], 1)

                def turn_probs(n):
                    hd, t = divmod(n, TILES)
                    if ph == "b":
                        pe.wait_ge(comb_done[ph], n + 1)
                    else:
                        pe.wait_ge(exp_done[ph], n + 1)
                    wait_bank_for(pe, (name, n, 0))
                    bank = tg[(name, n, 0)] % 2
                    at = 0
                    for j, (_, nk, _) in enumerate(key_tiles(t)):
                        last = pe.transpose(tp[0:nk, bank, j * P:j * P + ROWS[t]],
                                            pr[0:ROWS[t], n % 2, 0, at:at + nk], ident[0:ROWS[t], 0:ROWS[t]])
                        at += nk
                    last.then_inc(t_done, 1)

                def values(n):
                    hd, t = divmod(n, TILES)
                    pe.wait_ge(pt_copied, pt[(name, n, 0)] + 1)
                    if t == 0:
                        pe.wait_ge(ld_v[hd % 2], 48 * (hd // 2 + 1) if ph == "b" else 48 * 4 + 16 * (hd // 2 + 1))
                    if n >= 2:
                        pe.wait_ge(o_done[ph], n - 1)
                        if ph == "b":
                            pe.wait_ge(sqo_done, n - 1)
                    kt_ = key_tiles(t)
                    for j, (slot, nk, _) in enumerate(kt_):
                        mm = pe.matmul(acc[0:ROWS[t], 4 + n % 2, 0:VB], prT[0:nk, n % 2, j, 0:ROWS[t]],
                                       vh[0:nk, hd % 2, slot, :], start=(j == 0), stop=(j == len(kt_) - 1))
                    mm.then_inc(pv_done[ph], 1)

                n_units = H * TILES
                for n in range(n_units + 2):
                    if n < n_units:
                        scores(n)
                    if 1 <= n <= n_units:
                        turn_probs(n - 1)
                    if n >= 2:
                        values(n - 2)

            for t in range(TILES):
                pe.wait_ge(xn_done, t + 1)
                for s in range(2):
                    turn(("x", t, s), [gates[:, t, j * P:j * P + P] for j in range(4 * s, 4 * s + 4)])
            for s in range(2):
                turn(("cache_k", 0, s), [gates[:, 0, D + j * P:D + j * P + P] for j in range(4 * s, 4 * s + 4)])
            turn(("cache_ckv", 0, 0), [gates[:, 1, D + j * P:D + j * P + P] for j in range(2)])
            run(first)
            pe.wait_ge(z_copied, units[(last_first, TILES - 1)] + 1)
            pe.wait_ge(t_copied, copied[(start[id(latent)] - 1 - 6, TILES - 1, 0)] + 1)
            attention("b", 2, DB)
            pe.wait_ge(exp_done["b"], 2 * H * TILES)
            pe.wait_ge(o_done["b"], H * TILES)
            pe.wait_ge(sqo_done, H * TILES)
            pe.wait_ge(ld_wu, 48)
            run(latent)
            pe.wait_ge(z_copied, units[(start[id(outp)] - 1, TILES)] + 1)
            pe.wait_ge(t_copied, copied[(start[id(latent)] + 2, TILES, 1)] + 1)
            attention("a", 1, HD)
            pe.wait_ge(exp_done["a"], H * TILES)
            pe.wait_ge(o_done["a"], H * TILES)
            for t in range(TILES):
                pe.wait_ge(merged_done, t + 1)
                for s in range(2):
                    turn(("merged", t, s), [gates[:, t, j * P:j * P + P] for j in range(4 * s, 4 * s + 4)])
            run(outp)
            late_tensor(pe, turn, run)

        @block.scalar
        def _(act):
            own = [0]

            def link(ins):
                own[0] += 1
                ins.then_inc(act_own, 1)
                act.wait_ge(act_own, own[0])

            def split_hi(i, g):
                c, n = items[i], granules[(i, g)]
                act.wait_ge(ld_raw[n % RAW], 16 * (n // RAW + 1))
                wait_ring_free(act, n)
                act.activation(whi[:, n % RING, :, 0:c.width], raw[:, n % RAW, :, 0:c.width],
                               ACT.Copy).then_inc(hi_done, 1)

            def copy_out(i):
                c = items[i]
                for t in range(c.tiles):
                    act.wait_ge(z_done, units[(i, t)] + 1)
                    src = acc[:, t, 0:c.width]
                    if uses_zs(i):
                        wait_slot_free(act, i, t)
                        func = ACT.Sigmoid if c.kind == "ple" else ACT.Copy
                        act.activation(zs[:, t, 0:c.width], src, func).then_inc(z_copied, 1)
                    elif c.kind == "gate":
                        at = (0 if c.name == "ga" else D) + 512 * c.half
                        act.activation(gates[:, t, at:at + 512], src, ACT.Sigmoid).then_inc(z_copied, 1)
                    else:
                        act.activation(pj[:, t, 512 * c.half:512 * c.half + 512], src,
                                       ACT.Copy).then_inc(z_copied, 1)

            def squares(i):
                c = items[i]
                if c.kind != "norm":
                    return
                for t in range(c.tiles):
                    act.wait_ge(z_copied, units[(i, t)] + 1)
                    if y_norm[(i, t)] >= 1:
                        act.wait_ge(ss_done, y_norm[(i, t)])
                    act.activation(sq[:, 0:c.width], zs[:, t, 0:c.width], ACT.Square).then_inc(sq_done, 1)

            def run(ph):
                ids = list(phase_items(ph))
                for i in ids + [ids[-1] + 1]:
                    steps = items[i].kt // 2 if i in ids and items[i].split else 0
                    if steps > 0:
                        split_hi(i, 0)
                    if i - 1 in ids:
                        copy_out(i - 1)
                    if steps > 1:
                        split_hi(i, 1)
                    if i - 1 in ids:
                        squares(i - 1)
                    for g in range(2, steps):
                        split_hi(i, g)

            def halve_hi(name, s, t, n, hi):
                act.wait_ge(t_done, tg[(name, t, s)] + 1)
                act.activation(hi[:, 4 * s:4 * s + n, t * P:t * P + P],
                               tp[:, tg[(name, t, s)] % 2, 0:n * P].rearrange("p (k r) -> p k r", r=P),
                               ACT.Copy).then_inc(hi_copied, 1)

            for t in range(TILES):
                act.wait_ge(ld_x[t], 16)
                if t == 0:
                    act.wait_ge(zeroed, 1)
                if t:
                    act.wait_ge(x_sq, t)
                act.activation(zs[:, 0:2, :].rearrange("p a b -> p (a b)"), gates[:, t, 0:D], ACT.Square,
                               accum_out=ss_x[:, t:t + 1]).then_inc(x_sq, 1)
            act.wait_ge(x_sq, TILES)
            act.wait_ge(lam_dots, 2)
            act.activation(lamv[:, 2:4], lamv[:, 0:2], ACT.Exp).then_inc(lam_exp, 1)
            for t in range(TILES):
                for s in range(2):
                    halve_hi("x", s, t, 4, lhi)
            run(first)

            def attention(ph, maps):
                name = "attn_" + ph
                n_units = H * TILES

                def exps(n):
                    hd, t = divmod(n, TILES)
                    rows, nk = ROWS[t], sum(r for _, r, _ in key_tiles(t))
                    act.wait_ge(nm_done[ph], n + 1)
                    if n >= 2:
                        act.wait_ge(t_done, tg[(name, n - 2, 0)] + 1)
                    for c in range(maps):
                        act.activation(pr[0:rows, n % 2, c, 0:nk], acc[0:rows, 2 * (n % 2) + c, 0:nk], ACT.Exp,
                                       bias=negmax[0:rows, 2 * (n % 2) + c:2 * (n % 2) + c + 1],
                                       accum_out=sums[0:rows, 2 * (n % 2) + c:2 * (n % 2) + c + 1]
                                       ).then_inc(exp_done[ph], 1)

                def copy_turned(n):
                    hd, t = divmod(n, TILES)
                    rows, bank = ROWS[t], tg[(name, n, 0)] % 2
                    act.wait_ge(t_done, tg[(name, n, 0)] + 1)
                    if n >= 2:
                        act.wait_ge(pv_done[ph], n - 1)
                    if t < PT:
                        act.activation(prT[:, n % 2, 0:t + 1, :],
                                       tp[:, bank, 0:(t + 1) * P].rearrange("p (k r) -> p k r", r=P),
                                       ACT.Copy).then_inc(pt_copied, 1)
                    else:
                        act.activation(prT[:, n % 2, 0, 0:rows], tp[:, bank, 0:rows], ACT.Copy)
                        act.activation(prT[0:DEC, n % 2, 1, 0:rows], tp[0:DEC, bank, P:P + rows],
                                       ACT.Copy).then_inc(pt_copied, 1)

                def square_out(n):
                    hd, t = divmod(n, TILES)
                    rows = ROWS[t]
                    act.wait_ge(pv_done[ph], n + 1)
                    if n:
                        act.wait_ge(sqo_done, n)
                    act.activation(sq[0:rows, 0:VB], acc[0:rows, 4 + n % 2, 0:VB], ACT.Square,
                                   accum_out=ss_o[0:rows, t * H + hd:t * H + hd + 1]).then_inc(sqo_done, 1)

                for n in range(n_units + 2):
                    if n < n_units:
                        exps(n)
                    if 1 <= n <= n_units:
                        copy_turned(n - 1)
                    if n >= 2 and ph == "b":
                        square_out(n - 2)

            act.wait_ge(ss_done, y_norm_of_phase(first))
            attention("b", 2)
            act.wait_ge(sqo_done, H * TILES)
            act.wait_ge(t_done, tg[("attn_b", H * TILES - 1, 0)] + 1)
            run(latent)
            act.wait_ge(t_done, tg[(start[id(latent)] + 2, TILES, 1)] + 1)
            attention("a", 1)
            for t in range(TILES):
                for s in range(2):
                    halve_hi("merged", s, t, 4, lhi2)
            run(outp)
            late_scalar(act, link, halve_hi, run)

        @block.vector
        def _(dve):
            own = [0]

            def link(ins):
                own[0] += 1
                ins.then_inc(dve_own, 1)
                dve.wait_ge(dve_own, own[0])

            def split_lo(i, g):
                c, n = items[i], granules[(i, g)]
                dve.wait_ge(hi_done, n + 1)
                dve.tensor_tensor(wlo[:, n % RING, :, 0:c.width], raw[:, n % RAW, :, 0:c.width],
                                  whi[:, n % RING, :, 0:c.width].bitcast(F32), ALU.subtract).then_inc(lo_done, 1)

            def halve_lo(name, s, t, n, hi, lo):
                dve.wait_ge(hi_copied, hi_index[(name, t, s)] + 1)
                cols = (slice(4 * s, 4 * s + n), slice(t * P, t * P + P))
                dve.tensor_tensor(lo[:, cols[0], cols[1]],
                                  tp[:, tg[(name, t, s)] % 2, 0:n * P].rearrange("p (k r) -> p k r", r=P),
                                  hi[:, cols[0], cols[1]].bitcast(F32), ALU.subtract).then_inc(t_copied, 1)

            def copy_group(key, dst, rows, n, width):
                dve.wait_ge(t_done, tg[key] + 1)
                src = tp[0:rows, tg[key] % 2, 0:n * P].rearrange("p (k r) -> p k r", r=P)[:, :, 0:width]
                dve.tensor_copy(dst, src).then_inc(t_copied, 1)

            def copy_turned(i):
                c = items[i]
                if c.kind != "norm":
                    return
                for t in range(c.tiles):
                    q = slice(t * P, t * P + ROWS[t]) if t < TILES else None
                    k = slice(KCOL[t], KCOL[t] + (ROWS[t] if t < TILES else P))
                    hs = slice(4 * c.half, 4 * c.half + 4)
                    if c.name == "q_lat":
                        copy_group((i, t, 0), q_latT[:, :, t * P:t * P + P], P, 3, P)
                    elif c.name == "ckv":
                        copy_group((i, t, 0), ckvT[:, :, t * P:t * P + P], P, 2, P)
                    elif c.name == "dq":
                        copy_group((i, t, 0), qT[:, hs, q], P, 4, ROWS[t])
                    elif c.name == "dk":
                        copy_group((i, t, 0), kT[:, hs, k], P, 4, ROWS[t])
                    elif c.name == "uq":
                        copy_group((i, t, 0), qT[0:HD, hs, q], HD, 4, ROWS[t])
                    elif t >= c.tiles - 2:
                        copy_keys(i, t)

            def copy_keys(i, t):
                k = slice(KCOL[t], KCOL[t] + (ROWS[t] if t < TILES else P))
                for s in range(2):
                    copy_group((i, t, s), kT[0:HD, 4 * s:4 * s + 4, k], HD, 4, ROWS[t] if t < TILES else P)

            def sums_of(i):
                c = items[i]
                if c.kind != "norm":
                    return
                gs = groups(i)
                total = sum(g[1] for g in gs)
                m = normitems[i]
                if m >= 2:
                    dve.wait_ge(rstd_done, m - 1)
                for t in range(c.tiles):
                    dve.wait_ge(sq_done, y_norm[(i, t)] + 1)
                    at = t * total
                    for n, g in enumerate(gs):
                        ins = dve.tensor_reduce(ss_z[m % 2][:, at:at + g[1]], grouped(sq[:, :], g), AX.X, ALU.add)
                        at += g[1]
                    ins.then_inc(ss_done, 1)

            def rotate(t, z, n, half):
                table = 0 if half == RD // 2 else 2 * RD
                cc = rope[:, t, table:table + 2 * half].unsqueeze(1).broadcast_to([P, n, 2 * half])
                ss = rope[:, t, table + 2 * half:table + 4 * half].unsqueeze(1).broadcast_to([P, n, 2 * half])
                r = [rot[:, j, 0:n * 2 * half].rearrange("p (n s) -> p n s", n=n) for j in range(2)]
                dve.tensor_tensor(r[0], z, cc, ALU.mult)
                dve.tensor_tensor(r[1][:, :, 0:half], z[:, :, half:2 * half], ss[:, :, 0:half], ALU.mult)
                link(dve.tensor_tensor(r[1][:, :, half:2 * half], z[:, :, 0:half], ss[:, :, half:2 * half], ALU.mult))
                return dve.tensor_tensor(z, r[0], r[1], ALU.add)

            def normalise(i, tiles):
                c = items[i]
                if c.kind != "norm":
                    return
                gs = groups(i)
                total = sum(g[1] for g in gs)
                m = normitems[i]
                dve.wait_ge(rstd_done, m + 1)
                for t in tiles:
                    z = zs[:, t, :]
                    r = r_z[m % 2][:, t * total:t * total + total]
                    if c.name in ("q_lat", "ckv"):
                        gain = {"q_lat": gq_lat, "ckv": gkv}[c.name]
                        for n, (off, _, size, _, _) in enumerate(gs):
                            ins = dve.scalar_tensor_tensor(z[:, off:off + size], z[:, off:off + size], r[:, n:n + 1],
                                                           gain[:, off:off + size], ALU.mult, ALU.mult)
                        if c.name == "ckv":
                            link(ins)
                            link(rotate(t, z[:, KVL:KVL + RD].unsqueeze(1), 1, RD // 2))
                            ins = dve.tensor_copy(krope[:, t, :], z[:, KVL:KVL + RD])
                        ins.then_inc(y_done, 1)
                        continue
                    names = {"dq": ["diff_q"], "dk": ["diff_k"], "uq": ["mla_qn", "mla_qr"], "uk": ["mla_kn"]}[c.name]
                    at = 0
                    for g, nm in zip(gs, names):
                        ins = dve.tensor_tensor(grouped(z, g), grouped(z, g),
                                                r[:, at:at + g[1]].unsqueeze(2).broadcast_to([P, g[1], g[2]]), ALU.mult)
                        at += g[1]
                    link(ins)
                    if c.name == "uk":
                        kas = pr[:, t % 2, :, :].rearrange("p a b -> p (a b)")[:, 0:H * HD].rearrange(
                            "p (h s) -> p h s", s=HD)
                        if t >= 2:
                            copy_keys(i, t - 2)
                    for g, nm in zip(gs, names):
                        dst = grouped(z, g) if c.name != "uk" else kas[:, :, 0:NOPE]
                        ins = dve.tensor_tensor(dst, grouped(z, g),
                                                gvec[:, gv[nm], 0:g[2]].unsqueeze(1).broadcast_to([P, g[1], g[2]]),
                                                ALU.mult)
                    if c.name == "uk":
                        ins = dve.tensor_copy(kas[:, :, NOPE:HD],
                                              krope[:, t, :].unsqueeze(1).broadcast_to([P, H, RD]))
                    elif c.name == "uq":
                        link(ins)
                        ins = rotate(t, grouped(z, gs[1]), 4, RD // 2)
                    else:
                        link(ins)
                        ins = rotate(t, z.rearrange("p (n s) -> p n s", s=DB)[:, :, 0:ROT], 8, ROT // 2)
                    ins.then_inc(y_done, 1)

            def finish(i, tiles):
                c = items[i]
                normalise(i, tiles)
                if c.kind == "residual":
                    for t in tiles:
                        if (i, t) == (start[id(outp)], 0):
                            dve.wait_ge(ld_h, 16 * TILES)
                            dve.wait_ge(zeroed, 2)
                        dve.wait_ge(z_copied, units[(i, t)] + 1)
                        hh = h[:, t, 512 * c.half:512 * c.half + 512]
                        dve.tensor_tensor(hh, hh, zs[:, t, :], ALU.add).then_inc(y_done, 1)
                if c.kind == "ple":
                    for t in tiles:
                        cols = slice(512 * c.half, 512 * c.half + 512)
                        dve.wait_ge(z_copied, units[(i, t)] + 1)
                        link(dve.tensor_tensor(pj[:, t, cols], pj[:, t, cols], zs[:, t, :], ALU.mult))
                        dve.tensor_tensor(h[:, t, cols], h[:, t, cols], pj[:, t, cols], ALU.add).then_inc(y_done, 1)

            def run(ph):
                ids = list(phase_items(ph))
                for i in ids + [ids[-1] + 1, ids[-1] + 2]:
                    steps = items[i].kt // 2 if i in ids and items[i].split else 0
                    if steps > 0:
                        split_lo(i, 0)
                    if i - 2 in ids:
                        copy_turned(i - 2)
                    if steps > 1:
                        split_lo(i, 1)
                    if i - 1 in ids:
                        sums_of(i - 1)
                    if steps > 2:
                        split_lo(i, 2)
                    n = items[i - 1].tiles if i - 1 in ids else 0
                    if n:
                        finish(i - 1, range(0, n // 2 + 1))
                    if steps > 3:
                        split_lo(i, 3)
                    if n:
                        finish(i - 1, range(n // 2 + 1, n))

            dve.wait_ge(zeroed, 1)
            dve.wait_ge(ld_const, 16 * NCONST)
            lq = zs[:, 5, :]
            for j in range(2):
                dve.tensor_tensor_reduce(rot[:, j, 0:64], lq[:, 128 * j:128 * j + 64], lq[:, 128 * j + 64:128 * j + 128],
                                         1.0, 0.0, ALU.mult, ALU.add, lamv[:, j:j + 1]).then_inc(lam_dots, 1)
            dve.wait_ge(x_rstd, 1)
            for t in range(TILES):
                dve.scalar_tensor_tensor(gates[:, t, 0:D], gates[:, t, 0:D], r_x[:, t:t + 1], grow[:, :],
                                         ALU.mult, ALU.mult).then_inc(xn_done, 1)
            for t in range(TILES):
                for s in range(2):
                    halve_lo("x", s, t, 4, lhi, llo)
            for s in range(2):
                copy_group(("cache_k", 0, s), kT[:, 4 * s:4 * s + 4, SEQ:SEQ + PAST], P, 4, P)
            copy_group(("cache_ckv", 0, 0), ckvT[:, :, TOK:TOK + P], P, 2, P)
            dve.wait_ge(lam_exp, 1)
            link(dve.tensor_tensor(lamv[:, 4:5], lamv[:, 3:4], lamv[:, 2:3], ALU.subtract))
            dve.tensor_scalar(pair[:, 1:2], lamv[:, 4:5], -LAM_INIT, None, ALU.add)
            dve.tensor_scalar(pair[:, 0:1], lamv[:, 4:5], 0.0, 1.0, ALU.mult, ALU.add)
            link(dve.tensor_scalar(gvec[:, gv["diff_sub"], :], gvec[:, gv["diff_sub"], :], 1.0 - LAM_INIT, None,
                                   ALU.mult))
            run(first)

            def attention(ph, maps):
                n_units = H * TILES

                def maxima(n):
                    hd, t = divmod(n, TILES)
                    rows, nk, b = ROWS[t], sum(r for _, r, _ in key_tiles(t)), 2 * (n % 2)
                    dve.wait_ge(s_done[ph], n + 1)
                    if n >= 2:
                        dve.wait_ge(exp_done[ph], maps * (n - 1))
                    dve.tensor_reduce(negmax[0:rows, b:b + maps], acc[0:rows, b:b + maps, 0:nk], AX.X, ALU.max,
                                      negate=True).then_inc(nm_done[ph], 1)

                def combine(n):
                    hd, t = divmod(n, TILES)
                    rows, nk, b, q = ROWS[t], sum(r for _, r, _ in key_tiles(t)), 2 * (n % 2), 2 * (n % 4)
                    dve.wait_ge(exp_done[ph], maps * (n + 1))
                    rr = rsum[0:rows, q:q + maps]
                    ins = dve.reciprocal(rr, sums[0:rows, b:b + maps])
                    if ph == "a":
                        ins.then_inc(comb_done[ph], 1)
                        return
                    link(ins)
                    link(dve.tensor_tensor(rr, rr, pair[0:rows, :], ALU.mult))
                    p0, p1 = pr[0:rows, n % 2, 0, 0:nk], pr[0:rows, n % 2, 1, 0:nk]
                    link(dve.tensor_scalar(p1, p1, rsum[0:rows, q + 1:q + 2], None, ALU.mult))
                    dve.scalar_tensor_tensor(p0, p0, rsum[0:rows, q:q + 1], p1, ALU.mult,
                                             ALU.add).then_inc(comb_done[ph], 1)

                def gate_out(n):
                    hd, t = divmod(n, TILES)
                    rows = ROWS[t]
                    dve.wait_ge(pv_done[ph], n + 1)
                    out = acc[0:rows, 4 + n % 2, 0:VB]
                    if ph == "b":
                        dve.wait_ge(sqo_done, n + 1)
                        g = gates[0:rows, t, D + hd * VB:D + hd * VB + VB]
                        dve.tensor_tensor(g, out, g, ALU.mult).then_inc(o_done[ph], 1)
                    else:
                        g = gates[0:rows, t, hd * VB:hd * VB + VB]
                        dve.wait_ge(comb_done[ph], n + 1)
                        dve.scalar_tensor_tensor(g, out, rsum[0:rows, 2 * (n % 4):2 * (n % 4) + 1], g, ALU.mult,
                                                 ALU.mult).then_inc(o_done[ph], 1)

                for n in range(n_units + 2):
                    if n < n_units:
                        maxima(n)
                    if 1 <= n <= n_units:
                        combine(n - 1)
                    if n >= 2:
                        gate_out(n - 2)

            attention("b", 2)
            dve.wait_ge(ro_done, 1)
            dve.wait_ge(o_done["b"], H * TILES)
            heads = [gates[:, t, D:2 * D].rearrange("p (h v) -> p h v", v=VB) for t in range(TILES)]
            for t in range(TILES):
                link(dve.tensor_tensor(heads[t], heads[t],
                                       r_o[:, t * H:t * H + H].unsqueeze(2).broadcast_to([P, H, VB]), ALU.mult))
                ins = dve.tensor_tensor(heads[t], heads[t],
                                        gvec[:, gv["diff_sub"], :].unsqueeze(1).broadcast_to([P, H, VB]), ALU.mult)
            link(ins)
            run(latent)
            attention("a", 1)
            dve.wait_ge(o_done["a"], H * TILES)
            for t in range(TILES):
                dve.tensor_tensor(gates[:, t, 0:D], gates[:, t, 0:D], gates[:, t, D:2 * D],
                                  ALU.add).then_inc(merged_done, 1)
            for t in range(TILES):
                for s in range(2):
                    halve_lo("merged", s, t, 4, lhi2, llo2)
            run(outp)
            late_vector(dve, link, halve_lo, run)

        @block.gpsimd
        def _(pool):
            own = [0]

            def link(ins):
                own[0] += 1
                ins.then_inc(pool_own, 1)
                pool.wait_ge(pool_own, own[0])

            def inverse_rms(dst, src, n, size, eps_scale=1.0):
                f = eps_scale
                link(pool.tensor_scalar(src, src, 1.0 / (size * f), EPS / f, ALU.mult, ALU.add))
                return pool.tensor_tensor(dst, src, neghalf[:, 0:n], ALU.pow)

            link(pool.memset(small[:, :], 0.0))
            link(pool.memset(neghalf[:, :], -0.5))
            pool.memset(gates[DEC:P, PT, 0:D], 0.0).then_inc(zeroed, 1)

            pool.wait_ge(x_sq, TILES)
            inverse_rms(r_x, ss_x, TILES, D).then_inc(x_rstd, 1)

            def factors(i):
                c, gs, m = items[i], groups(i), normitems[i]
                total = sum(g[1] for g in gs)
                pool.wait_ge(ss_done, y_norm[(i, c.tiles - 1)] + 1)
                if m >= 2:
                    before = [n for n in normitems if normitems[n] == m - 2][0]
                    pool.wait_ge(y_done, y_index[(before, items[before].tiles - 1)] + 1)
                n = c.tiles * total
                src = ss_z[m % 2][:, 0:n]
                view = src.rearrange("p (t g) -> p t g", g=total)
                at = 0
                for off, k, size, _, f in gs:
                    part_ = view[:, :, at:at + k]
                    ins = pool.tensor_scalar(part_, part_, 1.0 / (size * f), EPS / f, ALU.mult, ALU.add)
                    at += k
                link(ins)
                pool.tensor_tensor(r_z[m % 2][:, 0:n], src, neghalf[:, 0:n], ALU.pow).then_inc(rstd_done, 1)

            def send(i):
                c = items[i]
                if not dmas_of(i):
                    return
                for t in range(c.tiles):
                    if c.kind == "norm":
                        pool.wait_ge(y_done, y_index[(i, t)] + 1)
                    else:
                        pool.wait_ge(z_copied, units[(i, t)] + 1)
                    cols = slice(512 * c.half, 512 * c.half + 512)
                    if c.name == "uv":
                        pool.dma_start(va_rows[t * P:t * P + P, cols], zs[:, t, :]).then_inc(outz[t], 16)
                        continue
                    rows = slice(t * P, t * P + P) if t < PT else slice(0, DEC)
                    who = "_p" if t < PT else "_s"
                    if c.name == "ckv":
                        pool.dma_start(o["ckv" + who][rows, :], zs[0:ROWS[t], t, 0:KVL]).then_inc(outz[t], 16)
                        pool.dma_start(o["kr" + who][rows, :], zs[0:ROWS[t], t, KVL:KVL + RD]).then_inc(outz[t], 16)
                    else:
                        pool.dma_start(o[c.name + who][rows, cols], zs[0:ROWS[t], t, :]).then_inc(outz[t], 16)

            for i in phase_items(first):
                if items[i].kind == "norm":
                    factors(i)
                send(i)
            pool.wait_ge(sqo_done, H * TILES)
            inverse_rms(r_o, ss_o, H * TILES, VB).then_inc(ro_done, 1)
            for i in phase_items(latent):
                if items[i].kind == "norm":
                    factors(i)
                send(i)
            pool.wait_ge(t_copied, copied[("merged", TILES - 1, 1)] + 1)
            pool.memset(h[DEC:P, PT, :], 0.0).then_inc(zeroed, 1)
            pool.wait_ge(zeroed, 2)
            late_gpsimd(pool, link, inverse_rms)


def constants():
    pos = np.concatenate([np.arange(SEQ), PAST + np.arange(DEC), np.zeros(TOK - SEQ - DEC)]).astype(np.float32)
    parts = []
    for r in (RD, ROT):
        half = r // 2
        inv = np.float32(ROPE_THETA) ** (-np.arange(half, dtype=np.float32) * np.float32(2.0 / r))
        ang = pos[:, None] * inv[None, :]
        c, s = np.cos(ang), np.sin(ang)
        parts += [c, c, -s, s]
    iota = np.zeros((1, 320), np.float32)
    iota[0, 0:P] = np.arange(P)
    iota[0, P:P + NBLK + 1] = P * np.arange(NBLK + 1)
    iota[0, 192:192 + NE] = np.arange(NE)
    n = np.arange(TOK)
    valid = (n < SEQ + DEC).astype(np.float32)
    return {
        "c_ident": np.eye(P, dtype=np.float32),
        "c_rope": np.concatenate(parts, axis=1).astype(np.float32),
        "c_mask": np.concatenate([(np.arange(P) < CHUNK).astype(np.float32), np.full(CHUNK, -BIG, np.float32)])[None],
        "c_before": (np.arange(P)[:, None] < np.arange(P)[None, :]).astype(np.float32),
        "c_iota": iota,
        "c_token": np.stack([n + 1.0, valid, valid - 1.0], axis=1).astype(np.float32),
    }


def kernel(**inputs):
    from concourse import bacc
    from concourse.bass_utils import run_bass_kernel_spmd

    def flat(name, *shape):
        return np.ascontiguousarray(inputs[name]).reshape(shape)

    arrays = {
        "x": np.concatenate([flat("x_prompt", SEQ, D), flat("x_sample", DEC, D)]),
        "p": np.concatenate([flat("p_prompt", SEQ, DP), flat("p_sample", DEC, DP)]),
        "cache_ckv": flat("cache_mla_ckv", PAST, KVL), "cache_krope": flat("cache_mla_krope", PAST, RD),
        "cache_k": flat("cache_diff_k", PAST, D), "cache_v": flat("cache_diff_v", PAST, D),
        "w_in": flat("w_in", D, -1), "w_uq": flat("w_uq", QL, H * HD), "w_uk": flat("w_uk", KVL, H * NOPE),
        "w_uv": flat("w_uv", KVL, D), "w_out": flat("w_out", D, D),
        "w_rg": flat("w_router_grp", D, NG), "w_re": flat("w_router_exp", D, NE),
        "w_ei": flat("w_exp_in", NE * D, 2 * DE), "w_eo": flat("w_exp_out", NE * DE, D),
        "w_ple_gate": flat("w_ple_gate", D, D), "w_ple_proj": flat("w_ple_proj", DP, D),
        "b_rg": flat("b_router_grp", NG), "b_re": flat("b_router_exp", NE),
    }
    for g in ("g_mix", "g_q_lat", "g_kv_lat", "g_mla_qn", "g_mla_qr", "g_mla_kn", "g_mla_kr", "g_diff_q", "g_diff_k",
              "lambda_q1", "lambda_k1", "lambda_q2", "lambda_k2", "g_diff_sub", "g_ffn", "g_ple"):
        arrays[g] = flat(g, -1)
    arrays.update(constants())
    outs = {"y_p": (SEQ, D), "y_s": (DEC, D), "ckv_p": (SEQ, KVL), "kr_p": (SEQ, RD), "dk_p": (SEQ, D),
            "dv_p": (SEQ, D), "ckv_s": (DEC, KVL), "kr_s": (DEC, RD), "dk_s": (DEC, D), "dv_s": (DEC, D)}
    nc = bacc.Bacc("TRN2", target_bir_lowering=False, num_devices=1)
    a = {n: nc.dram_tensor("in_" + n, v.shape, mybir.dt.from_np(v.dtype), kind="ExternalInput").ap()
         for n, v in arrays.items()}
    o = {n: nc.dram_tensor("out_" + n, s, F32, kind="ExternalOutput").ap() for n, s in outs.items()}
    trunk(nc, a, o)
    r = run_bass_kernel_spmd(nc, [{"in_" + n: v for n, v in arrays.items()}], core_ids=[0]).results[0]
    g = {n: r["out_" + n] for n in outs}
    res = [g["y_p"].reshape(1, SEQ, D), g["y_s"].reshape(1, DEC, D)]
    for who, n in (("p", SEQ), ("s", DEC)):
        res += [g["ckv_" + who].reshape(1, 1, n, KVL), g["kr_" + who].reshape(1, 1, n, RD),
                g["dk_" + who].reshape(1, 1, n, H, 2, DB), g["dv_" + who].reshape(1, 1, n, H, VB)]
    return tuple(res)
```

```python
import math
from contextlib import ExitStack

import numpy as np
import concourse.bass as bass
from concourse import mybir

F32 = mybir.dt.float32
F32R = mybir.dt.float32r
I32 = mybir.dt.int32
U32 = mybir.dt.uint32
ACT = mybir.ActivationFunctionType
ALU = mybir.AluOpType
AX = mybir.AxisListType

P = 128
D = 1024
SEQ, DEC, PAST = 512, 64, 128
CHUNK = 64
PT = SEQ // P
TILES = PT + 1
ROWS = [P] * PT + [DEC]
TOK = TILES * P
CACHE = TILES
KEYS = SEQ + PAST + DEC
KCOL = [t * P for t in range(PT)] + [SEQ + PAST, SEQ]
EPS = 1e-6
H = 8
QL, KVL, NOPE, RD = 384, 256, 64, 32
HD = NOPE + RD
MLA_SCALE = 1.0 / math.sqrt(HD)
DB = 64
VB = 128
ROT = DB // 4
DIFF_SCALE = 1.0 / math.sqrt(DB)
LAM_INIT = 0.8 - 0.6 * math.exp(-0.3 * 0)
NG, EPG = 4, 8
NE = NG * EPG
DE = 256
DP = 256
NBLK = NE + (2 * (SEQ + DEC) - NE) // P
REAL = SEQ + DEC
NASSIGN = 2 * REAL
BIG = 1e30
ROPE_THETA = 500000.0


class Item:

    def __init__(self, name, kind, src, col, width, kt, tiles, lhs, split, half=0):
        self.name, self.kind, self.src, self.col, self.width = name, kind, src, col, width
        self.kt, self.tiles, self.lhs, self.split, self.half = kt, tiles, lhs, split, half


def plan():
    columns, at = {}, 0
    for name, width in (("q_lat", QL), ("ckv", KVL + RD), ("dq", D), ("dk", D), ("dv", D), ("ga", D), ("gb", D)):
        columns[name] = at
        at += width

    def halves(name, kind, half):
        return Item(name, kind, "w_in", columns[name] + 512 * half, 512, 8, TILES, "act", True, half)

    first = [Item("q_lat", "norm", "w_in", columns["q_lat"], QL, 8, TILES, "act", True),
             Item("ckv", "norm", "w_in", columns["ckv"], KVL + RD, 8, TILES, "act", True),
             halves("dv", "store", 0),
             halves("dk", "norm", 0), halves("ga", "gate", 0), halves("dk", "norm", 1), halves("ga", "gate", 1),
             halves("dq", "norm", 0), halves("gb", "gate", 0), halves("dq", "norm", 1), halves("gb", "gate", 1),
             halves("dv", "store", 1)]
    uq = [Item("uq", "norm", "w_uq", 384 * half, 384, 3, TILES, "q_lat", False, half) for half in range(2)]
    uv = [Item("uv", "store", "w_uv", 512 * half, 512, 2, TILES + 1, "ckv", False, half) for half in range(2)]
    latent = [Item("uk", "norm", "w_uk", 0, 512, 2, TILES + 1, "ckv", False), uv[0], uq[0], uv[1], uq[1]]
    out = [Item("out", "residual", "w_out", 512 * half, 512, 8, TILES, "act", True, half) for half in range(2)]
    ple = [Item("proj", "store", "w_ple_proj", 512 * half, 512, 2, TILES, "pe", True, half) for half in range(2)]
    ple += [Item("pgate", "ple", "w_ple_gate", 512 * half, 512, 8, TILES, "act", True, half) for half in range(2)]
    return first, latent, out, ple


def number(keys):
    return {k: i for i, k in enumerate(keys)}


def trunk(nc, a, o):
    first, latent, outp, ple = plan()
    phases = [first, latent, outp, ple]
    items = [c for ph in phases for c in ph]
    start = {id(ph): sum(len(x) for x in phases[:i]) for i, ph in enumerate(phases)}

    units = number([(i, t) for i, c in enumerate(items) for t in range(c.tiles)])
    granules = number([(i, g) for i, c in enumerate(items) if c.split for g in range(c.kt // 2)])
    normed = number([(i, t) for i, c in enumerate(items) if c.kind == "norm" for t in range(c.tiles)])
    normitems = number([i for i, c in enumerate(items) if c.kind == "norm"])
    RAW, RING = 3, 2
    QZ = 3
    DEFERRED = [range(0, 2), range(2, 4), range(4, TILES), range(0)]
    EG, ERING = 12, 6
    PAIRS = (NBLK + 1) // 2

    def subs(i):
        c = items[i]
        return 2 if c.name == "uk" else 1 if c.kind == "norm" else 0

    tgroups = [("x", t, s) for t in range(TILES) for s in range(2)]
    tgroups += [("cache_k", 0, 0), ("cache_k", 0, 1), ("cache_ckv", 0, 0)]
    tgroups += [(i, t, s) for i in range(len(first)) for t in range(items[i].tiles) for s in range(subs(i))]
    tgroups += [("attn_b", n, 0) for n in range(H * TILES)]
    tgroups += [(i, t, s) for i in range(len(first), len(first) + len(latent))
                for t in range(items[i].tiles) for s in range(subs(i))]
    tgroups += [("attn_a", n, 0) for n in range(H * TILES)]
    tgroups += [("merged", t, s) for t in range(TILES) for s in range(2)]
    tgroups += [("hn", t, s) for t in range(TILES) for s in range(2)]
    tgroups += [("pe", t, 0) for t in range(TILES)]
    tgroups += [("hp", t, s) for t in range(TILES) for s in range(2)]
    tg = number(tgroups)

    with ExitStack() as ctx:
        def sb(name, shape, dt=F32, c=ctx):
            return c.enter_context(nc.sbuf_tensor(name, shape, dt))

        def sem(name):
            return ctx.enter_context(nc.semaphore(name))

        def dram(name, shape, dt=F32):
            return nc.dram_tensor(name, shape, dt, kind="Internal").ap()

        acc = ctx.enter_context(nc.psum_tensor("acc", [P, 6, 512], F32))
        tp = ctx.enter_context(nc.psum_tensor("tp", [P, 2, 512], F32))

        va_rows = dram("va_rows", [TOK + P, D])
        hn_rows = dram("hn_rows", [REAL, D])
        y_rows = dram("y_rows", [NASSIGN, D])

        ident = sb("ident", [P, P])
        small = sb("small", [P, 512])
        raw = sb("raw", [P, RAW, 2, 512])
        whi = sb("whi", [P, RING, 2, 512], F32R)
        wlo = sb("wlo", [P, RING, 2, 512], F32R)
        grow = sb("grow", [P, D])
        neghalf = sb("neghalf", [P, 64])

        mask = sb("mask", [1, P + 64])
        rope = sb("rope", [P, TILES, 96])
        zs = sb("zs", [P, 6, 512])
        sq = sb("sq", [P, 512])
        rot = sb("rot", [P, 2, 128])

        early = ExitStack()
        gates = sb("gates", [P, TILES, 2 * D], c=early)
        q_latT = sb("q_latT", [P, 3, TOK], c=early)
        ckvT = sb("ckvT", [P, 2, TOK + P], c=early)
        krope = sb("krope", [P, 6, RD], c=early)
        qT = sb("qT", [P, H, SEQ + DEC], c=early)
        kT = sb("kT", [P, H, KEYS], c=early)
        vh = sb("vh", [P, 2, 6, VB], c=early)
        gq_lat = sb("gq_lat", [P, QL], c=early)
        gkv = sb("gkv", [P, KVL + RD], c=early)
        gvec = sb("gvec", [P, 6, P], c=early)
        qz = sb("qz", [P, QZ, 2, P], c=early)
        halves = ExitStack()
        lhi = sb("lhi", [P, 8, TOK], F32R, c=halves)
        llo = sb("llo", [P, 8, TOK], F32R, c=halves)
        halves.close()
        inner = ExitStack()
        w_uq = sb("w_uq", [P, 3, 768], c=inner)
        w_uk = sb("w_uk", [P, 2, 512], c=inner)
        w_uv = sb("w_uv", [P, 2, 1024], c=inner)
        pr = sb("pr", [P, 3, 2, 512], c=inner)
        prT = sb("prT", [P, 2, 4, P], c=inner)
        inner.close()
        halves2 = ExitStack()
        lhi2 = sb("lhi2", [P, 8, TOK], F32R, c=halves2)
        llo2 = sb("llo2", [P, 8, TOK], F32R, c=halves2)
        halves2.close()
        early.close()
        h = sb("h", [P, TILES, D])
        src_row = sb("src_row", [P, NBLK + 6], I32)
        dst_row = sb("dst_row", [P, NBLK + 4], I32)
        gate_of = sb("gate_of", [P, NBLK + 2])
        expert_of = sb("expert_of", [1, NBLK + 2], I32)
        n_blocks = sb("n_blocks", [1, 2], I32)
        row_in = sb("row_in", [P, 2, 1], I32)
        row_out = sb("row_out", [P, 2, 1], I32)
        gate_in = sb("gate_in", [P, 2, 1])
        raw_e = sb("raw_e", [P, EG, D])
        route = ExitStack()
        xn = sb("xn", [P, 2, D], c=route)
        xnT = sb("xnT", [P, 2, 8, P], c=route)
        w_r = sb("w_r", [P, 8, NG + NE], c=route)
        b_r = sb("b_r", [P, NG + NE], c=route)
        iota = sb("iota", [P, 320], c=route)
        token = sb("token", [P, TILES, 3], c=route)
        before = sb("before", [P, P], c=route)
        ones = sb("ones", [P, P], c=route)
        rt = sb("rt", [P, 3008], c=route)
        route.close()
        moe = ExitStack()
        ehi = sb("ehi", [P, ERING, D], F32R, c=moe)
        elo = sb("elo", [P, ERING, D], F32R, c=moe)
        xg = sb("xg", [P, 2, D], c=moe)
        xhi = sb("xhi", [P, 2, 8, P], F32R, c=moe)
        xlo = sb("xlo", [P, 2, 8, P], F32R, c=moe)
        gg = sb("gg", [P, 2, DE], c=moe)
        ghi = sb("ghi", [P, 2, 2, P], F32R, c=moe)
        glo = sb("glo", [P, 2, 2, P], F32R, c=moe)
        ye = zs[:, 0:4, :].rearrange("p (b a) n -> p b (a n)", b=2)
        moe.close()
        tail = ExitStack()
        ptok = sb("ptok", [P, TILES, DP], c=tail)
        phi = sb("phi", [P, 2, TOK], F32R, c=tail)
        plo = sb("plo", [P, 2, TOK], F32R, c=tail)
        ysum = raw_e[:, 0:4, :].rearrange("p (b j) n -> p b j n", b=2)
        hp = raw_e[:, 4:6, :]
        pj = raw_e[:, 6:11, :]
        grow2 = raw_e[:, 11, :]
        tail.close()

        def part(at, n):
            return small[:, at:at + n]

        ss_z = [part(0, 48), part(48, 48)]
        r_z = [part(96, 48), part(144, 48)]
        ss_x, r_x = part(192, 5), part(200, 5)
        ss_o, r_o = part(208, 40), part(248, 40)
        negmax, sums, rsum = part(288, 4), part(292, 4), part(296, 8)
        lamv = part(304, 8)
        pair = part(312, 2)

        ld_const = sem("ld_const")
        ld_x = [sem(f"ld_x{t}") for t in range(TILES)]
        ld_raw = [sem(f"ld_raw{s}") for s in range(RAW)]
        ld_v = [sem(f"ld_v{s}") for s in range(2)]
        ld_wu = sem("ld_wu")
        zeroed = sem("zeroed")
        hi_done, lo_done, w_used = sem("hi_done"), sem("lo_done"), sem("w_used")
        z_done, z_copied = sem("z_done"), sem("z_copied")
        sq_done, ss_done, rstd_done, y_done = sem("sq_done"), sem("ss_done"), sem("rstd_done"), sem("y_done")
        t_done, t_copied, hi_copied, pt_copied = sem("t_done"), sem("t_copied"), sem("hi_copied"), sem("pt_copied")
        x_sq, x_rstd, xn_done = sem("x_sq"), sem("x_rstd"), sem("xn_done")
        outz = [sem(f"outz{t}") for t in range(6)]
        lam_dots, lam_exp, lam_done = sem("lam_dots"), sem("lam_exp"), sem("lam_done")
        s_done = {p: sem(f"s_done_{p}") for p in "ba"}
        qz_done = sem("qz_done")
        nm_done = {p: sem(f"nm_done_{p}") for p in "ba"}
        exp_done = {p: sem(f"exp_done_{p}") for p in "ba"}
        pv_done = {p: sem(f"pv_done_{p}") for p in "ba"}
        o_done = {p: sem(f"o_done_{p}") for p in "ba"}
        comb_done = {p: sem(f"comb_done_{p}") for p in "ba"}
        sqo_done, ro_done = sem("sqo_done"), sem("ro_done")
        merged_done = sem("merged_done")
        sub_done = sem("sub_done")
        ld_h = sem("ld_h")
        dve_own, act_own, pool_own = sem("dve_own"), sem("act_own"), sem("pool_own")

        copied = number([k for k in tgroups if k[0] not in ("attn_b", "attn_a")])
        pt = number([k for k in tgroups if k[0] in ("attn_b", "attn_a")])

        def wait_group_copied(eng, key):
            if key in copied:
                eng.wait_ge(t_copied, copied[key] + 1)
            else:
                eng.wait_ge(pt_copied, pt[key] + 1)

        def wait_bank_for(eng, key):
            if tg[key] >= 2:
                wait_group_copied(eng, tgroups[tg[key] - 2])

        def dmas_of(i):
            return {"ckv": 2, "dk": 1, "dv": 1, "uv": 1}.get(items[i].name, 0)

        def out_count(i, t):
            return sum(dmas_of(n) for n in range(i + 1) if items[n].tiles > t)

        def uses_zs(i):
            return items[i].kind in ("norm", "residual", "ple") or items[i].name == "dv"

        def deferred(i):
            ph = next(ph for ph in phases if i in phase_items(ph))
            return items[i].kind == "norm" and i + 2 in phase_items(ph) and not uses_zs(i + 1)

        def uv_tile(t):
            return raw[:, t // 2, t % 2, :]

        def kas(t):
            flat = [pr, prT, qz][max(t - 3, 0)][:, :, :, :].rearrange("p a b c -> p (a b c)")
            at = t * H * HD if t < 4 else 0
            return flat[:, at:at + H * HD]

        def wait_slot_free(eng, i, t):
            before = [n for n in range(i) if uses_zs(n) and items[n].tiles > t]
            if not before:
                return
            n = before[-1]
            c = items[n]
            if c.kind == "norm" and c.name != "uk":
                eng.wait_ge(t_done, tg[(n, t, subs(n) - 1)] + 1)
            if c.name == "uk":
                eng.wait_ge(y_done, y_index[(n, t)] + 1)
            if c.kind in ("residual", "ple"):
                eng.wait_ge(y_done, y_index[(n, t)] + 1)
            if out_count(n, t):
                eng.wait_ge(outz[t], 16 * out_count(n, t))

        y_norm = number([(i, t) for i, c in enumerate(items) if c.kind == "norm" for t in range(c.tiles)])

        def last_norm(ph):
            return [i for i in phase_items(ph) if items[i].kind == "norm"][-1]

        def y_norm_of_phase(ph):
            return sum(c.tiles for x in phases[:phases.index(ph) + 1] for c in x if c.kind == "norm")

        hi_index = number([k for k in tgroups if k[0] in ("x", "merged", "pe", "hp")])
        y_index = number([(i, t) for i, c in enumerate(items) if c.kind in ("norm", "residual", "ple")
                          for t in range(c.tiles)])

        def groups(i):
            return {"q_lat": [(0, 1, QL, QL, 1.0)],
                    "ckv": [(0, 1, KVL, KVL, 1.0), (KVL, 1, RD, RD, 1.0)],
                    "dq": [(0, 8, DB, DB, DIFF_SCALE ** 2)],
                    "dk": [(0, 8, DB, DB, 1.0)],
                    "uq": [(0, 4, NOPE, HD, 1.0 / HD), (NOPE, 4, RD, HD, 1.0 / HD)],
                    "uk": [(0, 8, NOPE, NOPE, 1.0)]}[items[i].name]

        def grouped(tile, g):
            off, n, size, stride, _ = g
            if n == 1:
                return tile[:, off:off + size].unsqueeze(1)
            return tile[:, 0:n * stride].rearrange("p (n s) -> p n s", s=stride)[:, :, off % stride:off % stride + size]

        inner_granules = number([k for k in granules if k[1] < items[k[0]].kt // 2 - 1])
        granule_list = list(granules)

        def wait_ring_free(eng, n):
            if n < RING:
                return
            i, g = granule_list[n - RING]
            if (i, g) in inner_granules:
                eng.wait_ge(w_used, inner_granules[(i, g)] + 1)
            else:
                eng.wait_ge(z_done, units[(i, items[i].tiles - 1)] + 1)

        def phase_items(ph):
            return range(start[id(ph)], start[id(ph)] + len(ph))

        ds = bass.ds
        ss_h, r_h = part(320, 5), part(328, 5)
        ss_f, r_f = part(336, 5), part(344, 5)
        h_sq, h_rstd, hn_done, hn_sent = sem("h_sq"), sem("h_rstd"), sem("hn_done"), [sem(f"hn_sent{j}") for j in range(2)]
        ld_g, ld_late = sem("ld_g"), sem("ld_late")
        ones_set = sem("ones_set")
        logits_done, grp_shift, grp_exp, exp2_in, exp2_out = (
            sem("logits_done"), sem("grp_shift"), sem("grp_exp"), sem("exp2_in"), sem("exp2_out"))
        hot_done, rank_done, plan_in, plan_done, routed = (
            sem("hot_done"), sem("rank_done"), sem("plan_in"), sem("plan_done"), sem("routed"))
        ld_e = [sem(f"ld_e{j}") for j in range(EG)]
        ld_xg = [sem(f"ld_xg{j}") for j in range(2)]
        hi_e, lo_e, used_e, t_e, thi_e, tlo_e = (sem("hi_e"), sem("lo_e"), sem("used_e"), sem("t_e"), sem("thi_e"),
                                                 sem("tlo_e"))
        silu_e, g_e, ya_e, yd_e, sent_e = (sem("silu_e"), sem("g_e"), sem("ya_e"), sem("yd_e"),
                                           [sem(f"sent_e{j}") for j in range(2)])
        gate_e, own_e = sem("gate_e"), sem("own_e")
        left_e = sem("left_e")
        sp_steps = sem("sp_steps")
        pool_steps = sem("pool_steps")
        moe_done = sem("moe_done")
        ld_y, y_added, f_sq, f_rstd, fn_done, ld_p = (
            [sem(f"ld_y{j}") for j in range(2)], sem("y_added"), sem("f_sq"), sem("f_rstd"), sem("fn_done"), sem("ld_p"))
        st_y = sem("st_y")
        ORDER = [(0, g) for g in range(4)] + [(1, g) for g in range(4)] + [(0, 4), (0, 5), (1, 4), (1, 5)]
        residual_last = start[id(outp)] + 1
        ple_first = start[id(ple)]

        def late_sync(sp):
            for dst, src in ((w_r[:, :, 0:NG], a["w_rg"].rearrange("(k p) n -> p k n", p=P)),
                             (w_r[:, :, NG:NG + NE], a["w_re"].rearrange("(k p) n -> p k n", p=P)),
                             (b_r[:, 0:NG], a["b_rg"].partition_broadcast(P)),
                             (b_r[:, NG:NG + NE], a["b_re"].partition_broadcast(P)),
                             (iota[:, :], a["c_iota"].partition_broadcast(P)),
                             (token[:, :, :], a["c_token"].rearrange("(t p) n -> p t n", p=P)),
                             (before[:, :], a["c_before"])):
                sp.dma_start(dst, src).then_inc(ld_late, 16)
            every = [(i, g) for i in phase_items(ple) for g in range(items[i].kt // 2)]
            for i, g in every[:RAW]:
                load_granule(sp, i, g)
            sp.wait_ge(routed, 1)
            n = sp.value_load(n_blocks[0:1, 0:1], min_val=1, max_val=NBLK)

            def load_pair(first_block, queue, before=None):
                e = [sp.value_load(expert_of[0:1, ds(first_block + j, 1)], min_val=0, max_val=NE - 1)
                     for j in range(2)]
                for q in queue:
                    b, g = ORDER[q]
                    if g < 4:
                        src = a["w_ei"][ds(e[b] * D + 2 * g * P, 2 * P), :].rearrange("(k p) n -> p k n", p=P)
                        dst = raw_e[:, q, :].rearrange("p (k n) -> p k n", k=2)
                    else:
                        src = a["w_eo"][ds(e[b] * DE + (g - 4) * P, P), :]
                        dst = raw_e[:, q, :]
                    if before:
                        before(q)
                    sp.dma_start(dst, src).then_inc(ld_e[q], 16)

            load_pair(0, range(EG))
            with sp.Fori(0, PAIRS) as i:
                with sp.If(i * 2 < n):
                    def halved(q):
                        sp.wait_ge(lo_e, i * EG + (q + 1))

                    load_pair(i * 2 + 2, range(ERING), halved)
                    with sp.If(i * 2 + 2 < n):
                        load_pair(i * 2 + 2, range(ERING, EG), halved)
                    sp.sem_inc(sp_steps, 1)
            sp.wait_ge(moe_done, 1)
            sp.dma_start(grow2, a["g_ple"].partition_broadcast(P)).then_inc(ld_g, 16)
            for t in range(TILES):
                if t >= 2:
                    sp.wait_ge(y_added, t - 1)
                sp.dma_start(ysum[0:ROWS[t], t % 2, :, :],
                             y_rows.rearrange("(j n) d -> n j d", j=2)[t * P:t * P + ROWS[t], :, :]
                             ).then_inc(ld_y[t % 2], 16)
                sp.dma_start(ptok[0:ROWS[t], t, :], a["p"][t * P:t * P + ROWS[t], :]).then_inc(ld_p, 16)
            for i, g in every[RAW:]:
                load_granule(sp, i, g)

        def late_tensor(pe, turn, run):
            for t in range(TILES):
                pe.wait_ge(hn_done, t + 1)
                for s in range(2):
                    turn(("hn", t, s), [xn[:, t % 2, j * P:j * P + P] for j in range(4 * s, 4 * s + 4)])
                if t == 0:
                    pe.wait_ge(ld_late, 16 * 7)
                    pe.wait_ge(z_copied, units[(residual_last, TILES - 1)] + 1)
                pe.wait_ge(t_copied, copied[("hn", t, 1)] + 1)
                for k in range(8):
                    mm = pe.matmul(acc[:, t, 0:NG + NE], xnT[:, t % 2, k, :], w_r[:, k, :], start=(k == 0),
                                   stop=(k == 7))
                mm.then_inc(logits_done, 1)
            pe.wait_ge(hot_done, 1)
            pe.wait_ge(ones_set, 1)
            for t in range(TILES):
                for u in range(t + 1):
                    pe.matmul(acc[:, t, 0:NE], (before if u == t else ones)[:, :], R["hot"][:, u, :],
                              start=(u == 0), stop=(u == t))
            for u in range(TILES):
                mm = pe.matmul(acc[:, 5, 0:NE], ones[:, :], R["hot"][:, u, :], start=(u == 0), stop=(u == TILES - 1))
            mm.then_inc(rank_done, 1)
            pe.wait_ge(plan_in, 1)
            for n in range(2 * TILES):
                mm = pe.matmul(acc[:, 0, 0:3 * NBLK], R["in_block"][:, n, :], R["what"][:, n, :], start=(n == 0),
                               stop=(n == 2 * TILES - 1))
            mm.then_inc(plan_done, 1)

            pe.wait_ge(routed, 1)
            n = pe.value_load(n_blocks[0:1, 0:1], min_val=1, max_val=NBLK)

            def turn_tokens(b, s, bank):
                for j in range(4):
                    k = 4 * s + j
                    tr = pe.transpose(tp[:, bank, j * P:j * P + P], xg[:, b, k * P:k * P + P], ident[:, :])
                tr.then_inc(t_e, 1)

            for b in range(2):
                pe.wait_ge(ld_xg[b], 16)
                for s in range(2):
                    if b:
                        pe.wait_ge(tlo_e, s + 1)
                    turn_tokens(b, s, s)
            pe.wait_ge(tlo_e, 4)
            with pe.Fori(0, PAIRS) as i:
                with pe.If(i * 2 < n):
                    def bank_free(g):
                        pe.wait_ge(tlo_e, i * 6 + (g + 3))

                    def product(q, out, lhs, n0, n1, first_, last_):
                        for x, w in ((0, 0), (0, 1), (1, 0)):
                            mm = pe.matmul(out, lhs[x], (ehi, elo)[w][:, q % ERING, n0:n1],
                                           start=(first_ and x + w == 0), stop=(last_ and x == 1))
                        return mm

                    def hidden(b):
                        pe.wait_ge(tlo_e, i * 6 + (1, 3)[b])
                        for g in range(4):
                            q = 4 * b + g
                            pe.wait_ge(lo_e, i * EG + (q + 1))
                            for k in range(2):
                                kk = 2 * g + k
                                mm = product(q, acc[:, b, :], (xhi[:, b, kk, :], xlo[:, b, kk, :]), 512 * k,
                                             512 * k + 512, kk == 0, kk == 7)
                            mm.then_inc(used_e, 1)

                    def next_tokens(b, group):
                        pe.wait_ge(ld_xg[b], i * 16 + 32)
                        for s in range(2):
                            bank_free(group + s)
                            turn_tokens(b, s, (group + s) % 2)

                    def turn_hidden(b, group):
                        pe.wait_ge(g_e, i * 2 + (b + 1))
                        bank_free(group)
                        for j in range(2):
                            tr = pe.transpose(tp[:, group % 2, j * P:j * P + P], gg[:, b, j * P:j * P + P],
                                              ident[:, :])
                        tr.then_inc(t_e, 1)

                    def outputs(b, group):
                        pe.wait_ge(tlo_e, i * 6 + (group + 5))
                        pe.wait_ge(ya_e, i * 2 + (b + 1))
                        pe.wait_ge(yd_e, i * 2 + (b + 1))
                        for k in range(2):
                            q = 8 + 2 * b + k
                            pe.wait_ge(lo_e, i * EG + (q + 1))
                            for half in range(2):
                                mm = product(q, acc[:, 2 + 2 * b + half, :], (ghi[:, b, k, :], glo[:, b, k, :]),
                                             512 * half, 512 * half + 512, k == 0, k == 1)
                            mm.then_inc(used_e, 1)

                    hidden(0)
                    next_tokens(0, 0)
                    hidden(1)
                    turn_hidden(0, 2)
                    next_tokens(1, 3)
                    turn_hidden(1, 5)
                    outputs(0, 2)
                    outputs(1, 5)

            pe.wait_ge(moe_done, 1)
            pe.wait_ge(ld_p, 16 * TILES)
            pe.wait_ge(zeroed, 3)
            for t in range(TILES):
                turn(("pe", t, 0), [ptok[:, t, j * P:j * P + P] for j in range(2)])
            for t in range(TILES):
                pe.wait_ge(fn_done, t + 1)
                for s in range(2):
                    turn(("hp", t, s), [hp[:, t % 2, j * P:j * P + P] for j in range(4 * s, 4 * s + 4)])
            run(ple)

        def steps_of_pair(split, turned, hidden, turned_g, result):
            for q in (6, 7, 8):
                split(q)
            hidden(0)
            turned(0, 0, 0)
            turned(0, 1, 1)
            for q in (9, 10, 11):
                split(q)
            split(0, 1)
            hidden(1)
            turned_g(0, 2)
            turned(1, 0, 3)
            turned(1, 1, 4)
            turned_g(1, 5)
            split(1, 1)
            split(2, 1)
            split(3, 1)
            result(0)
            split(4, 1)
            split(5, 1)
            result(1)

        def squares_of_h(act, after, done, dst):
            for t in range(TILES):
                after(t)
                if t:
                    act.wait_ge(done, t)
                act.activation(zs[:, 4:6, :].rearrange("p a b -> p (a b)"), h[:, t, :], ACT.Square,
                               accum_out=dst[:, t:t + 1]).then_inc(done, 1)

        def late_scalar(act, link, halve_hi, run):
            squares_of_h(act, lambda t: act.wait_ge(y_done, y_index[(residual_last, TILES - 1)] + 1), h_sq, ss_h)
            act.wait_ge(grp_shift, 1)
            act.activation(R["e_grp"], R["shifted"], ACT.Exp).then_inc(grp_exp, 1)
            act.wait_ge(exp2_in, 1)
            act.activation(R["e2"], R["d2"], ACT.Exp).then_inc(exp2_out, 1)

            act.wait_ge(routed, 1)
            act.wait_ge(h_sq, TILES)
            n = act.value_load(n_blocks[0:1, 0:1], min_val=1, max_val=NBLK)

            def halve_weights(q):
                act.activation(ehi[:, q % ERING, :], raw_e[:, q, :], ACT.Copy).then_inc(hi_e, 1)

            def halve_tokens(b, s, bank):
                act.activation(xhi[:, b, 4 * s:4 * s + 4, :], tp[:, bank, :].rearrange("p (k r) -> p k r", r=P),
                               ACT.Copy).then_inc(thi_e, 1)

            for q in range(2):
                act.wait_ge(ld_e[q], 16)
                halve_weights(q)
            for g in range(4):
                act.wait_ge(t_e, g + 1)
                halve_tokens(g // 2, g % 2, g % 2)
            for q in range(2, ERING):
                act.wait_ge(ld_e[q], 16)
                halve_weights(q)
            with act.Fori(0, PAIRS) as i:
                with act.If(i * 2 < n):
                    def split(q, next_=0):
                        act.wait_ge(ld_e[q], i * 16 + 16 * (1 + next_))
                        act.wait_ge(used_e, i * EG + (EG * next_ + q - ERING + 1))
                        halve_weights(q)

                    def turned(b, s, group):
                        act.wait_ge(t_e, i * 6 + (group + 5))
                        halve_tokens(b, s, group % 2)

                    def silu(b):
                        act.wait_ge(used_e, i * EG + (4 * b + 4))
                        act.activation(gg[:, b, :], acc[:, b, 0:DE], ACT.Silu).then_inc(silu_e, 1)

                    def turned_g(b, group):
                        act.wait_ge(t_e, i * 6 + (group + 5))
                        act.activation(ghi[:, b, :, :], tp[:, group % 2, 0:DE].rearrange("p (k r) -> p k r", r=P),
                                       ACT.Copy).then_inc(thi_e, 1)

                    def result(b):
                        act.wait_ge(used_e, i * EG + (2 * b + 10))
                        act.wait_ge(gate_e, i * 2 + (b + 1))
                        act.wait_ge(left_e, i * 2 + (b + 1))
                        act.activation(ye[:, b, 0:512], acc[:, 2 + 2 * b, :], ACT.Copy,
                                       scale=gate_in[:, b, :]).then_inc(ya_e, 1)

                    steps_of_pair(split, turned, silu, turned_g, result)

            squares_of_h(act, lambda t: act.wait_ge(y_added, t + 1), f_sq, ss_f)
            for t in range(TILES):
                halve_hi("pe", 0, t, 2, phi)
            for t in range(TILES):
                for s in range(2):
                    halve_hi("hp", s, t, 4, lhi2)
            run(ple)

        R, at = {}, 0
        for name, shape in (("lg", (TILES, 8)), ("m8", (TILES, 8)), ("le", (TILES, NE)), ("v8", (TILES, 8)),
                            ("shifted", (TILES, NG)), ("e_grp", (TILES, NG)), ("pen", (TILES, NG)),
                            ("gsum", (TILES,)), ("gidx", (TILES,)), ("d2", (TILES,)), ("e2", (TILES,)),
                            ("idx", (2, TILES)), ("w", (2, TILES)), ("hot1", (2, TILES, NE)), ("hot", (TILES, NE)),
                            ("cnt", (NE,)), ("cum", (NE,)), ("startof", (NE,)), ("slot", (2 * TILES,)),
                            ("nge", (2 * TILES,))):
            n = int(np.prod(shape))
            v = rt[:, at:at + n]
            names = "abc"[:len(shape)]
            if len(shape) > 1:
                v = v.rearrange(f"p ({' '.join(names)}) -> p {' '.join(names)}", **dict(zip(names, shape)))
            R[name] = v
            at += n
        R["i8"] = rt[:, at:at + 8 * TILES].bitcast(U32).rearrange("p (a b) -> p a b", b=8)
        at += 8 * TILES
        base = at
        R["slotbase"] = rt[:, at:at + TILES * NE].rearrange("p (a b) -> p a b", b=NE)
        big = xn[:, :, :].rearrange("p a b -> p (a b)")
        R["in_block"] = big[:, 0:2 * TILES * P].rearrange("p (a b) -> p a b", b=P)
        R["ge"] = big[:, 1280:1280 + 10 * (NBLK + 1)].rearrange("p (a b) -> p a b", b=NBLK + 1)
        bigT = xnT[:, :, :, :].rearrange("p a b c -> p (a b c)")
        R["what"] = bigT[:, 0:10 * 3 * NBLK].rearrange("p (a b) -> p a b", b=3 * NBLK)
        at = base + TILES * NE
        R["oh_blk"] = rt[:, at:at + 10 * NBLK].rearrange("p (a b) -> p a b", b=NBLK)
        at += 10 * NBLK
        R["pl"] = rt[:, at:at + 3 * NBLK].rearrange("p (a b) -> p a b", b=NBLK)
        at += 3 * NBLK
        R["tmp"] = rt[:, at:at + NBLK * NE // 2]
        at += NBLK * NE // 2
        assert at <= 3008, at
        assert 1280 + 10 * (NBLK + 1) <= 2 * D

        def late_vector(dve, link, halve_lo, run):
            io128, io_blk, io_e = iota[:, 0:P], iota[:, P:P + NBLK + 1], iota[:, 192:192 + NE]
            dve.wait_ge(ld_g, 16)
            dve.wait_ge(h_rstd, 1)

            def copy_hn(t):
                for s in range(2):
                    dve.wait_ge(t_done, tg[("hn", t, s)] + 1)
                    if t >= 2:
                        dve.wait_ge(logits_done, t - 1)
                    dve.tensor_copy(xnT[:, t % 2, 4 * s:4 * s + 4, :],
                                    tp[:, tg[("hn", t, s)] % 2, :].rearrange("p (k r) -> p k r", r=P)
                                    ).then_inc(t_copied, 1)

            for t in range(TILES):
                if t >= 2:
                    dve.wait_ge(hn_sent[t % 2], 16 * (t // 2))
                dve.scalar_tensor_tensor(xn[:, t % 2, :], h[:, t, :], r_h[:, t:t + 1], grow[:, :], ALU.mult,
                                         ALU.mult).then_inc(hn_done, 1)
                if t >= 1:
                    copy_hn(t - 1)
            copy_hn(TILES - 1)
            dve.wait_ge(ld_late, 16 * 7)
            for j in range(2):
                dve.wait_ge(hn_sent[j], 16 * ((TILES - j + 1) // 2))
            dve.wait_ge(logits_done, TILES)
            lgt = acc[:, 0:TILES, 0:NG + NE]
            dve.memset(R["lg"], -3e38)
            link(dve.tensor_tensor(R["le"], lgt[:, :, NG:NG + NE],
                                   b_r[:, NG:NG + NE].unsqueeze(1).broadcast_to([P, TILES, NE]), ALU.add))
            link(dve.tensor_tensor(R["lg"][:, :, 0:NG], lgt[:, :, 0:NG],
                                   b_r[:, 0:NG].unsqueeze(1).broadcast_to([P, TILES, NG]), ALU.add))
            for t in range(TILES):
                ins = dve.max(R["m8"][:, t, :], R["lg"][:, t, :])
            link(ins)
            dve.tensor_tensor(R["shifted"], R["lg"][:, :, 0:NG], R["m8"][:, :, 0:1].broadcast_to([P, TILES, NG]),
                              ALU.subtract).then_inc(grp_shift, 1)
            for t in range(TILES):
                ins = dve.max_index(R["i8"][:, t, :], R["m8"][:, t, :], R["lg"][:, t, :])
            link(ins)
            link(dve.tensor_copy(R["gidx"], R["i8"][:, :, 0]))
            link(dve.tensor_tensor(R["pen"], R["gidx"].unsqueeze(2).broadcast_to([P, TILES, NG]),
                                   io_e[:, 0:NG].unsqueeze(1).broadcast_to([P, TILES, NG]), ALU.is_equal))
            link(dve.tensor_scalar(R["pen"], R["pen"], -1.0, BIG, ALU.add, ALU.mult))
            le3 = R["le"].rearrange("p t (g e) -> p (t g) e", e=EPG)
            link(dve.tensor_tensor(le3, le3, R["pen"].rearrange("p t g -> p (t g)").unsqueeze(2).broadcast_to(
                [P, TILES * NG, EPG]), ALU.add))
            for t in range(TILES):
                ins = dve.max(R["v8"][:, t, :], R["le"][:, t, :])
            link(ins)
            dve.tensor_tensor(R["d2"], R["v8"][:, :, 1], R["v8"][:, :, 0], ALU.subtract).then_inc(exp2_in, 1)
            for t in range(TILES):
                ins = dve.max_index(R["i8"][:, t, :], R["v8"][:, t, :], R["le"][:, t, :])
            link(ins)
            for j in range(2):
                ins = dve.tensor_copy(R["idx"][:, j, :], R["i8"][:, :, j])
            link(ins)
            for j in range(2):
                ins = dve.tensor_tensor(R["hot1"][:, j, :, :],
                                        R["idx"][:, j, :].unsqueeze(2).broadcast_to([P, TILES, NE]),
                                        io_e.unsqueeze(1).broadcast_to([P, TILES, NE]), ALU.is_equal)
            link(ins)
            for j in range(2):
                ins = dve.tensor_tensor(R["hot1"][:, j, :, :], R["hot1"][:, j, :, :],
                                        token[:, :, 1:2].broadcast_to([P, TILES, NE]), ALU.mult)
            link(ins)
            dve.tensor_tensor(R["hot"], R["hot1"][:, 0, :, :], R["hot1"][:, 1, :, :], ALU.add).then_inc(hot_done, 1)
            dve.wait_ge(grp_exp, 1)
            link(dve.tensor_reduce(R["gsum"], R["e_grp"], AX.X, ALU.add))
            link(dve.reciprocal(R["gsum"], R["gsum"]))
            dve.wait_ge(exp2_out, 1)
            link(dve.tensor_scalar(R["d2"], R["e2"], 1.0, None, ALU.add))
            link(dve.reciprocal(R["d2"], R["d2"]))
            link(dve.tensor_tensor(R["w"][:, 0, :], R["d2"], R["gsum"], ALU.mult))
            dve.tensor_tensor(R["w"][:, 1, :], R["w"][:, 0, :], R["e2"], ALU.mult)
            dve.wait_ge(rank_done, 1)
            link(dve.tensor_scalar(R["cnt"], acc[:, 5, 0:NE], 0.0, None, ALU.is_gt))
            for m in range(1, -(-(SEQ + DEC) // P)):
                link(dve.scalar_tensor_tensor(R["cnt"], acc[:, 5, 0:NE], float(P * m), R["cnt"], ALU.is_gt, ALU.add))
            link(dve.tensor_tensor_scan(R["cum"], ones[:, 0:NE], R["cnt"], 0.0, ALU.mult, ALU.add))
            link(dve.tensor_tensor(R["startof"], R["cum"], R["cnt"], ALU.subtract))
            link(dve.tensor_scalar(R["startof"], R["startof"], float(P), None, ALU.mult))
            link(dve.tensor_tensor(R["slotbase"], acc[:, 0:TILES, 0:NE],
                                   R["startof"].unsqueeze(1).broadcast_to([P, TILES, NE]), ALU.add))
            for j in range(2):
                ins = dve.tensor_tensor(R["hot1"][:, j, :, :], R["hot1"][:, j, :, :], R["slotbase"], ALU.mult)
            link(ins)
            for j in range(2):
                ins = dve.tensor_reduce(R["slot"][:, j * TILES:j * TILES + TILES], R["hot1"][:, j, :, :], AX.X,
                                        ALU.add)
            link(ins)
            for j in range(2):
                ins = dve.tensor_tensor(R["slot"][:, j * TILES:j * TILES + TILES],
                                        R["slot"][:, j * TILES:j * TILES + TILES], token[:, :, 2], ALU.add)
            link(ins)
            n2 = 2 * TILES
            link(dve.tensor_tensor(R["ge"], io_blk.unsqueeze(1).broadcast_to([P, n2, NBLK + 1]),
                                   R["slot"].unsqueeze(2).broadcast_to([P, n2, NBLK + 1]), ALU.is_le))
            dve.tensor_tensor(R["oh_blk"], R["ge"][:, :, 0:NBLK], R["ge"][:, :, 1:NBLK + 1], ALU.subtract)
            link(dve.tensor_reduce(R["nge"], R["ge"], AX.X, ALU.add))
            link(dve.scalar_tensor_tensor(R["slot"], R["nge"], -float(P), R["slot"], ALU.mult, ALU.add))
            link(dve.tensor_scalar(R["slot"], R["slot"], float(P), None, ALU.add))
            dve.tensor_tensor(R["in_block"], R["slot"].unsqueeze(2).broadcast_to([P, n2, P]),
                              io128.unsqueeze(1).broadcast_to([P, n2, P]), ALU.is_equal)
            for j in range(2):
                ohb = R["oh_blk"][:, j * TILES:j * TILES + TILES, :]
                what = R["what"][:, j * TILES:j * TILES + TILES, :]
                tok = token[:, :, 0:1].broadcast_to([P, TILES, NBLK])
                link(dve.tensor_tensor(what[:, :, 0:NBLK], ohb, tok, ALU.mult))
                dve.scalar_tensor_tensor(what[:, :, NBLK:2 * NBLK], ohb, float(REAL * j), what[:, :, 0:NBLK],
                                         ALU.mult, ALU.add)
                ins = dve.tensor_tensor(what[:, :, 2 * NBLK:3 * NBLK], ohb,
                                        R["w"][:, j, :].unsqueeze(2).broadcast_to([P, TILES, NBLK]), ALU.mult)
            ins.then_inc(plan_in, 1)
            for half in range(2):
                nb = NBLK // 2
                cmp_ = R["tmp"].rearrange("p (b e) -> p b e", e=NE)
                link(dve.scalar_tensor_tensor(cmp_, R["cum"].unsqueeze(1).broadcast_to([P, nb, NE]), float(P),
                                              io_blk[:, half * nb:half * nb + nb].unsqueeze(2).broadcast_to(
                                                  [P, nb, NE]), ALU.mult, ALU.is_le))
                link(dve.tensor_reduce(R["ge"][:, 0, half * nb:half * nb + nb], cmp_, AX.X, ALU.add))
            link(dve.tensor_scalar(R["ge"][:, 0, 0:NBLK], R["ge"][:, 0, 0:NBLK], float(NE - 1), None, ALU.min))
            link(dve.tensor_copy(expert_of[:, 0:NBLK], R["ge"][0:1, 0, 0:NBLK]))
            dve.tensor_copy(n_blocks[:, 0:1], R["cum"][0:1, NE - 1:NE])
            dve.wait_ge(plan_done, 1)
            pl3 = acc[:, 0, 0:3 * NBLK].rearrange("p (a b) -> p a b", b=NBLK)
            dve.tensor_scalar(R["pl"][:, 0, :], pl3[:, 0, :], -1.0, 0.0, ALU.add, ALU.max)
            link(dve.tensor_scalar(R["pl"][:, 1, :], pl3[:, 1, :], 0.0, 4.0 * NASSIGN, ALU.is_equal, ALU.mult))
            link(dve.tensor_tensor(R["pl"][:, 1, :], pl3[:, 1, :], R["pl"][:, 1, :], ALU.add))
            link(dve.tensor_scalar(R["pl"][:, 1, :], R["pl"][:, 1, :], -1.0, None, ALU.add))
            dve.tensor_copy(gate_of[:, 0:NBLK], pl3[:, 2, :])
            dve.tensor_copy(src_row[:, 0:NBLK], R["pl"][:, 0, :])
            dve.tensor_copy(dst_row[:, 0:NBLK], R["pl"][:, 1, :])
            dve.memset(expert_of[:, NBLK:NBLK + 2], 0)
            link(dve.memset(src_row[:, NBLK:NBLK + 6], 0))
            dve.sem_inc(ya_e, 2)
            dve.sem_inc(yd_e, 2)
            dve.sem_inc(routed, 1)

            n = dve.value_load(n_blocks[0:1, 0:1], min_val=1, max_val=NBLK)

            def halve_weights(q):
                dve.tensor_tensor(elo[:, q % ERING, :], raw_e[:, q, :], ehi[:, q % ERING, :].bitcast(F32),
                                  ALU.subtract).then_inc(lo_e, 1)

            def halve_tokens(b, s, bank):
                dve.tensor_tensor(xlo[:, b, 4 * s:4 * s + 4, :], tp[:, bank, :].rearrange("p (k r) -> p k r", r=P),
                                  xhi[:, b, 4 * s:4 * s + 4, :].bitcast(F32), ALU.subtract).then_inc(tlo_e, 1)

            for q in range(2):
                dve.wait_ge(hi_e, q + 1)
                halve_weights(q)
            for g in range(4):
                dve.wait_ge(thi_e, g + 1)
                halve_tokens(g // 2, g % 2, g % 2)
            for q in range(2, ERING):
                dve.wait_ge(hi_e, q + 1)
                halve_weights(q)
            with dve.Fori(0, PAIRS) as i:
                with dve.If(i * 2 < n):
                    def split(q, next_=0):
                        dve.wait_ge(hi_e, i * EG + (EG * next_ + q + 1))
                        halve_weights(q)

                    def turned(b, s, group):
                        dve.wait_ge(thi_e, i * 6 + (group + 5))
                        halve_tokens(b, s, group % 2)

                    def product(b):
                        dve.wait_ge(silu_e, i * 2 + (b + 1))
                        dve.tensor_tensor(gg[:, b, :], acc[:, b, DE:2 * DE], gg[:, b, :], ALU.mult).then_inc(g_e, 1)

                    def turned_g(b, group):
                        dve.wait_ge(thi_e, i * 6 + (group + 5))
                        dve.tensor_tensor(glo[:, b, :, :], tp[:, group % 2, 0:DE].rearrange("p (k r) -> p k r", r=P),
                                          ghi[:, b, :, :].bitcast(F32), ALU.subtract).then_inc(tlo_e, 1)

                    def result(b):
                        dve.wait_ge(used_e, i * EG + (2 * b + 10))
                        dve.wait_ge(left_e, i * 2 + (b + 1))
                        dve.wait_ge(gate_e, i * 2 + 2)
                        dve.tensor_scalar(ye[:, b, 512:D], acc[:, 3 + 2 * b, :], gate_in[:, b, :], None,
                                          ALU.mult).then_inc(yd_e, 1)

                    for b in range(2):
                        dve.wait_ge(ya_e, i * 2 + (b + 1))
                        dve.wait_ge(yd_e, i * 2 + (b + 1))
                        dve.tensor_copy(gate_in[:, b, :], gate_of[:, ds(i * 2 + b, 1)]).then_inc(gate_e, 1)
                    steps_of_pair(split, turned, product, turned_g, result)

            for t in range(TILES):
                rows = ROWS[t]
                dve.wait_ge(ld_y[t % 2], 16 * (t // 2 + 1))
                link(dve.tensor_tensor(h[0:rows, t, :], h[0:rows, t, :], ysum[0:rows, t % 2, 0, :], ALU.add))
                dve.tensor_tensor(h[0:rows, t, :], h[0:rows, t, :], ysum[0:rows, t % 2, 1, :],
                                  ALU.add).then_inc(y_added, 1)
            for t in range(TILES):
                halve_lo("pe", 0, t, 2, phi, plo)
            dve.wait_ge(ld_g, 32)
            dve.wait_ge(f_rstd, 1)
            for t in range(TILES):
                if t >= 2:
                    dve.wait_ge(t_done, tg[("hp", t - 2, 1)] + 1)
                dve.scalar_tensor_tensor(hp[:, t % 2, :], h[:, t, :], r_f[:, t:t + 1], grow2, ALU.mult,
                                         ALU.mult).then_inc(fn_done, 1)
                if t >= 1:
                    for s in range(2):
                        halve_lo("hp", s, t - 1, 4, lhi2, llo2)
            for s in range(2):
                halve_lo("hp", s, TILES - 1, 4, lhi2, llo2)
            run(ple)

        def late_gpsimd(pool, link, inverse_rms):
            pool.memset(ones[:, :], 1.0).then_inc(ones_set, 1)
            pool.wait_ge(h_sq, TILES)
            inverse_rms(r_h, ss_h, TILES, D).then_inc(h_rstd, 1)
            for t in range(TILES):
                pool.wait_ge(hn_done, t + 1)
                pool.dma_start(hn_rows[t * P:t * P + ROWS[t], :], xn[0:ROWS[t], t % 2, :]).then_inc(hn_sent[t % 2], 16)
            for j in range(2):
                pool.wait_ge(hn_sent[j], 16 * ((TILES - j + 1) // 2))
            pool.sem_inc(left_e, 2)

            pool.wait_ge(routed, 1)
            n = pool.value_load(n_blocks[0:1, 0:1], min_val=1, max_val=NBLK)
            for b in range(2):
                pool.tensor_copy(row_in[:, b, :], src_row[:, b:b + 1]).then_inc(own_e, 1)
            pool.wait_ge(own_e, 2)

            def gather(b):
                pool.indirect_dma_start(xg[:, b, :], None, hn_rows,
                                        bass.IndirectOffsetOnAxis(ap=row_in[:, b, :], axis=0)).then_inc(ld_xg[b], 16)

            for b in range(2):
                gather(b)
            for b in range(2):
                pool.wait_ge(ld_xg[b], 16)
                pool.tensor_copy(row_in[:, b, :], src_row[:, b + 2:b + 3]).then_inc(own_e, 1)
            pool.wait_ge(own_e, 4)
            for b in range(2):
                pool.wait_ge(t_e, 2 * b + 2)
                gather(b)
            with pool.Fori(0, PAIRS) as i:
                with pool.If(i * 2 < n):
                    for b in range(2):
                        pool.wait_ge(t_e, i * 6 + (6, 9)[b])
                        pool.wait_ge(ld_xg[b], i * 16 + 32)
                        pool.sem_inc(pool_steps, 1)
                        pool.tensor_copy(row_in[:, b, :], src_row[:, ds(i * 2 + (4 + b), 1)]).then_inc(own_e, 1)
                        pool.wait_ge(own_e, i * 4 + (b + 5))
                        pool.sem_inc(pool_steps, 1)
                        gather(b)
                    for b in range(2):
                        pool.tensor_copy(row_out[:, b, :], dst_row[:, ds(i * 2 + b, 1)]).then_inc(own_e, 1)
                        pool.wait_ge(own_e, i * 4 + (b + 7))
                        pool.wait_ge(ya_e, i * 2 + (b + 3))
                        pool.wait_ge(yd_e, i * 2 + (b + 3))
                        pool.sem_inc(pool_steps, 1)
                        pool.indirect_dma_start(y_rows, bass.IndirectOffsetOnAxis(ap=row_out[:, b, :], axis=0),
                                                ye[:, b, :], None, bounds_check=NASSIGN - 1,
                                                oob_is_err=False).then_inc(sent_e[b], 16)
                    for b in range(2):
                        pool.wait_ge(sent_e[b], i * 16 + 16)
                        pool.sem_inc(left_e, 1)
            steps = (n + 1) // 2
            for b in range(2):
                pool.wait_ge(sent_e[b], steps * 16)
                pool.wait_ge(ld_xg[b], steps * 16 + 32)
            pool.sem_inc(moe_done, 1)
            pool.memset(ptok[DEC:P, PT, :], 0.0).then_inc(zeroed, 1)
            pool.wait_ge(zeroed, 3)
            pool.wait_ge(f_sq, TILES)
            inverse_rms(r_f, ss_f, TILES, D).then_inc(f_rstd, 1)
            for t in range(TILES):
                pool.wait_ge(y_done, y_index[(ple_first + 3, t)] + 1)
                dst = o["y_p"][t * P:t * P + P, :] if t < PT else o["y_s"]
                pool.dma_start(dst, h[0:ROWS[t], t, :]).then_inc(st_y, 16)
            pool.wait_ge(st_y, 16 * TILES)

        block = ctx.enter_context(nc.Block())
        last_first = len(first) - 1
        NCONST = 20
        gv = {"mla_qn": 0, "mla_qr": 1, "mla_kn": 2, "diff_q": 3, "diff_k": 4, "diff_sub": 5}

        def load_granule(sp, i, g):
            c, n = items[i], granules[(i, g)]
            if n >= RAW:
                sp.wait_ge(lo_done, n - RAW + 1)
            src = a[c.src].rearrange("(k p) n -> p k n", p=P)[:, 2 * g:2 * g + 2, c.col:c.col + c.width]
            sp.dma_start(raw[:, n % RAW, :, 0:c.width], src).then_inc(ld_raw[n % RAW], 16)

        @block.sync
        def _(sp):
            for t in range(TILES):
                sp.dma_start(gates[0:ROWS[t], t, 0:D], a["x"][t * P:t * P + ROWS[t], :]).then_inc(ld_x[t], 16)
            load_granule(sp, 0, 0)
            sp.dma_start(ident[:, :], a["c_ident"]).then_inc(ld_const, 16)
            sp.dma_start(grow[:, :], a["g_mix"].partition_broadcast(P)).then_inc(ld_const, 16)
            sp.dma_start(rope[:, :, :], a["c_rope"].rearrange("(t p) n -> p t n", p=P)).then_inc(ld_const, 16)
            sp.dma_start(mask[:, :], a["c_mask"]).then_inc(ld_const, 16)
            sp.dma_start(gq_lat[:, :], a["g_q_lat"].partition_broadcast(P)).then_inc(ld_const, 16)
            sp.dma_start(gkv[:, 0:KVL], a["g_kv_lat"].partition_broadcast(P)).then_inc(ld_const, 16)
            sp.dma_start(gkv[:, KVL:KVL + RD], a["g_mla_kr"].partition_broadcast(P)).then_inc(ld_const, 16)
            for name, j in gv.items():
                g = a["g_" + name]
                sp.dma_start(gvec[:, j, 0:g.shape[-1]], g.partition_broadcast(P)).then_inc(ld_const, 16)
            for j, name in enumerate(("lambda_q1", "lambda_k1", "lambda_q2", "lambda_k2")):
                sp.dma_start(zs[:, 5, 64 * j:64 * j + 64], a[name].partition_broadcast(P)).then_inc(ld_const, 16)
            sp.dma_start(gates[:, 0, D:2 * D], a["cache_k"]).then_inc(ld_const, 16)
            sp.dma_start(gates[:, 1, D:D + KVL], a["cache_ckv"]).then_inc(ld_const, 16)
            sp.dma_start(krope[:, CACHE, :], a["cache_krope"]).then_inc(ld_const, 16)
            every = [(i, g) for i in range(len(first)) for g in range(items[i].kt // 2)][1:]
            for n, (i, g) in enumerate(every):
                load_granule(sp, i, g)
                if n == 3:
                    sp.wait_ge(xn_done, TILES)
                    sp.dma_start(grow[:, :], a["g_ffn"].partition_broadcast(P)).then_inc(ld_g, 16)
            sp.wait_ge(z_done, units[(last_first, TILES - 1)] + 1)
            sp.dma_start(w_uq[:, :, :], a["w_uq"].rearrange("(k p) n -> p k n", p=P)).then_inc(ld_wu, 16)
            sp.dma_start(w_uk[:, :, :], a["w_uk"].rearrange("(k p) n -> p k n", p=P)).then_inc(ld_wu, 16)
            sp.dma_start(w_uv[:, :, :], a["w_uv"].rearrange("(k p) n -> p k n", p=P)).then_inc(ld_wu, 16)
            first_dv = next(i for i, c in enumerate(first) if c.name == "dv")
            for hd in range(H):
                cols = slice(hd * VB, hd * VB + VB)
                if hd >= 2:
                    sp.wait_ge(pv_done["b"], TILES * (hd - 1))
                if hd % (H // 2) == 0:
                    for t in range(TILES):
                        sp.wait_ge(outz[t], 16 * out_count(last_first if hd else first_dv, t))
                s = ld_v[hd % 2]
                sp.dma_start(vh[:, hd % 2, 0:PT, :],
                             o["dv_p"].rearrange("(t p) n -> p t n", p=P)[:, :, cols]).then_inc(s, 16)
                sp.dma_start(vh[0:DEC, hd % 2, PT, :], o["dv_s"][:, cols]).then_inc(s, 16)
                sp.dma_start(vh[:, hd % 2, CACHE, :], a["cache_v"][:, cols]).then_inc(s, 16)
            last_latent = start[id(outp)] - 1
            for t in range(TILES + 1):
                sp.wait_ge(outz[t], 16 * out_count(last_latent, t))
            o_first = start[id(outp)]
            rest = [(i, g) for i in range(o_first, o_first + 2) for g in range(4)]
            for hd in range(H):
                cols = slice(hd * VB, hd * VB + VB)
                if hd >= 2:
                    sp.wait_ge(pv_done["a"], TILES * (hd - 1))
                else:
                    sp.wait_ge(pv_done["b"], TILES * H)
                sp.dma_start(vh[:, hd % 2, :, :],
                             va_rows.rearrange("(t p) n -> p t n", p=P)[:, :, cols]).then_inc(ld_v[hd % 2], 16)
                if hd == 1:
                    for i, g in rest[:RAW]:
                        load_granule(sp, i, g)
            sp.wait_ge(t_copied, copied[("merged", TILES - 1, 1)] + 1)
            for t in range(TILES):
                sp.dma_start(h[0:ROWS[t], t, :], a["x"][t * P:t * P + ROWS[t], :]).then_inc(ld_h, 16)
            for i, g in rest[RAW:]:
                load_granule(sp, i, g)
            late_sync(sp)

        def key_tiles(t):
            if t < PT:
                return [(j, P, j * P) for j in range(t + 1)]
            return [(CACHE, PAST, SEQ), (PT, DEC, SEQ + PAST)]

        @block.tensor
        def _(pe):
            pe.wait_ge(ld_const, 16 * NCONST)

            def turn(key, blocks, rows=P, cols=P, pitch=P):
                wait_bank_for(pe, key)
                bank = tg[key] % 2
                for j, src in enumerate(blocks):
                    last = pe.transpose(tp[0:cols, bank, j * P:j * P + rows], src, ident[0:rows, 0:rows])
                last.then_inc(t_done, 1)

            def multiply(i, between):
                c = items[i]
                lo_name = {"act": {0: "x", 2: "merged", 3: "hp"}.get(
                    next(n for n, ph in enumerate(phases) if c in ph)), "pe": "pe"}.get(c.lhs)
                steps = c.kt // 2 if c.split else 1
                for g in range(steps):
                    if c.split:
                        pe.wait_ge(lo_done, granules[(i, g)] + 1)
                    for t in range(c.tiles):
                        bank = acc[:, t, 0:c.width]
                        rows = slice(t * P, t * P + P)
                        if g == 0:
                            if lo_name:
                                wait_group_copied(pe, (lo_name, t, 0 if lo_name == "pe" else 1))
                            before = [n for n in range(i) if items[n].tiles > t]
                            if before:
                                pe.wait_ge(z_copied, units[(before[-1], t)] + 1)
                        if c.split:
                            for k in range(2):
                                n = granules[(i, g)] % RING
                                kk = 2 * g + k
                                L, W = {"x": (lhi, llo), "pe": (phi, plo)}.get(lo_name, (lhi2, llo2)), (whi, wlo)
                                for x, w in ((0, 0), (0, 1), (1, 0)):
                                    mm = pe.matmul(bank, L[x][:, kk, rows], W[w][:, n, k, 0:c.width],
                                                   start=(kk == 0 and x + w == 0),
                                                   stop=(kk == c.kt - 1 and x == 1))
                        else:
                            L = {"q_lat": q_latT, "ckv": ckvT}[c.lhs]
                            W = {"w_uq": w_uq, "w_uk": w_uk, "w_uv": w_uv}[c.src]
                            for k in range(c.kt):
                                mm = pe.matmul(bank, L[:, k, rows], W[:, k, c.col:c.col + c.width],
                                               start=(k == 0), stop=(k == c.kt - 1))
                        if g == steps - 1:
                            mm.then_inc(z_done, 1)
                    if c.split and g < steps - 1:
                        mm.then_inc(w_used, 1)
                    between(g)

            def transposes(i, tiles=range(TILES + 1)):
                c = items[i]
                if c.kind != "norm":
                    return
                for t in tiles:
                    if t >= c.tiles:
                        continue
                    pe.wait_ge(y_done, y_index[(i, t)] + 1)
                    z = zs[:, t, :]
                    if c.name == "uq":
                        turn((i, t, 0), [z[:, j * HD:j * HD + HD] for j in range(4)], cols=HD)
                    elif c.name == "uk":
                        for s in range(2):
                            turn((i, t, s), [kas(t)[:, j * HD:j * HD + HD] for j in range(4 * s, 4 * s + 4)], cols=HD)
                    else:
                        n = {"q_lat": 3, "ckv": 2}.get(c.name, 4)
                        turn((i, t, 0), [z[:, j * P:j * P + P] for j in range(n)])

            def run(ph):
                ids = phase_items(ph)
                for i in ids:
                    def between(g):
                        if i - 2 in ids and deferred(i - 2):
                            if items[i].split:
                                transposes(i - 2, DEFERRED[g])
                            else:
                                transposes(i - 2)

                    multiply(i, between)
                    if i - 1 in ids and not deferred(i - 1):
                        transposes(i - 1)
                transposes(ids[-1])

            def attention(ph, maps, dim):
                name = "attn_" + ph

                def scores(n):
                    hd, t = divmod(n, TILES)
                    kt_ = key_tiles(t)
                    k0, nk = kt_[0][2], sum(r for _, r, _ in kt_)
                    if n >= 2:
                        pe.wait_ge(exp_done[ph], maps * (n - 1))
                    if ph == "b":
                        pe.wait_ge(qz_done, n + 1)
                    for c in range(maps):
                        bank = 2 * (n % 2) + c
                        lhs = qz[:, n % QZ, c, 0:ROWS[t]] if ph == "b" else qT[0:dim, hd, t * P:t * P + ROWS[t]]
                        mm = pe.matmul(acc[0:ROWS[t], bank, 0:nk], lhs, kT[0:lhs.shape[0], hd, k0:k0 + nk],
                                       start=True, stop=(t == PT))
                        if t < PT:
                            mm = pe.matmul(acc[:, bank, nk - CHUNK:nk], mask[:, 0:P], mask[:, P:P + CHUNK],
                                           start=False, stop=True)
                    mm.then_inc(s_done[ph], 1)

                def turn_probs(n):
                    hd, t = divmod(n, TILES)
                    if ph == "b":
                        pe.wait_ge(comb_done[ph], n + 1)
                    else:
                        pe.wait_ge(exp_done[ph], n + 1)
                    wait_bank_for(pe, (name, n, 0))
                    bank = tg[(name, n, 0)] % 2
                    at = 0
                    for j, (_, nk, _) in enumerate(key_tiles(t)):
                        last = pe.transpose(tp[0:nk, bank, j * P:j * P + ROWS[t]],
                                            pr[0:ROWS[t], n % 3, 0, at:at + nk], ident[0:ROWS[t], 0:ROWS[t]])
                        at += nk
                    last.then_inc(t_done, 1)

                def values(n):
                    hd, t = divmod(n, TILES)
                    pe.wait_ge(pt_copied, pt[(name, n, 0)] + 1)
                    if t == 0:
                        pe.wait_ge(ld_v[hd % 2], 48 * (hd // 2 + 1) if ph == "b" else 48 * 4 + 16 * (hd // 2 + 1))
                    if n >= 2:
                        pe.wait_ge(o_done[ph], n - 1)
                        if ph == "b":
                            pe.wait_ge(sqo_done, n - 1)
                    kt_ = key_tiles(t)
                    for j, (slot, nk, _) in enumerate(kt_):
                        mm = pe.matmul(acc[0:ROWS[t], 4 + n % 2, 0:VB], prT[0:nk, n % 2, j, 0:ROWS[t]],
                                       vh[0:nk, hd % 2, slot, :], start=(j == 0), stop=(j == len(kt_) - 1))
                    mm.then_inc(pv_done[ph], 1)

                n_units = H * TILES
                for n in range(n_units + 3):
                    if n < n_units:
                        scores(n)
                    if 2 <= n < n_units + 2:
                        turn_probs(n - 2)
                    if n >= 3:
                        values(n - 3)

            for t in range(TILES):
                pe.wait_ge(xn_done, t + 1)
                for s in range(2):
                    turn(("x", t, s), [gates[:, t, j * P:j * P + P] for j in range(4 * s, 4 * s + 4)])
            for s in range(2):
                turn(("cache_k", 0, s), [gates[:, 0, D + j * P:D + j * P + P] for j in range(4 * s, 4 * s + 4)])
            turn(("cache_ckv", 0, 0), [gates[:, 1, D + j * P:D + j * P + P] for j in range(2)])
            run(first)
            pe.wait_ge(z_copied, units[(last_first, TILES - 1)] + 1)
            pe.wait_ge(t_copied, copied[(last_norm(first), TILES - 1, 0)] + 1)
            attention("b", 2, DB)
            pe.wait_ge(exp_done["b"], 2 * H * TILES)
            pe.wait_ge(o_done["b"], H * TILES)
            pe.wait_ge(sqo_done, H * TILES)
            pe.wait_ge(ld_wu, 48)
            run(latent)
            pe.wait_ge(z_copied, units[(start[id(outp)] - 1, TILES - 1)] + 1)
            pe.wait_ge(t_copied, copied[(last_norm(latent), TILES - 1, 0)] + 1)
            attention("a", 1, HD)
            pe.wait_ge(exp_done["a"], H * TILES)
            pe.wait_ge(o_done["a"], H * TILES)
            for t in range(TILES):
                pe.wait_ge(merged_done, t + 1)
                for s in range(2):
                    turn(("merged", t, s), [gates[:, t, j * P:j * P + P] for j in range(4 * s, 4 * s + 4)])
            run(outp)
            late_tensor(pe, turn, run)

        @block.scalar
        def _(act):
            own = [0]

            def link(ins):
                own[0] += 1
                ins.then_inc(act_own, 1)
                act.wait_ge(act_own, own[0])

            def split_hi(i, g):
                c, n = items[i], granules[(i, g)]
                act.wait_ge(ld_raw[n % RAW], 16 * (n // RAW + 1))
                wait_ring_free(act, n)
                act.activation(whi[:, n % RING, :, 0:c.width], raw[:, n % RAW, :, 0:c.width],
                               ACT.Copy).then_inc(hi_done, 1)

            def copy_out(i):
                c = items[i]
                for t in range(c.tiles):
                    act.wait_ge(z_done, units[(i, t)] + 1)
                    src = acc[:, t, 0:c.width]
                    if uses_zs(i):
                        wait_slot_free(act, i, t)
                        func = ACT.Sigmoid if c.kind == "ple" else ACT.Copy
                        act.activation(zs[:, t, 0:c.width], src, func).then_inc(z_copied, 1)
                    elif c.name == "uv":
                        act.wait_ge(outz[t], 16 * out_count(i - 1, t))
                        act.activation(uv_tile(t), src, ACT.Copy).then_inc(z_copied, 1)
                    elif c.kind == "gate":
                        at = (0 if c.name == "ga" else D) + 512 * c.half
                        act.activation(gates[:, t, at:at + 512], src, ACT.Sigmoid).then_inc(z_copied, 1)
                    else:
                        act.activation(pj[:, t, 512 * c.half:512 * c.half + 512], src,
                                       ACT.Copy).then_inc(z_copied, 1)

            def squares(i):
                c = items[i]
                if c.kind != "norm":
                    return
                for t in range(c.tiles):
                    act.wait_ge(z_copied, units[(i, t)] + 1)
                    if y_norm[(i, t)] >= 1:
                        act.wait_ge(ss_done, y_norm[(i, t)])
                    act.activation(sq[:, 0:c.width], zs[:, t, 0:c.width], ACT.Square).then_inc(sq_done, 1)

            def run(ph):
                ids = list(phase_items(ph))
                for i in ids + [ids[-1] + 1]:
                    steps = items[i].kt // 2 if i in ids and items[i].split else 0
                    if steps > 0:
                        split_hi(i, 0)
                    if i - 1 in ids:
                        copy_out(i - 1)
                    if steps > 1:
                        split_hi(i, 1)
                    if i - 1 in ids:
                        squares(i - 1)
                    for g in range(2, steps):
                        split_hi(i, g)

            def halve_hi(name, s, t, n, hi):
                act.wait_ge(t_done, tg[(name, t, s)] + 1)
                act.activation(hi[:, 4 * s:4 * s + n, t * P:t * P + P],
                               tp[:, tg[(name, t, s)] % 2, 0:n * P].rearrange("p (k r) -> p k r", r=P),
                               ACT.Copy).then_inc(hi_copied, 1)

            for t in range(TILES):
                act.wait_ge(ld_x[t], 16)
                if t == 0:
                    act.wait_ge(zeroed, 1)
                if t:
                    act.wait_ge(x_sq, t)
                act.activation(zs[:, 0:2, :].rearrange("p a b -> p (a b)"), gates[:, t, 0:D], ACT.Square,
                               accum_out=ss_x[:, t:t + 1]).then_inc(x_sq, 1)
            act.wait_ge(x_sq, TILES)
            act.wait_ge(lam_dots, 2)
            act.activation(lamv[:, 2:4], lamv[:, 0:2], ACT.Exp).then_inc(lam_exp, 1)
            for t in range(TILES):
                for s in range(2):
                    halve_hi("x", s, t, 4, lhi)
            run(first)

            def attention(ph, maps):
                name = "attn_" + ph
                n_units = H * TILES

                def exps(n):
                    hd, t = divmod(n, TILES)
                    rows, nk = ROWS[t], sum(r for _, r, _ in key_tiles(t))
                    act.wait_ge(nm_done[ph], n + 1)
                    if n >= 3:
                        act.wait_ge(t_done, tg[(name, n - 3, 0)] + 1)
                    for c in range(maps):
                        act.activation(pr[0:rows, n % 3, c, 0:nk], acc[0:rows, 2 * (n % 2) + c, 0:nk], ACT.Exp,
                                       bias=negmax[0:rows, 2 * (n % 2) + c:2 * (n % 2) + c + 1],
                                       accum_out=sums[0:rows, 2 * (n % 2) + c:2 * (n % 2) + c + 1]
                                       ).then_inc(exp_done[ph], 1)

                def copy_turned(n):
                    hd, t = divmod(n, TILES)
                    rows, bank = ROWS[t], tg[(name, n, 0)] % 2
                    act.wait_ge(t_done, tg[(name, n, 0)] + 1)
                    if n >= 2:
                        act.wait_ge(pv_done[ph], n - 1)
                    if t < PT:
                        act.activation(prT[:, n % 2, 0:t + 1, :],
                                       tp[:, bank, 0:(t + 1) * P].rearrange("p (k r) -> p k r", r=P),
                                       ACT.Copy).then_inc(pt_copied, 1)
                    else:
                        act.activation(prT[:, n % 2, 0, 0:rows], tp[:, bank, 0:rows], ACT.Copy)
                        act.activation(prT[0:DEC, n % 2, 1, 0:rows], tp[0:DEC, bank, P:P + rows],
                                       ACT.Copy).then_inc(pt_copied, 1)

                def square_out(n):
                    hd, t = divmod(n, TILES)
                    rows = ROWS[t]
                    act.wait_ge(pv_done[ph], n + 1)
                    if n:
                        act.wait_ge(sqo_done, n)
                    act.activation(sq[0:rows, 0:VB], acc[0:rows, 4 + n % 2, 0:VB], ACT.Square,
                                   accum_out=ss_o[0:rows, t * H + hd:t * H + hd + 1]).then_inc(sqo_done, 1)

                for n in range(n_units + 3):
                    if n < n_units:
                        exps(n)
                    if 2 <= n < n_units + 2:
                        copy_turned(n - 2)
                    if n >= 3 and ph == "b":
                        square_out(n - 3)

            act.wait_ge(ss_done, y_norm_of_phase(first))
            attention("b", 2)
            act.wait_ge(sqo_done, H * TILES)
            act.wait_ge(t_done, tg[("attn_b", H * TILES - 1, 0)] + 1)
            run(latent)
            act.wait_ge(t_done, tg[(start[id(latent)], TILES, 1)] + 1)
            attention("a", 1)
            for t in range(TILES):
                for s in range(2):
                    halve_hi("merged", s, t, 4, lhi2)
            run(outp)
            late_scalar(act, link, halve_hi, run)

        @block.vector
        def _(dve):
            own = [0]

            def link(ins):
                own[0] += 1
                ins.then_inc(dve_own, 1)
                dve.wait_ge(dve_own, own[0])

            def split_lo(i, g):
                c, n = items[i], granules[(i, g)]
                dve.wait_ge(hi_done, n + 1)
                dve.tensor_tensor(wlo[:, n % RING, :, 0:c.width], raw[:, n % RAW, :, 0:c.width],
                                  whi[:, n % RING, :, 0:c.width].bitcast(F32), ALU.subtract).then_inc(lo_done, 1)

            def halve_lo(name, s, t, n, hi, lo):
                dve.wait_ge(hi_copied, hi_index[(name, t, s)] + 1)
                cols = (slice(4 * s, 4 * s + n), slice(t * P, t * P + P))
                dve.tensor_tensor(lo[:, cols[0], cols[1]],
                                  tp[:, tg[(name, t, s)] % 2, 0:n * P].rearrange("p (k r) -> p k r", r=P),
                                  hi[:, cols[0], cols[1]].bitcast(F32), ALU.subtract).then_inc(t_copied, 1)

            def copy_group(key, dst, rows, n, width):
                dve.wait_ge(t_done, tg[key] + 1)
                src = tp[0:rows, tg[key] % 2, 0:n * P].rearrange("p (k r) -> p k r", r=P)[:, :, 0:width]
                dve.tensor_copy(dst, src).then_inc(t_copied, 1)

            def copy_turned(i, tiles=range(TILES + 1)):
                c = items[i]
                if c.kind != "norm":
                    return
                for t in tiles:
                    if t >= c.tiles:
                        continue
                    q = slice(t * P, t * P + ROWS[t]) if t < TILES else None
                    k = slice(KCOL[t], KCOL[t] + (ROWS[t] if t < TILES else P))
                    hs = slice(4 * c.half, 4 * c.half + 4)
                    if c.name == "q_lat":
                        copy_group((i, t, 0), q_latT[:, :, t * P:t * P + P], P, 3, P)
                    elif c.name == "ckv":
                        copy_group((i, t, 0), ckvT[:, :, t * P:t * P + P], P, 2, P)
                    elif c.name == "dq":
                        copy_group((i, t, 0), qT[:, hs, q], P, 4, ROWS[t])
                    elif c.name == "dk":
                        copy_group((i, t, 0), kT[:, hs, k], P, 4, ROWS[t])
                    elif c.name == "uq":
                        copy_group((i, t, 0), qT[0:HD, hs, q], HD, 4, ROWS[t])
                    else:
                        for s in range(2):
                            copy_group((i, t, s), kT[0:HD, 4 * s:4 * s + 4, k], HD, 4, ROWS[t] if t < TILES else P)

            def sums_of(i):
                c = items[i]
                if c.kind != "norm":
                    return
                gs = groups(i)
                total = sum(g[1] for g in gs)
                m = normitems[i]
                if m >= 2:
                    old = list(normitems)[m - 2]
                    dve.wait_ge(rstd_done, y_norm[(old, items[old].tiles - 1)] + 1)
                for t in range(c.tiles):
                    dve.wait_ge(sq_done, y_norm[(i, t)] + 1)
                    at = t * total
                    for n, g in enumerate(gs):
                        ins = dve.tensor_reduce(ss_z[m % 2][:, at:at + g[1]], grouped(sq[:, :], g), AX.X, ALU.add)
                        at += g[1]
                    ins.then_inc(ss_done, 1)

            def rotate(t, z, n, half):
                table = 0 if half == RD // 2 else 2 * RD
                cc = rope[:, t, table:table + 2 * half].unsqueeze(1).broadcast_to([P, n, 2 * half])
                ss = rope[:, t, table + 2 * half:table + 4 * half].unsqueeze(1).broadcast_to([P, n, 2 * half])
                r = [rot[:, j, 0:n * 2 * half].rearrange("p (n s) -> p n s", n=n) for j in range(2)]
                dve.tensor_tensor(r[0], z, cc, ALU.mult)
                dve.tensor_tensor(r[1][:, :, 0:half], z[:, :, half:2 * half], ss[:, :, 0:half], ALU.mult)
                link(dve.tensor_tensor(r[1][:, :, half:2 * half], z[:, :, 0:half], ss[:, :, half:2 * half], ALU.mult))
                return dve.tensor_tensor(z, r[0], r[1], ALU.add)

            def normalise(i, tiles):
                c = items[i]
                if c.kind != "norm":
                    return
                gs = groups(i)
                total = sum(g[1] for g in gs)
                m = normitems[i]
                for t in tiles:
                    dve.wait_ge(rstd_done, y_norm[(i, t)] + 1)
                    z = zs[:, t, :]
                    r = r_z[m % 2][:, t * total:t * total + total]
                    if c.name in ("q_lat", "ckv"):
                        gain = {"q_lat": gq_lat, "ckv": gkv}[c.name]
                        for n, (off, _, size, _, _) in enumerate(gs):
                            ins = dve.scalar_tensor_tensor(z[:, off:off + size], z[:, off:off + size], r[:, n:n + 1],
                                                           gain[:, off:off + size], ALU.mult, ALU.mult)
                        if c.name == "ckv":
                            link(ins)
                            link(rotate(t, z[:, KVL:KVL + RD].unsqueeze(1), 1, RD // 2))
                            ins = dve.tensor_copy(krope[:, t, :], z[:, KVL:KVL + RD])
                        ins.then_inc(y_done, 1)
                        continue
                    names = {"dq": ["diff_q"], "dk": ["diff_k"], "uq": ["mla_qn", "mla_qr"], "uk": ["mla_kn"]}[c.name]
                    at = 0
                    for g, nm in zip(gs, names):
                        ins = dve.tensor_tensor(grouped(z, g), grouped(z, g),
                                                r[:, at:at + g[1]].unsqueeze(2).broadcast_to([P, g[1], g[2]]), ALU.mult)
                        at += g[1]
                    link(ins)
                    if c.name == "uk":
                        keys = kas(t).rearrange("p (h s) -> p h s", s=HD)
                    for g, nm in zip(gs, names):
                        dst = grouped(z, g) if c.name != "uk" else keys[:, :, 0:NOPE]
                        ins = dve.tensor_tensor(dst, grouped(z, g),
                                                gvec[:, gv[nm], 0:g[2]].unsqueeze(1).broadcast_to([P, g[1], g[2]]),
                                                ALU.mult)
                    if c.name == "uk":
                        ins = dve.tensor_copy(keys[:, :, NOPE:HD],
                                              krope[:, t, :].unsqueeze(1).broadcast_to([P, H, RD]))
                    elif c.name == "uq":
                        link(ins)
                        ins = rotate(t, grouped(z, gs[1]), 4, RD // 2)
                    else:
                        link(ins)
                        ins = rotate(t, z.rearrange("p (n s) -> p n s", s=DB)[:, :, 0:ROT], 8, ROT // 2)
                    ins.then_inc(y_done, 1)

            def finish(i, tiles):
                c = items[i]
                normalise(i, tiles)
                if c.kind == "residual":
                    for t in tiles:
                        if (i, t) == (start[id(outp)], 0):
                            dve.wait_ge(ld_h, 16 * TILES)
                            dve.wait_ge(zeroed, 2)
                        dve.wait_ge(z_copied, units[(i, t)] + 1)
                        hh = h[:, t, 512 * c.half:512 * c.half + 512]
                        dve.tensor_tensor(hh, hh, zs[:, t, :], ALU.add).then_inc(y_done, 1)
                if c.kind == "ple":
                    for t in tiles:
                        cols = slice(512 * c.half, 512 * c.half + 512)
                        dve.wait_ge(z_copied, units[(i, t)] + 1)
                        link(dve.tensor_tensor(pj[:, t, cols], pj[:, t, cols], zs[:, t, :], ALU.mult))
                        dve.tensor_tensor(h[:, t, cols], h[:, t, cols], pj[:, t, cols], ALU.add).then_inc(y_done, 1)

            def run(ph):
                ids = list(phase_items(ph))
                for i in ids + [ids[-1] + 1, ids[-1] + 2]:
                    steps = items[i].kt // 2 if i in ids and items[i].split else 0
                    spread = steps == 4 and i - 2 in ids and deferred(i - 2)
                    n = items[i - 1].tiles if i - 1 in ids else 0
                    if steps > 0:
                        split_lo(i, 0)
                    if i - 2 in ids and not spread:
                        copy_turned(i - 2)
                    if steps > 1:
                        split_lo(i, 1)
                    if spread:
                        copy_turned(i - 2, DEFERRED[0])
                    if i - 1 in ids:
                        sums_of(i - 1)
                    if steps > 2:
                        split_lo(i, 2)
                    if spread:
                        copy_turned(i - 2, DEFERRED[1])
                    if n:
                        finish(i - 1, range(0, n // 2 + 1))
                    if steps > 3:
                        split_lo(i, 3)
                    if spread:
                        copy_turned(i - 2, DEFERRED[2])
                    if n:
                        finish(i - 1, range(n // 2 + 1, n))

            dve.wait_ge(zeroed, 1)
            dve.wait_ge(ld_const, 16 * NCONST)
            lq = zs[:, 5, :]
            for j in range(2):
                dve.tensor_tensor_reduce(rot[:, j, 0:64], lq[:, 128 * j:128 * j + 64], lq[:, 128 * j + 64:128 * j + 128],
                                         1.0, 0.0, ALU.mult, ALU.add, lamv[:, j:j + 1]).then_inc(lam_dots, 1)
            dve.wait_ge(x_rstd, 1)
            for t in range(TILES):
                dve.scalar_tensor_tensor(gates[:, t, 0:D], gates[:, t, 0:D], r_x[:, t:t + 1], grow[:, :],
                                         ALU.mult, ALU.mult).then_inc(xn_done, 1)
            for t in range(TILES):
                for s in range(2):
                    halve_lo("x", s, t, 4, lhi, llo)
            for s in range(2):
                copy_group(("cache_k", 0, s), kT[:, 4 * s:4 * s + 4, SEQ:SEQ + PAST], P, 4, P)
            copy_group(("cache_ckv", 0, 0), ckvT[:, :, TOK:TOK + P], P, 2, P)
            dve.wait_ge(lam_exp, 1)
            link(dve.tensor_tensor(lamv[:, 4:5], lamv[:, 3:4], lamv[:, 2:3], ALU.subtract))
            dve.tensor_scalar(pair[:, 1:2], lamv[:, 4:5], -LAM_INIT, None, ALU.add)
            dve.tensor_scalar(pair[:, 0:1], lamv[:, 4:5], 0.0, 1.0, ALU.mult, ALU.add)
            link(dve.tensor_scalar(gvec[:, gv["diff_sub"], :], gvec[:, gv["diff_sub"], :], 1.0 - LAM_INIT, None,
                                   ALU.mult))
            run(first)

            def attention(ph, maps):
                n_units = H * TILES

                def maxima(n):
                    hd, t = divmod(n, TILES)
                    rows, nk, b = ROWS[t], sum(r for _, r, _ in key_tiles(t)), 2 * (n % 2)
                    dve.wait_ge(s_done[ph], n + 1)
                    if n >= 2:
                        dve.wait_ge(exp_done[ph], maps * (n - 1))
                    dve.tensor_reduce(negmax[0:rows, b:b + maps], acc[0:rows, b:b + maps, 0:nk], AX.X, ALU.max,
                                      negate=True).then_inc(nm_done[ph], 1)

                def combine(n):
                    hd, t = divmod(n, TILES)
                    rows, nk, b, q = ROWS[t], sum(r for _, r, _ in key_tiles(t)), 2 * (n % 2), 2 * (n % 4)
                    dve.wait_ge(exp_done[ph], maps * (n + 1))
                    rr = rsum[0:rows, q:q + maps]
                    ins = dve.reciprocal(rr, sums[0:rows, b:b + maps])
                    if ph == "a":
                        ins.then_inc(comb_done[ph], 1)
                        return
                    link(ins)
                    link(dve.tensor_tensor(rr, rr, pair[0:rows, :], ALU.mult))
                    p0, p1 = pr[0:rows, n % 3, 0, 0:nk], pr[0:rows, n % 3, 1, 0:nk]
                    link(dve.tensor_scalar(p1, p1, rsum[0:rows, q + 1:q + 2], None, ALU.mult))
                    dve.scalar_tensor_tensor(p0, p0, rsum[0:rows, q:q + 1], p1, ALU.mult,
                                             ALU.add).then_inc(comb_done[ph], 1)

                def gate_out(n):
                    hd, t = divmod(n, TILES)
                    rows = ROWS[t]
                    dve.wait_ge(pv_done[ph], n + 1)
                    out = acc[0:rows, 4 + n % 2, 0:VB]
                    if ph == "b":
                        dve.wait_ge(sqo_done, n + 1)
                        g = gates[0:rows, t, D + hd * VB:D + hd * VB + VB]
                        dve.tensor_tensor(g, out, g, ALU.mult).then_inc(o_done[ph], 1)
                    else:
                        g = gates[0:rows, t, hd * VB:hd * VB + VB]
                        dve.wait_ge(comb_done[ph], n + 1)
                        dve.scalar_tensor_tensor(g, out, rsum[0:rows, 2 * (n % 4):2 * (n % 4) + 1], g, ALU.mult,
                                                 ALU.mult).then_inc(o_done[ph], 1)

                for n in range(n_units + 3):
                    if n < n_units:
                        maxima(n)
                    if 1 <= n <= n_units:
                        combine(n - 1)
                    if n >= 3:
                        gate_out(n - 3)

            attention("b", 2)
            run(latent)
            attention("a", 1)
            dve.wait_ge(o_done["a"], H * TILES)
            for t in range(TILES):
                dve.wait_ge(sub_done, t + 1)
                dve.tensor_tensor(gates[:, t, 0:D], gates[:, t, 0:D], gates[:, t, D:2 * D],
                                  ALU.add).then_inc(merged_done, 1)
            for t in range(TILES):
                for s in range(2):
                    halve_lo("merged", s, t, 4, lhi2, llo2)
            run(outp)
            late_vector(dve, link, halve_lo, run)

        @block.gpsimd
        def _(pool):
            own = [0]

            def link(ins):
                own[0] += 1
                ins.then_inc(pool_own, 1)
                pool.wait_ge(pool_own, own[0])

            def inverse_rms(dst, src, n, size, eps_scale=1.0):
                f = eps_scale
                link(pool.tensor_scalar(src, src, 1.0 / (size * f), EPS / f, ALU.mult, ALU.add))
                return pool.tensor_tensor(dst, src, neghalf[:, 0:n], ALU.pow)

            link(pool.memset(small[:, :], 0.0))
            link(pool.memset(neghalf[:, :], -0.5))
            link(pool.memset(qz[:, :, :, :], 0.0))
            pool.memset(gates[DEC:P, PT, 0:D], 0.0).then_inc(zeroed, 1)
            pool.wait_ge(zeroed, 1)

            pool.wait_ge(x_sq, TILES)
            inverse_rms(r_x, ss_x, TILES, D).then_inc(x_rstd, 1)

            def factors(i):
                c, gs, m = items[i], groups(i), normitems[i]
                total = sum(g[1] for g in gs)
                if m >= 2:
                    before = list(normitems)[m - 2]
                    pool.wait_ge(y_done, y_index[(before, items[before].tiles - 1)] + 1)
                for t in range(c.tiles):
                    pool.wait_ge(ss_done, y_norm[(i, t)] + 1)
                    at = t * total
                    for off, k, size, _, f in gs:
                        part_ = ss_z[m % 2][:, at:at + k]
                        link(pool.tensor_scalar(part_, part_, 1.0 / (size * f), EPS / f, ALU.mult, ALU.add))
                        at += k
                    n = slice(t * total, t * total + total)
                    pool.tensor_tensor(r_z[m % 2][:, n], ss_z[m % 2][:, n], neghalf[:, 0:total],
                                       ALU.pow).then_inc(rstd_done, 1)
                    pool.wait_ge(rstd_done, y_norm[(i, t)] + 1)

            def send(i):
                c = items[i]
                if not dmas_of(i):
                    return
                for t in range(c.tiles):
                    if c.kind == "norm":
                        pool.wait_ge(y_done, y_index[(i, t)] + 1)
                    else:
                        pool.wait_ge(z_copied, units[(i, t)] + 1)
                    cols = slice(512 * c.half, 512 * c.half + 512)
                    if c.name == "uv":
                        pool.dma_start(va_rows[t * P:t * P + P, cols], uv_tile(t)).then_inc(outz[t], 16)
                        continue
                    rows = slice(t * P, t * P + P) if t < PT else slice(0, DEC)
                    who = "_p" if t < PT else "_s"
                    if c.name == "ckv":
                        pool.dma_start(o["ckv" + who][rows, :], zs[0:ROWS[t], t, 0:KVL]).then_inc(outz[t], 16)
                        pool.dma_start(o["kr" + who][rows, :], zs[0:ROWS[t], t, KVL:KVL + RD]).then_inc(outz[t], 16)
                    else:
                        pool.dma_start(o[c.name + who][rows, cols], zs[0:ROWS[t], t, :]).then_inc(outz[t], 16)

            for i in phase_items(first):
                if items[i].kind == "norm":
                    factors(i)
                send(i)
            pool.wait_ge(t_copied, copied[(last_norm(first), TILES - 1, 0)] + 1)
            for n in range(H * TILES):
                hd, t = divmod(n, TILES)
                if n >= QZ:
                    pool.wait_ge(s_done["b"], n - QZ + 1)
                q = slice(t * P, t * P + ROWS[t])
                link(pool.tensor_copy(qz[0:DB, n % QZ, 0, 0:ROWS[t]], qT[0:DB, hd, q]))
                pool.tensor_copy(qz[DB:P, n % QZ, 1, 0:ROWS[t]], qT[DB:P, hd, q]).then_inc(qz_done, 1)
                pool.wait_ge(qz_done, n + 1)
            pool.wait_ge(sqo_done, H * TILES)
            inverse_rms(r_o, ss_o, H * TILES, VB).then_inc(ro_done, 1)
            pool.wait_ge(ro_done, 1)
            for i in phase_items(latent):
                if items[i].kind == "norm":
                    factors(i)
                send(i)
            pool.wait_ge(o_done["b"], H * TILES)
            for t in range(TILES):
                heads = gates[:, t, D:2 * D].rearrange("p (h v) -> p h v", v=VB)
                link(pool.tensor_tensor(heads, heads, r_o[:, t * H:t * H + H].unsqueeze(2).broadcast_to([P, H, VB]),
                                        ALU.mult))
                pool.tensor_tensor(heads, heads, gvec[:, gv["diff_sub"], :].unsqueeze(1).broadcast_to([P, H, VB]),
                                   ALU.mult).then_inc(sub_done, 1)
                pool.wait_ge(sub_done, t + 1)
            pool.wait_ge(t_copied, copied[("merged", TILES - 1, 1)] + 1)
            pool.memset(h[DEC:P, PT, :], 0.0).then_inc(zeroed, 1)
            pool.wait_ge(zeroed, 2)
            late_gpsimd(pool, link, inverse_rms)


def constants():
    pos = np.concatenate([np.arange(SEQ), PAST + np.arange(DEC), np.zeros(TOK - SEQ - DEC)]).astype(np.float32)
    parts = []
    for r in (RD, ROT):
        half = r // 2
        inv = np.float32(ROPE_THETA) ** (-np.arange(half, dtype=np.float32) * np.float32(2.0 / r))
        ang = pos[:, None] * inv[None, :]
        c, s = np.cos(ang), np.sin(ang)
        parts += [c, c, -s, s]
    iota = np.zeros((1, 320), np.float32)
    iota[0, 0:P] = np.arange(P)
    iota[0, P:P + NBLK + 1] = P * np.arange(NBLK + 1)
    iota[0, 192:192 + NE] = np.arange(NE)
    n = np.arange(TOK)
    valid = (n < SEQ + DEC).astype(np.float32)
    return {
        "c_ident": np.eye(P, dtype=np.float32),
        "c_rope": np.concatenate(parts, axis=1).astype(np.float32),
        "c_mask": np.concatenate([(np.arange(P) < CHUNK).astype(np.float32), np.full(CHUNK, -BIG, np.float32)])[None],
        "c_before": (np.arange(P)[:, None] < np.arange(P)[None, :]).astype(np.float32),
        "c_iota": iota,
        "c_token": np.stack([n + 1.0, valid, valid - 1.0], axis=1).astype(np.float32),
    }


def kernel(**inputs):
    from concourse import bacc
    from concourse.bass_utils import run_bass_kernel_spmd

    def flat(name, *shape):
        return np.ascontiguousarray(inputs[name]).reshape(shape)

    arrays = {
        "x": np.concatenate([flat("x_prompt", SEQ, D), flat("x_sample", DEC, D)]),
        "p": np.concatenate([flat("p_prompt", SEQ, DP), flat("p_sample", DEC, DP)]),
        "cache_ckv": flat("cache_mla_ckv", PAST, KVL), "cache_krope": flat("cache_mla_krope", PAST, RD),
        "cache_k": flat("cache_diff_k", PAST, D), "cache_v": flat("cache_diff_v", PAST, D),
        "w_in": flat("w_in", D, -1), "w_uq": flat("w_uq", QL, H * HD), "w_uk": flat("w_uk", KVL, H * NOPE),
        "w_uv": flat("w_uv", KVL, D), "w_out": flat("w_out", D, D),
        "w_rg": flat("w_router_grp", D, NG), "w_re": flat("w_router_exp", D, NE),
        "w_ei": flat("w_exp_in", NE * D, 2 * DE), "w_eo": flat("w_exp_out", NE * DE, D),
        "w_ple_gate": flat("w_ple_gate", D, D), "w_ple_proj": flat("w_ple_proj", DP, D),
        "b_rg": flat("b_router_grp", NG), "b_re": flat("b_router_exp", NE),
    }
    for g in ("g_mix", "g_q_lat", "g_kv_lat", "g_mla_qn", "g_mla_qr", "g_mla_kn", "g_mla_kr", "g_diff_q", "g_diff_k",
              "lambda_q1", "lambda_k1", "lambda_q2", "lambda_k2", "g_diff_sub", "g_ffn", "g_ple"):
        arrays[g] = flat(g, -1)
    arrays.update(constants())
    outs = {"y_p": (SEQ, D), "y_s": (DEC, D), "ckv_p": (SEQ, KVL), "kr_p": (SEQ, RD), "dk_p": (SEQ, D),
            "dv_p": (SEQ, D), "ckv_s": (DEC, KVL), "kr_s": (DEC, RD), "dk_s": (DEC, D), "dv_s": (DEC, D)}
    nc = bacc.Bacc("TRN2", target_bir_lowering=False, num_devices=1)
    a = {n: nc.dram_tensor("in_" + n, v.shape, mybir.dt.from_np(v.dtype), kind="ExternalInput").ap()
         for n, v in arrays.items()}
    o = {n: nc.dram_tensor("out_" + n, s, F32, kind="ExternalOutput").ap() for n, s in outs.items()}
    trunk(nc, a, o)
    r = run_bass_kernel_spmd(nc, [{"in_" + n: v for n, v in arrays.items()}], core_ids=[0]).results[0]
    g = {n: r["out_" + n] for n in outs}
    res = [g["y_p"].reshape(1, SEQ, D), g["y_s"].reshape(1, DEC, D)]
    for who, n in (("p", SEQ), ("s", DEC)):
        res += [g["ckv_" + who].reshape(1, 1, n, KVL), g["kr_" + who].reshape(1, 1, n, RD),
                g["dk_" + who].reshape(1, 1, n, H, 2, DB), g["dv_" + who].reshape(1, 1, n, H, VB)]
    return tuple(res)
```

```python
import math
from contextlib import ExitStack

import numpy as np
import concourse.bass as bass
from concourse import mybir

F32 = mybir.dt.float32
F32R = mybir.dt.float32r
I32 = mybir.dt.int32
U32 = mybir.dt.uint32
ACT = mybir.ActivationFunctionType
ALU = mybir.AluOpType
AX = mybir.AxisListType

P = 128
D = 1024
SEQ, DEC, PAST = 512, 64, 128
CHUNK = 64
PT = SEQ // P
TILES = PT + 1
ROWS = [P] * PT + [DEC]
TOK = TILES * P
CACHE = TILES
KEYS = SEQ + PAST + DEC
KCOL = [t * P for t in range(PT)] + [SEQ + PAST, SEQ]
EPS = 1e-6
H = 8
QL, KVL, NOPE, RD = 384, 256, 64, 32
HD = NOPE + RD
MLA_SCALE = 1.0 / math.sqrt(HD)
DB = 64
VB = 128
ROT = DB // 4
DIFF_SCALE = 1.0 / math.sqrt(DB)
LAM_INIT = 0.8 - 0.6 * math.exp(-0.3 * 0)
NG, EPG = 4, 8
NE = NG * EPG
DE = 256
DP = 256
SLOTS = P // 2
NBLK = NE + (2 * (SEQ + DEC) - 2) // SLOTS
MORE = -(-(SEQ + DEC) // SLOTS) - 1
REAL = SEQ + DEC
NASSIGN = 2 * REAL
BIG = 1e30
ROPE_THETA = 500000.0


class Item:

    def __init__(self, name, kind, src, col, width, kt, tiles, lhs, split, half=0):
        self.name, self.kind, self.src, self.col, self.width = name, kind, src, col, width
        self.kt, self.tiles, self.lhs, self.split, self.half = kt, tiles, lhs, split, half


def plan():
    columns, at = {}, 0
    for name, width in (("q_lat", QL), ("ckv", KVL + RD), ("dq", D), ("dk", D), ("dv", D), ("ga", D), ("gb", D)):
        columns[name] = at
        at += width

    def halves(name, kind, half):
        return Item(name, kind, "w_in", columns[name] + 512 * half, 512, 8, TILES, "act", True, half)

    first = [Item("q_lat", "norm", "w_in", columns["q_lat"], QL, 8, TILES, "act", True),
             Item("ckv", "norm", "w_in", columns["ckv"], KVL + RD, 8, TILES, "act", True),
             halves("dv", "store", 0),
             halves("dk", "norm", 0), halves("ga", "gate", 0), halves("dk", "norm", 1), halves("ga", "gate", 1),
             halves("dq", "norm", 0), halves("gb", "gate", 0), halves("dq", "norm", 1), halves("gb", "gate", 1),
             halves("dv", "store", 1)]
    uq = [Item("uq", "norm", "w_uq", 384 * half, 384, 3, TILES, "q_lat", False, half) for half in range(2)]
    uv = [Item("uv", "store", "w_uv", 512 * half, 512, 2, TILES + 1, "ckv", False, half) for half in range(2)]
    latent = [Item("uk", "norm", "w_uk", 0, 512, 2, TILES + 1, "ckv", False), uv[0], uq[0], uv[1], uq[1]]
    out = [Item("out", "residual", "w_out", 512 * half, 512, 8, TILES, "act", True, half) for half in range(2)]
    out += [Item("proj", "store", "w_ple_proj", 512 * half, 512, 2, TILES, "pe", True, half) for half in range(2)]
    ple = [Item("pgate", "ple", "w_ple_gate", 512 * half, 512, 8, TILES, "act", True, half) for half in range(2)]
    return first, latent, out, ple


def number(keys):
    return {k: i for i, k in enumerate(keys)}


def trunk(nc, a, o):
    first, latent, outp, ple = plan()
    phases = [first, latent, outp, ple]
    items = [c for ph in phases for c in ph]
    start = {id(ph): sum(len(x) for x in phases[:i]) for i, ph in enumerate(phases)}

    units = number([(i, t) for i, c in enumerate(items) for t in range(c.tiles)])
    granules = number([(i, g) for i, c in enumerate(items) if c.split for g in range(c.kt // 2)])
    normitems = number([i for i, c in enumerate(items) if c.kind == "norm"])
    RAW, RING = 3, 2
    QZ = 3
    RSUM = 6
    DEFERRED = [range(0, 2), range(2, 4), range(4, TILES), range(0)]
    EG, ERING = 12, 6
    PAIRS = (NBLK + 1) // 2
    TILE_ORDER = [0, 3, 4, 2, 1]
    LAG = {"b": 3, "a": 4}
    NORM_AT = {3 * t + 2: t for t in range(TILES)}
    TURN_AT = {3 * t + 6: t for t in range(TILES)}
    LATE_SLOT = 8
    EARLY = 2

    def subs(i):
        c = items[i]
        return 2 if c.name == "uk" else 1 if c.kind == "norm" else 0

    tgroups = [("x", t, s) for t in range(TILES) for s in range(2)]
    tgroups += [("cache_k", 0, 0), ("cache_k", 0, 1), ("cache_ckv", 0, 0)]
    tgroups += [(i, t, s) for i in range(len(first)) for t in range(items[i].tiles) for s in range(subs(i))]
    tgroups += [("attn_b", n, 0) for n in range(H * TILES)]
    last_uq = len(first) + len(latent) - 1
    tgroups += [(i, t, s) for i in range(len(first), last_uq) for t in range(items[i].tiles) for s in range(subs(i))]
    for n in range(H * TILES + LAG["a"]):
        tgroups += [("attn_a", n - LAG["a"], 0)] if n >= LAG["a"] else []
        tgroups += [(last_uq, TURN_AT[n], 0)] if n in TURN_AT else []
    tgroups += [("merged", t, s) for t in TILE_ORDER for s in range(2)]
    tgroups += [("pe", t, 0) for t in range(TILES)]
    tgroups += [("hn", t, s) for t in range(TILES) for s in range(2)]
    tgroups += [("hp", t, s) for t in range(TILES) for s in range(2)]
    tg = number(tgroups)

    with ExitStack() as ctx:
        def sb(name, shape, dt=F32, c=ctx):
            return c.enter_context(nc.sbuf_tensor(name, shape, dt))

        def sem(name):
            return ctx.enter_context(nc.semaphore(name))

        def dram(name, shape, dt=F32):
            return nc.dram_tensor(name, shape, dt, kind="Internal").ap()

        acc = ctx.enter_context(nc.psum_tensor("acc", [P, 6, 512], F32))
        tp = ctx.enter_context(nc.psum_tensor("tp", [P, 2, 512], F32))

        va_rows = dram("va_rows", [TOK + P, D])
        hn_rows = dram("hn_rows", [REAL, D])
        y_rows = dram("y_rows", [NASSIGN, D])
        pj_rows = dram("pj_rows", [TOK, D])

        ident = sb("ident", [P, P])
        small = sb("small", [P, 512])
        raw = sb("raw", [P, RAW, 2, 512])
        whi = sb("whi", [P, RING, 2, 512], F32R)
        wlo = sb("wlo", [P, RING, 2, 512], F32R)
        grow = sb("grow", [P, D])
        neghalf = sb("neghalf", [P, 64])

        mask = sb("mask", [1, P + 64])
        rope = sb("rope", [P, TILES, 96])
        zs = sb("zs", [P, 6, 512])
        sq = sb("sq", [P, 512])
        rot = sb("rot", [P, 2, 128])

        early = ExitStack()
        gates = sb("gates", [P, TILES, 2 * D], c=early)
        q_latT = sb("q_latT", [P, 3, TOK], c=early)
        ckvT = sb("ckvT", [P, 2, TOK + P], c=early)
        krope = sb("krope", [P, 6, RD], c=early)
        qT = sb("qT", [P, H, SEQ + DEC], c=early)
        kT = sb("kT", [P, H, KEYS], c=early)
        vh = sb("vh", [P, 2, 6, VB], c=early)
        gq_lat = sb("gq_lat", [P, QL], c=early)
        gkv = sb("gkv", [P, KVL + RD], c=early)
        gvec = sb("gvec", [P, 6, P], c=early)
        qz = sb("qz", [P, QZ, 2, P], c=early)
        halves = ExitStack()
        lhi = sb("lhi", [P, 8, TOK], F32R, c=halves)
        llo = sb("llo", [P, 8, TOK], F32R, c=halves)
        halves.close()
        inner = ExitStack()
        w_uq = sb("w_uq", [P, 3, 768], c=inner)
        w_uk = sb("w_uk", [P, 2, 512], c=inner)
        w_uv = sb("w_uv", [P, 2, 1024], c=inner)
        pr = sb("pr", [P, 3, 2, 512], c=inner)
        prT = sb("prT", [P, 2, 4, P], c=inner)
        inner.close()
        halves2 = ExitStack()
        lhi2 = sb("lhi2", [P, 8, TOK], F32R, c=halves2)
        llo2 = sb("llo2", [P, 8, TOK], F32R, c=halves2)
        halves2.close()
        early.close()
        h = sb("h", [P, TILES, D])
        src_row = sb("src_row", [P, PAIRS + 2], I32)
        dst_row = sb("dst_row", [P, PAIRS], I32)
        gate_of = sb("gate_of", [P, PAIRS])
        expert_of = sb("expert_of", [1, 2 * PAIRS + 2], I32)
        n_blocks = sb("n_blocks", [1, 2], I32)
        row_in = sb("row_in", [P, 1], I32)
        row_out = sb("row_out", [P, 1], I32)
        gate_in = sb("gate_in", [P, 1])
        embed = ExitStack()
        sb("first_slots", [P, LATE_SLOT, D], c=embed)
        ptok = sb("ptok", [P, TILES, DP], c=embed)
        phi = sb("phi", [P, 2, TOK], F32R, c=embed)
        plo = sb("plo", [P, 2, TOK], F32R, c=embed)
        embed.close()
        raw_e = sb("raw_e", [P, EG, D])
        route = ExitStack()
        xn = sb("xn", [P, TILES, D], c=route)
        xnT = sb("xnT", [P, 2, 8, P], c=route)
        w_r = sb("w_r", [P, 8, NG + NE], c=route)
        b_r = sb("b_r", [P, NG + NE], c=route)
        iota = sb("iota", [P, 320], c=route)
        token = sb("token", [P, TILES, 3], c=route)
        before = sb("before", [P, P], c=route)
        ones = sb("ones", [P, P], c=route)
        rt = sb("rt", [P, 3584], c=route)
        big = sb("big", [P, 2 * TILES * (P + PAIRS + 1)], c=route)
        route.close()
        moe = ExitStack()
        xg = sb("xg", [P, 2, D], c=moe)
        ehi = sb("ehi", [P, ERING, D], F32R, c=moe)
        elo = sb("elo", [P, ERING, D], F32R, c=moe)
        xhi = sb("xhi", [P, 8, P], F32R, c=moe)
        xlo = sb("xlo", [P, 8, P], F32R, c=moe)
        gg = sb("gg", [P, DE], c=moe)
        ghi = sb("ghi", [P, 2, P], F32R, c=moe)
        glo = sb("glo", [P, 2, P], F32R, c=moe)
        ye = zs[:, 0:2, :].rearrange("p a n -> p (a n)")
        moe.close()
        ysum = raw_e[:, 0:6, :].rearrange("p (b j) n -> p b j n", b=3)
        hp = xg
        pj = raw_e[:, 6:6 + TILES, :]

        def part(at, n):
            return small[:, at:at + n]

        ss_z = [part(0, 48), part(48, 48)]
        r_z = [part(96, 48), part(144, 48)]
        ss_x, r_x = part(192, 5), part(200, 5)
        ss_o, r_o = part(208, 40), part(248, 40)
        negmax, sums, rsum = part(288, 4), part(292, 4), part(352, 12)
        lamv = part(304, 8)
        pair = part(312, 2)

        ld_start, ld_const = sem("ld_start"), sem("ld_const")
        ld_x = [sem(f"ld_x{t}") for t in range(TILES)]
        ld_raw = [sem(f"ld_raw{s}") for s in range(RAW)]
        ld_v = [sem(f"ld_v{s}") for s in range(2)]
        ld_wu = sem("ld_wu")
        zeroed = sem("zeroed")
        hi_done, lo_done, w_used = sem("hi_done"), sem("lo_done"), sem("w_used")
        z_done, z_copied = sem("z_done"), sem("z_copied")
        sq_done, ss_done, rstd_done, y_done = sem("sq_done"), sem("ss_done"), sem("rstd_done"), sem("y_done")
        t_done, t_copied, hi_copied, pt_copied = sem("t_done"), sem("t_copied"), sem("hi_copied"), sem("pt_copied")
        x_sq, x_rstd, xn_done = sem("x_sq"), sem("x_rstd"), sem("xn_done")
        outz = [sem(f"outz{t}") for t in range(6)]
        lam_dots, lam_exp = sem("lam_dots"), sem("lam_exp")
        s_done = {p: sem(f"s_done_{p}") for p in "ba"}
        qz_done, q_zeroed = sem("qz_done"), sem("q_zeroed")
        nm_done = {p: sem(f"nm_done_{p}") for p in "ba"}
        exp_done = {p: sem(f"exp_done_{p}") for p in "ba"}
        pv_done = {p: sem(f"pv_done_{p}") for p in "ba"}
        o_done = {p: sem(f"o_done_{p}") for p in "ba"}
        comb_done = {p: sem(f"comb_done_{p}") for p in "ba"}
        sqo_done, ro_done = sem("sqo_done"), sem("ro_done")
        merged_done = sem("merged_done")
        sub_done = sem("sub_done")
        ld_h = sem("ld_h")
        dve_own, act_own, pool_own = sem("dve_own"), sem("act_own"), sem("pool_own")

        copied = number([k for k in tgroups if k[0] not in ("attn_b", "attn_a", "hn")])
        pt = number([k for k in tgroups if k[0] in ("attn_b", "attn_a")])

        def wait_group_copied(eng, key):
            if key in copied:
                eng.wait_ge(t_copied, copied[key] + 1)
            elif key[0] == "hn":
                eng.wait_ge(hn_copied, 2 * key[1] + key[2] + 1)
            else:
                eng.wait_ge(pt_copied, pt[key] + 1)

        def wait_bank_for(eng, key):
            if tg[key] >= 2:
                wait_group_copied(eng, tgroups[tg[key] - 2])

        def dmas_of(i):
            return {"ckv": 2, "dk": 1, "dv": 1, "uv": 1}.get(items[i].name, 0)

        def out_count(i, t):
            return sum(dmas_of(n) for n in range(i + 1) if items[n].tiles > t)

        def uses_zs(i):
            return items[i].kind in ("norm", "residual", "ple") or items[i].name == "dv" or (
                items[i].name == "proj" and not items[i].half)

        def embed_tile(half, t):
            return raw_e[:, t // 2, 512 * (t % 2):512 * (t % 2) + 512] if half else zs[:, t, :]

        def deferred(i):
            ph = next(ph for ph in phases if i in phase_items(ph))
            return items[i].kind == "norm" and i + 2 in phase_items(ph) and not uses_zs(i + 1)

        def uv_tile(t):
            return raw[:, t // 2, t % 2, :]

        def kas(t):
            flat = [pr, prT, qz][max(t - 3, 0)][:, :, :, :].rearrange("p a b c -> p (a b c)")
            at = t * H * HD if t < 4 else 0
            return flat[:, at:at + H * HD]

        def wait_slot_free(eng, i, t):
            before = [n for n in range(i) if uses_zs(n) and items[n].tiles > t]
            if not before:
                return
            n = before[-1]
            c = items[n]
            if c.kind == "norm" and c.name != "uk":
                eng.wait_ge(t_done, tg[(n, t, subs(n) - 1)] + 1)
            if c.name == "uk":
                eng.wait_ge(y_done, y_index[(n, t)] + 1)
            if c.kind in ("residual", "ple"):
                eng.wait_ge(y_done, y_index[(n, t)] + 1)
            if c.name == "proj":
                eng.wait_ge(pj_sent[t], 16)
            if out_count(n, t):
                eng.wait_ge(outz[t], 16 * out_count(n, t))

        y_norm = number([(i, t) for i, c in enumerate(items) if c.kind == "norm" for t in range(c.tiles)])

        def last_norm(ph):
            return [i for i in phase_items(ph) if items[i].kind == "norm"][-1]

        def unit(n):
            return n // TILES, TILE_ORDER[n % TILES]

        def score_bank(ph, n, c):
            return 2 * (n % 2) + c if ph == "b" else n % 4

        def bank_uses(ph):
            return 2 if ph == "b" else 4

        def probs(ph, n, c):
            return pr[:, n % 3, c, :] if ph == "b" else pr[:, n % 3, (n // 3) % 2, :]

        def prob_slots(ph):
            return 3 if ph == "b" else 6

        def y_norm_of_phase(ph):
            return sum(c.tiles for x in phases[:phases.index(ph) + 1] for c in x if c.kind == "norm")

        hi_index = number([k for k in tgroups if k[0] in ("x", "merged", "pe", "hp")])
        y_index = number([(i, t) for i, c in enumerate(items) if c.kind in ("norm", "residual", "ple")
                          for t in range(c.tiles)])

        def groups(i):
            return {"q_lat": [(0, 1, QL, QL, 1.0)],
                    "ckv": [(0, 1, KVL, KVL, 1.0), (KVL, 1, RD, RD, 1.0)],
                    "dq": [(0, 8, DB, DB, DIFF_SCALE ** 2)],
                    "dk": [(0, 8, DB, DB, 1.0)],
                    "uq": [(0, 4, NOPE, HD, 1.0 / HD), (NOPE, 4, RD, HD, 1.0 / HD)],
                    "uk": [(0, 8, NOPE, NOPE, 1.0)]}[items[i].name]

        def grouped(tile, g):
            off, n, size, stride, _ = g
            if n == 1:
                return tile[:, off:off + size].unsqueeze(1)
            return tile[:, 0:n * stride].rearrange("p (n s) -> p n s", s=stride)[:, :, off % stride:off % stride + size]

        inner_granules = number([k for k in granules if k[1] < items[k[0]].kt // 2 - 1])
        granule_list = list(granules)

        def wait_ring_free(eng, n):
            if n < RING:
                return
            i, g = granule_list[n - RING]
            if (i, g) in inner_granules:
                eng.wait_ge(w_used, inner_granules[(i, g)] + 1)
            else:
                eng.wait_ge(z_done, units[(i, items[i].tiles - 1)] + 1)

        def phase_items(ph):
            return range(start[id(ph)], start[id(ph)] + len(ph))

        ds = bass.ds
        ss_h, sum_h, r_h = part(368, 10), part(320, 5), part(328, 5)
        ss_f, r_f = part(336, 6), part(344, 5)
        h_sq, h_rstd, hn_done, hn_sent = sem("h_sq"), sem("h_rstd"), sem("hn_done"), sem("hn_sent")
        hn_copied = sem("hn_copied")
        ld_g, ld_late = sem("ld_g"), sem("ld_late")
        ones_set = sem("ones_set")
        logits_done, grp_shift, grp_exp, exp2_in, exp2_out = (
            sem("logits_done"), sem("grp_shift"), sem("grp_exp"), sem("exp2_in"), sem("exp2_out"))
        hot_done, rank_done, plan_in, plan_done, routed = (
            sem("hot_done"), sem("rank_done"), sem("plan_in"), sem("plan_done"), sem("routed"))
        ld_e = [sem(f"ld_e{j}") for j in range(EG)]
        ld_xg = sem("ld_xg")
        hi_e, lo_e, used_e, t_e, thi_e, tlo_e = (sem("hi_e"), sem("lo_e"), sem("used_e"), sem("t_e"), sem("thi_e"),
                                                 sem("tlo_e"))
        silu_e, g_e, ya_e, yd_e, sent_e = sem("silu_e"), sem("g_e"), sem("ya_e"), sem("yd_e"), sem("sent_e")
        tg_e, ghi_e, glo_e = sem("tg_e"), sem("ghi_e"), sem("glo_e")
        gate_e, own_e, in_e = sem("gate_e"), sem("own_e"), sem("in_e")
        left_e = sem("left_e")
        sp_steps = sem("sp_steps")
        pool_steps = sem("pool_steps")
        moe_done = sem("moe_done")
        ld_y, y_added, f_sq, f_rstd, fn_done, ld_p = (
            [sem(f"ld_y{j}") for j in range(3)], sem("y_added"), sem("f_sq"), sem("f_rstd"), sem("fn_done"), sem("ld_p"))
        st_y, y_summed, ld_pj = sem("st_y"), sem("y_summed"), sem("ld_pj")
        pj_sent = [sem(f"pj_sent{t}") for t in range(TILES)]
        ORDER = [(0, g) for g in range(4)] + [(1, g) for g in range(4)] + [(0, 4), (0, 5), (1, 4), (1, 5)]
        residual_last = start[id(outp)] + 1
        ple_first = start[id(ple)]

        def each_pair(eng, n, pair):
            with eng.Fori(0, NE // 2) as i:
                pair(i)
            with eng.If(NE < n):
                with eng.Fori(NE // 2, PAIRS) as i:
                    with eng.If(i * 2 < n):
                        pair(i)

        def late_sync(sp):
            for dst, src in ((w_r[:, :, 0:NG], a["w_rg"].rearrange("(k p) n -> p k n", p=P)),
                             (w_r[:, :, NG:NG + NE], a["w_re"].rearrange("(k p) n -> p k n", p=P)),
                             (b_r[:, 0:NG], a["b_rg"].partition_broadcast(P)),
                             (b_r[:, NG:NG + NE], a["b_re"].partition_broadcast(P)),
                             (iota[:, :], a["c_iota"].partition_broadcast(P)),
                             (token[:, :, :], a["c_token"].rearrange("(t p) n -> p t n", p=P)),
                             (before[:, :], a["c_before"])):
                sp.dma_start(dst, src).then_inc(ld_late, 16)
            every = [(i, g) for i in phase_items(ple) for g in range(items[i].kt // 2)]
            for i, g in every[:RAW]:
                load_granule(sp, i, g)

            def load_expert(e, q):
                g = ORDER[q][1]
                if g < 4:
                    sp.dma_start(raw_e[:, q, :].rearrange("p (k n) -> p k n", k=2),
                                 a["w_ei"][ds(e * D + 2 * g * P, 2 * P), :].rearrange("(k p) n -> p k n", p=P)
                                 ).then_inc(ld_e[q], 16)
                else:
                    sp.dma_start(raw_e[:, q, :], a["w_eo"][ds(e * DE + (g - 4) * P, P), :]).then_inc(ld_e[q], 16)

            for t in range(TILES):
                sp.wait_ge(hn_done, t + 1)
                sp.dma_start(hn_rows[t * P:t * P + ROWS[t], :], xn[0:ROWS[t], t, :]).then_inc(hn_sent, 16)
            sp.dma_start(grow[:, :], a["g_ple"].partition_broadcast(P)).then_inc(ld_g, 16)
            for i in (residual_last + 1, residual_last + 2):
                for t in range(TILES):
                    sp.wait_ge(z_copied, units[(i, t)] + 1)
                    sp.dma_start(pj_rows[t * P:t * P + P, 512 * items[i].half:512 * items[i].half + 512],
                                 embed_tile(items[i].half, t)).then_inc(pj_sent[t], 16)
            for t in range(TILES):
                sp.wait_ge(pj_sent[t], 32)
            for q in range(EG):
                load_expert(ORDER[q][0], q)
            sp.wait_ge(routed, 1)
            for i, g in every[RAW:RAW + EARLY]:
                load_granule(sp, i, g)
            n = sp.value_load(n_blocks[0:1, 0:1], min_val=1, max_val=NBLK)

            def load_pair(first_block, queue, before):
                e = [sp.value_load(expert_of[0:1, ds(first_block + j, 1)], min_val=0, max_val=NE - 1)
                     for j in range(2)]
                for q in queue:
                    before(q)
                    load_expert(e[ORDER[q][0]], q)

            def pair(i):
                def halved(q):
                    sp.wait_ge(lo_e, i * EG + (q + 1))

                with sp.If(i * 2 + 2 < n):
                    load_pair(i * 2 + 2, range(EG), halved)
                sp.sem_inc(sp_steps, 1)

            each_pair(sp, n, pair)
            sp.wait_ge(moe_done, 1)
            for t in range(TILES):
                if t >= 3:
                    sp.wait_ge(y_added, t - 2)
                sp.dma_start(ysum[0:ROWS[t], t % 3, :, :],
                             y_rows.rearrange("(j n) d -> n j d", j=2)[t * P:t * P + ROWS[t], :, :]
                             ).then_inc(ld_y[t % 3], 16)
            for t in range(TILES):
                sp.wait_ge(pj_sent[t], 32)
            sp.dma_start(pj, pj_rows.rearrange("(t p) n -> p t n", p=P)).then_inc(ld_pj, 16)
            for i, g in every[RAW + EARLY:]:
                load_granule(sp, i, g)

        def late_tensor(pe, turn, run):
            for t in range(TILES + 1):
                if t < TILES:
                    pe.wait_ge(hn_done, t + 1)
                    for s in range(2):
                        turn(("hn", t, s), [xn[:, t, j * P:j * P + P] for j in range(4 * s, 4 * s + 4)])
                if t == 0:
                    pe.wait_ge(ld_late, 16 * 7)
                    pe.wait_ge(z_copied, units[(residual_last + 2, TILES - 1)] + 1)
                    continue
                t -= 1
                wait_group_copied(pe, ("hn", t, 1))
                for k in range(8):
                    mm = pe.matmul(acc[:, t, 0:NG + NE], xnT[:, t % 2, k, :], w_r[:, k, :], start=(k == 0),
                                   stop=(k == 7))
                mm.then_inc(logits_done, 1)
            pe.wait_ge(hot_done, 1)
            pe.wait_ge(ones_set, 1)
            ranks = acc[:, 5, 0:(TILES + 1) * NE].rearrange("p (t e) -> p t e", e=NE)
            mm = pe.matmul(ranks, before[:, :], R["hot"][:, :, :], start=True, stop=False)
            for u in range(TILES):
                left = TILES - u
                mm = pe.matmul(ranks[:, u + 1:, :], ones[:, :],
                               R["hot"][:, u, :].unsqueeze(1).broadcast_to([P, left, NE]), start=False,
                               stop=(u == TILES - 1))
            mm.then_inc(rank_done, 1)
            pe.wait_ge(plan_in, 1)
            for n in range(2 * TILES):
                mm = pe.matmul(acc[:, 0, 0:3 * PAIRS], R["in_block"][:, n, :], R["what"][:, n, :], start=(n == 0),
                               stop=(n == 2 * TILES - 1))
            mm.then_inc(plan_done, 1)

            pe.wait_ge(routed, 1)
            n = pe.value_load(n_blocks[0:1, 0:1], min_val=1, max_val=NBLK)

            def turn_tokens(s):
                for j in range(4):
                    k = 4 * s + j
                    tr = pe.transpose(tp[:, s, j * P:j * P + P], xg[:, 0, k * P:k * P + P], ident[:, :])
                tr.then_inc(t_e, 1)

            pe.wait_ge(ld_xg, 16)
            for s in range(2):
                turn_tokens(s)
            pe.wait_ge(tlo_e, 2)
            def pair(i):
                def product(q, out, lhs, n0, n1, first_, last_):
                    for x, w in ((0, 0), (0, 1), (1, 0)):
                        mm = pe.matmul(out, lhs[x], (ehi, elo)[w][:, q % ERING, n0:n1],
                                       start=(first_ and x + w == 0), stop=(last_ and x == 1))
                    return mm

                def hidden(b):
                    for g in range(4):
                        q = 4 * b + g
                        pe.wait_ge(lo_e, i * EG + (q + 1))
                        for k in range(2):
                            kk = 2 * g + k
                            mm = product(q, acc[:, b, :], (xhi[:, kk, :], xlo[:, kk, :]), 512 * k,
                                         512 * k + 512, kk == 0, kk == 7)
                        mm.then_inc(used_e, 1)

                def outputs(b):
                    for k in range(2):
                        q = 8 + 2 * b + k
                        pe.wait_ge(lo_e, i * EG + (q + 1))
                        for half in range(2):
                            mm = product(q, acc[:, 2 + 2 * b + half, :], (ghi[:, k, :], glo[:, k, :]),
                                         512 * half, 512 * half + 512, k == 0, k == 1)
                        mm.then_inc(used_e, 1)

                pe.wait_ge(tlo_e, i * 2 + 2)
                hidden(0)
                hidden(1)
                with pe.If(i * 2 + 2 < n):
                    pe.wait_ge(ld_xg, i * 16 + 32)
                    for s in range(2):
                        turn_tokens(s)
                pe.wait_ge(g_e, i * 2 + 2)
                pe.wait_ge(ya_e, i * 2 + 2)
                pe.wait_ge(yd_e, i * 2 + 2)
                for j in range(2):
                    tr = pe.transpose(acc[:, 4, j * P:j * P + P], gg[:, j * P:j * P + P], ident[:, :])
                tr.then_inc(tg_e, 1)
                pe.wait_ge(glo_e, i + 1)
                outputs(0)
                outputs(1)

            each_pair(pe, n, pair)

            pe.wait_ge(moe_done, 1)
            for t in range(TILES):
                pe.wait_ge(fn_done, t + 1)
                for s in range(2):
                    turn(("hp", t, s), [hp[:, t % 2, j * P:j * P + P] for j in range(4 * s, 4 * s + 4)])
            run(ple)

        def steps_of_pair(split, turned, hidden, turned_g, result, another):
            for q in (6, 7, 8):
                split(q)
            hidden(0)
            for q in (9, 10, 11):
                split(q)
            hidden(1)
            turned_g()
            with another():
                for s in range(2):
                    turned(s)
                for q in range(4):
                    split(q, 1)
            result(0)
            with another():
                for q in range(4, ERING):
                    split(q, 1)
            result(1)

        def late_scalar(act, link, halve_hi, split_hi, run):
            for t in range(TILES):
                for s in range(2):
                    act.wait_ge(t_done, tg[("hn", t, s)] + 1)
                    if t >= 2:
                        act.wait_ge(logits_done, t - 1)
                    act.activation(xnT[:, t % 2, 4 * s:4 * s + 4, :],
                                   tp[:, tg[("hn", t, s)] % 2, :].rearrange("p (k r) -> p k r", r=P),
                                   ACT.Copy).then_inc(hn_copied, 1)
            act.wait_ge(grp_shift, 1)
            act.activation(R["e_grp"], R["shifted"], ACT.Exp).then_inc(grp_exp, 1)
            act.wait_ge(exp2_in, 1)
            act.activation(R["e2"], R["d2"], ACT.Exp).then_inc(exp2_out, 1)

            act.wait_ge(routed, 1)
            act.wait_ge(hn_sent, 16 * TILES)
            n = act.value_load(n_blocks[0:1, 0:1], min_val=1, max_val=NBLK)

            def halve_weights(q):
                act.activation(ehi[:, q % ERING, :], raw_e[:, q, :], ACT.Copy).then_inc(hi_e, 1)

            def halve_tokens(s):
                act.activation(xhi[:, 4 * s:4 * s + 4, :], tp[:, s, :].rearrange("p (k r) -> p k r", r=P),
                               ACT.Copy).then_inc(thi_e, 1)

            for q in range(2):
                act.wait_ge(ld_e[q], 16)
                halve_weights(q)
            for g in range(EARLY):
                split_hi(ple_first, g)
            for s in range(2):
                act.wait_ge(t_e, s + 1)
                halve_tokens(s)
            for q in range(2, ERING):
                act.wait_ge(ld_e[q], 16)
                halve_weights(q)
            def pair(i):
                def split(q, next_=0):
                    act.wait_ge(ld_e[q], i * 16 + 16 * (1 + next_))
                    act.wait_ge(used_e, i * EG + (EG * next_ + q - ERING + 1))
                    halve_weights(q)

                def turned(s):
                    act.wait_ge(t_e, i * 2 + (s + 3))
                    halve_tokens(s)

                def silu(b):
                    act.wait_ge(used_e, i * EG + (4 * b + 4))
                    rows = slice(SLOTS * b, SLOTS * b + SLOTS)
                    act.activation(gg[rows, :], acc[rows, b, 0:DE], ACT.Silu).then_inc(silu_e, 1)

                def turned_g():
                    act.wait_ge(tg_e, i + 1)
                    act.activation(ghi[:, :, :], acc[:, 4, 0:DE].rearrange("p (k r) -> p k r", r=P),
                                   ACT.Copy).then_inc(ghi_e, 1)

                def result(b):
                    act.wait_ge(used_e, i * EG + (2 * b + 10))
                    act.wait_ge(gate_e, i + 1)
                    act.wait_ge(left_e, i + 1)
                    rows = slice(SLOTS * b, SLOTS * b + SLOTS)
                    act.activation(ye[rows, 0:512], acc[rows, 2 + 2 * b, :], ACT.Copy,
                                   scale=gate_in[rows, :]).then_inc(ya_e, 1)

                steps_of_pair(split, turned, silu, turned_g, result, lambda: act.If(i * 2 + 2 < n))

            each_pair(act, n, pair)

            act.activation(ss_f[0:1, TILES:TILES + 1], neghalf[0:1, 0:1], ACT.Square)
            act.wait_ge(pj_sent[4], 32)
            for t in range(TILES + 2):
                if t < TILES:
                    act.wait_ge(y_added, t + 1)
                    if t:
                        act.wait_ge(f_sq, t)
                    act.activation(zs[:, 4:6, :].rearrange("p a b -> p (a b)"), h[:, t, :], ACT.Square,
                                   accum_out=ss_f[:, t:t + 1]).then_inc(f_sq, 1)
                if t >= 2:
                    for s in range(2):
                        halve_hi("hp", s, t - 2, 4, lhi2)
            run(ple, EARLY)

        R, at = {}, 0
        for name, shape in (("lg", (TILES, 8)), ("m8", (TILES, 8)), ("le", (TILES, NE)), ("v8", (TILES, 8)),
                            ("shifted", (TILES, NG)), ("e_grp", (TILES, NG)), ("pen", (TILES, NG)),
                            ("gsum", (TILES,)), ("gidx", (TILES,)), ("d2", (TILES,)), ("e2", (TILES,)),
                            ("idx", (2, TILES)), ("w", (2, TILES)), ("hot1", (2, TILES, NE)), ("hot", (TILES + 1, NE)), ("more", (NE, MORE)),
                            ("cnt", (NE,)), ("cum", (NE,)), ("startof", (NE,)), ("later", (TILES, NE)), ("slot", (2 * TILES,)),
                            ("nge", (2 * TILES,))):
            n = int(np.prod(shape))
            v = rt[:, at:at + n]
            names = "abc"[:len(shape)]
            if len(shape) > 1:
                v = v.rearrange(f"p ({' '.join(names)}) -> p {' '.join(names)}", **dict(zip(names, shape)))
            R[name] = v
            at += n
        R["i8"] = rt[:, at:at + 8 * TILES].bitcast(U32).rearrange("p (a b) -> p a b", b=8)
        at += 8 * TILES
        base = at
        R["slotbase"] = rt[:, at:at + TILES * NE].rearrange("p (a b) -> p a b", b=NE)
        R["in_block"] = big[:, 0:2 * TILES * P].rearrange("p (a b) -> p a b", b=P)
        R["ge"] = big[:, 2 * TILES * P:2 * TILES * (P + PAIRS + 1)].rearrange("p (a b) -> p a b", b=PAIRS + 1)
        bigT = xnT[:, :, :, :].rearrange("p a b c -> p (a b c)")
        R["what"] = bigT[:, 0:10 * 3 * PAIRS].rearrange("p (a b) -> p a b", b=3 * PAIRS)
        at = base + TILES * NE
        R["oh_blk"] = rt[:, at:at + 10 * PAIRS].rearrange("p (a b) -> p a b", b=PAIRS)
        at += 10 * PAIRS
        R["pl"] = rt[:, at:at + 3 * PAIRS].rearrange("p (a b) -> p a b", b=PAIRS)
        at += 3 * PAIRS
        R["tmp"] = rt[:, at:at + (NBLK - NE) * NE]
        at += (NBLK - NE) * NE
        assert at <= 3584, at

        def late_vector(dve, link, halve_lo, split_lo, run):
            io128, io_pair, io_slots, io_e = (iota[:, 0:P], iota[:, P:P + PAIRS + 1], iota[:, 160:160 + MORE + 1],
                                              iota[:, 192:192 + NE])
            dve.wait_ge(ld_late, 16 * 7)
            dve.wait_ge(logits_done, TILES)
            lgt = acc[:, 0:TILES, 0:NG + NE]
            dve.memset(R["hot"][:, TILES, :], 0.0)
            dve.memset(R["lg"], -3e38)
            link(dve.tensor_tensor(R["le"], lgt[:, :, NG:NG + NE],
                                   b_r[:, NG:NG + NE].unsqueeze(1).broadcast_to([P, TILES, NE]), ALU.add))
            link(dve.tensor_tensor(R["lg"][:, :, 0:NG], lgt[:, :, 0:NG],
                                   b_r[:, 0:NG].unsqueeze(1).broadcast_to([P, TILES, NG]), ALU.add))
            for t in range(TILES):
                ins = dve.max(R["m8"][:, t, :], R["lg"][:, t, :])
            link(ins)
            dve.tensor_tensor(R["shifted"], R["lg"][:, :, 0:NG], R["m8"][:, :, 0:1].broadcast_to([P, TILES, NG]),
                              ALU.subtract).then_inc(grp_shift, 1)
            for t in range(TILES):
                ins = dve.max_index(R["i8"][:, t, :], R["m8"][:, t, :], R["lg"][:, t, :])
            link(ins)
            link(dve.tensor_copy(R["gidx"], R["i8"][:, :, 0]))
            link(dve.tensor_tensor(R["pen"], R["gidx"].unsqueeze(2).broadcast_to([P, TILES, NG]),
                                   io_e[:, 0:NG].unsqueeze(1).broadcast_to([P, TILES, NG]), ALU.is_equal))
            link(dve.tensor_scalar(R["pen"], R["pen"], -1.0, BIG, ALU.add, ALU.mult))
            le3 = R["le"].rearrange("p t (g e) -> p (t g) e", e=EPG)
            link(dve.tensor_tensor(le3, le3, R["pen"].rearrange("p t g -> p (t g)").unsqueeze(2).broadcast_to(
                [P, TILES * NG, EPG]), ALU.add))
            for t in range(TILES):
                ins = dve.max(R["v8"][:, t, :], R["le"][:, t, :])
            link(ins)
            dve.tensor_tensor(R["d2"], R["v8"][:, :, 1], R["v8"][:, :, 0], ALU.subtract).then_inc(exp2_in, 1)
            for t in range(TILES):
                ins = dve.max_index(R["i8"][:, t, :], R["v8"][:, t, :], R["le"][:, t, :])
            link(ins)
            for j in range(2):
                ins = dve.tensor_copy(R["idx"][:, j, :], R["i8"][:, :, j])
            link(ins)
            for j in range(2):
                ins = dve.tensor_tensor(R["hot1"][:, j, :, :],
                                        R["idx"][:, j, :].unsqueeze(2).broadcast_to([P, TILES, NE]),
                                        io_e.unsqueeze(1).broadcast_to([P, TILES, NE]), ALU.is_equal)
            link(ins)
            for j in range(2):
                ins = dve.tensor_tensor(R["hot1"][:, j, :, :], R["hot1"][:, j, :, :],
                                        token[:, :, 1:2].broadcast_to([P, TILES, NE]), ALU.mult)
            link(ins)
            dve.tensor_tensor(R["hot"][:, 0:TILES, :], R["hot1"][:, 0, :, :], R["hot1"][:, 1, :, :], ALU.add).then_inc(hot_done, 1)
            dve.wait_ge(grp_exp, 1)
            link(dve.tensor_reduce(R["gsum"], R["e_grp"], AX.X, ALU.add))
            link(dve.reciprocal(R["gsum"], R["gsum"]))
            dve.wait_ge(exp2_out, 1)
            link(dve.tensor_scalar(R["d2"], R["e2"], 1.0, None, ALU.add))
            link(dve.reciprocal(R["d2"], R["d2"]))
            link(dve.tensor_tensor(R["w"][:, 0, :], R["d2"], R["gsum"], ALU.mult))
            dve.tensor_tensor(R["w"][:, 1, :], R["w"][:, 0, :], R["e2"], ALU.mult)
            dve.wait_ge(rank_done, 1)
            ranks = acc[:, 5, 0:(TILES + 1) * NE].rearrange("p (t e) -> p t e", e=NE)
            dve.tensor_scalar(R["later"], ranks[:, 0:TILES, :], float(SLOTS), None, ALU.is_ge)
            link(dve.tensor_tensor(R["more"], ranks[:, TILES, :].unsqueeze(2).broadcast_to([P, NE, MORE]),
                                   io_slots[:, 1:].unsqueeze(1).broadcast_to([P, NE, MORE]), ALU.is_gt))
            link(dve.tensor_reduce(R["cnt"], R["more"], AX.X, ALU.add))
            link(dve.tensor_tensor_scan(R["cum"], ones[:, 0:NE], R["cnt"], 0.0, ALU.mult, ALU.add))
            link(dve.tensor_tensor(R["startof"], R["cum"], R["cnt"], ALU.subtract))
            link(dve.tensor_scalar(R["startof"], R["startof"], float(NE - 1), None, ALU.add))
            link(dve.tensor_tensor(R["startof"], R["startof"], io_e, ALU.subtract))
            link(dve.tensor_tensor(R["later"], R["later"], R["startof"].unsqueeze(1).broadcast_to([P, TILES, NE]),
                                   ALU.mult))
            link(dve.tensor_tensor(R["later"], R["later"], io_e.unsqueeze(1).broadcast_to([P, TILES, NE]), ALU.add))
            link(dve.scalar_tensor_tensor(R["slotbase"], R["later"], float(SLOTS), ranks[:, 0:TILES, :], ALU.mult,
                                          ALU.add))
            for j in range(2):
                ins = dve.tensor_tensor(R["hot1"][:, j, :, :], R["hot1"][:, j, :, :], R["slotbase"], ALU.mult)
            link(ins)
            for j in range(2):
                ins = dve.tensor_reduce(R["slot"][:, j * TILES:j * TILES + TILES], R["hot1"][:, j, :, :], AX.X,
                                        ALU.add)
            link(ins)
            for j in range(2):
                ins = dve.tensor_tensor(R["slot"][:, j * TILES:j * TILES + TILES],
                                        R["slot"][:, j * TILES:j * TILES + TILES], token[:, :, 2], ALU.add)
            link(ins)
            n2 = 2 * TILES
            link(dve.tensor_tensor(R["ge"], io_pair.unsqueeze(1).broadcast_to([P, n2, PAIRS + 1]),
                                   R["slot"].unsqueeze(2).broadcast_to([P, n2, PAIRS + 1]), ALU.is_le))
            dve.tensor_tensor(R["oh_blk"], R["ge"][:, :, 0:PAIRS], R["ge"][:, :, 1:PAIRS + 1], ALU.subtract)
            link(dve.tensor_reduce(R["nge"], R["ge"], AX.X, ALU.add))
            link(dve.scalar_tensor_tensor(R["slot"], R["nge"], -float(P), R["slot"], ALU.mult, ALU.add))
            link(dve.tensor_scalar(R["slot"], R["slot"], float(P), None, ALU.add))
            dve.tensor_tensor(R["in_block"], R["slot"].unsqueeze(2).broadcast_to([P, n2, P]),
                              io128.unsqueeze(1).broadcast_to([P, n2, P]), ALU.is_equal)
            for j in range(2):
                ohb = R["oh_blk"][:, j * TILES:j * TILES + TILES, :]
                what = R["what"][:, j * TILES:j * TILES + TILES, :]
                tok = token[:, :, 0:1].broadcast_to([P, TILES, PAIRS])
                link(dve.tensor_tensor(what[:, :, 0:PAIRS], ohb, tok, ALU.mult))
                dve.scalar_tensor_tensor(what[:, :, PAIRS:2 * PAIRS], ohb, float(REAL * j), what[:, :, 0:PAIRS],
                                         ALU.mult, ALU.add)
                ins = dve.tensor_tensor(what[:, :, 2 * PAIRS:3 * PAIRS], ohb,
                                        R["w"][:, j, :].unsqueeze(2).broadcast_to([P, TILES, PAIRS]), ALU.mult)
            ins.then_inc(plan_in, 1)
            more = NBLK - NE
            cmp_ = R["tmp"].rearrange("p (b e) -> p b e", e=NE)
            link(dve.tensor_tensor(cmp_, R["cum"].unsqueeze(1).broadcast_to([P, more, NE]),
                                   io128[:, 0:more].unsqueeze(2).broadcast_to([P, more, NE]), ALU.is_le))
            link(dve.tensor_reduce(R["ge"][:, 0, 0:more], cmp_, AX.X, ALU.add))
            link(dve.tensor_scalar(R["ge"][:, 0, 0:more], R["ge"][:, 0, 0:more], float(NE - 1), None, ALU.min))
            dve.tensor_copy(expert_of[:, 0:NE], io_e[0:1, :])
            dve.tensor_copy(expert_of[:, NE:NBLK], R["ge"][0:1, 0, 0:more])
            dve.tensor_scalar(n_blocks[:, 0:1], R["cum"][0:1, NE - 1:NE], float(NE), None, ALU.add)
            dve.wait_ge(plan_done, 1)
            pl3 = acc[:, 0, 0:3 * PAIRS].rearrange("p (a b) -> p a b", b=PAIRS)
            dve.tensor_scalar(R["pl"][:, 0, :], pl3[:, 0, :], -1.0, 0.0, ALU.add, ALU.max)
            link(dve.tensor_scalar(R["pl"][:, 1, :], pl3[:, 1, :], 0.0, 4.0 * NASSIGN, ALU.is_equal, ALU.mult))
            link(dve.tensor_tensor(R["pl"][:, 1, :], pl3[:, 1, :], R["pl"][:, 1, :], ALU.add))
            link(dve.tensor_scalar(R["pl"][:, 1, :], R["pl"][:, 1, :], -1.0, None, ALU.add))
            dve.tensor_copy(gate_of[:, 0:PAIRS], pl3[:, 2, :])
            dve.tensor_copy(src_row[:, 0:PAIRS], R["pl"][:, 0, :])
            dve.tensor_copy(dst_row[:, 0:PAIRS], R["pl"][:, 1, :])
            dve.memset(expert_of[:, NBLK:2 * PAIRS + 2], 0)
            link(dve.memset(src_row[:, PAIRS:PAIRS + 2], 0))
            dve.sem_inc(ya_e, 2)
            dve.sem_inc(yd_e, 2)
            dve.sem_inc(routed, 1)

            n = dve.value_load(n_blocks[0:1, 0:1], min_val=1, max_val=NBLK)

            def halve_weights(q):
                dve.tensor_tensor(elo[:, q % ERING, :], raw_e[:, q, :], ehi[:, q % ERING, :].bitcast(F32),
                                  ALU.subtract).then_inc(lo_e, 1)

            def halve_tokens(s):
                dve.tensor_tensor(xlo[:, 4 * s:4 * s + 4, :], tp[:, s, :].rearrange("p (k r) -> p k r", r=P),
                                  xhi[:, 4 * s:4 * s + 4, :].bitcast(F32), ALU.subtract).then_inc(tlo_e, 1)

            for q in range(2):
                dve.wait_ge(hi_e, q + 1)
                halve_weights(q)
            for g in range(EARLY):
                split_lo(ple_first, g)
            for s in range(2):
                dve.wait_ge(thi_e, s + 1)
                halve_tokens(s)
            for q in range(2, ERING):
                dve.wait_ge(hi_e, q + 1)
                halve_weights(q)
            def pair(i):
                def split(q, next_=0):
                    dve.wait_ge(hi_e, i * EG + (EG * next_ + q + 1))
                    halve_weights(q)

                def turned(s):
                    dve.wait_ge(thi_e, i * 2 + (s + 3))
                    halve_tokens(s)

                def product(b):
                    dve.wait_ge(silu_e, i * 2 + (b + 1))
                    rows = slice(SLOTS * b, SLOTS * b + SLOTS)
                    dve.tensor_tensor(gg[rows, :], acc[rows, b, DE:2 * DE], gg[rows, :], ALU.mult).then_inc(g_e, 1)

                def turned_g():
                    dve.wait_ge(ghi_e, i + 1)
                    dve.tensor_tensor(glo[:, :, :], acc[:, 4, 0:DE].rearrange("p (k r) -> p k r", r=P),
                                      ghi[:, :, :].bitcast(F32), ALU.subtract).then_inc(glo_e, 1)

                def result(b):
                    dve.wait_ge(used_e, i * EG + (2 * b + 10))
                    dve.wait_ge(left_e, i + 1)
                    dve.wait_ge(gate_e, i + 1)
                    rows = slice(SLOTS * b, SLOTS * b + SLOTS)
                    dve.tensor_scalar(ye[rows, 512:D], acc[rows, 3 + 2 * b, :], gate_in[rows, :], None,
                                      ALU.mult).then_inc(yd_e, 1)

                dve.wait_ge(ya_e, i * 2 + 2)
                dve.wait_ge(yd_e, i * 2 + 2)
                dve.tensor_copy(gate_in[:, :], gate_of[:, ds(i, 1)]).then_inc(gate_e, 1)
                steps_of_pair(split, turned, product, turned_g, result, lambda: dve.If(i * 2 + 2 < n))

            each_pair(dve, n, pair)

            dve.wait_ge(ld_g, 32)
            for t in range(TILES + 2):
                if t < TILES:
                    rows = ROWS[t]
                    if t == 0:
                        dve.wait_ge(ld_y[0], 16)
                        link(dve.tensor_tensor(h[0:rows, t, :], h[0:rows, t, :], ysum[0:rows, t, 1, :], ALU.add))
                    else:
                        dve.wait_ge(y_summed, t)
                    dve.tensor_tensor(h[0:rows, t, :], h[0:rows, t, :], ysum[0:rows, t % 3, 0, :],
                                      ALU.add).then_inc(y_added, 1)
                if 1 <= t <= TILES:
                    u = t - 1
                    if u >= 2:
                        dve.wait_ge(t_done, tg[("hp", u - 2, 1)] + 1)
                    dve.wait_ge(f_rstd, u + 1)
                    dve.scalar_tensor_tensor(hp[:, u % 2, :], h[:, u, :], r_f[:, u:u + 1], grow[:, :], ALU.mult,
                                             ALU.mult).then_inc(fn_done, 1)
                if t >= 2:
                    for s in range(2):
                        halve_lo("hp", s, t - 2, 4, lhi2, llo2)
            dve.wait_ge(ld_pj, 16)
            run(ple, EARLY)

        def late_gpsimd(pool, link, inverse_rms):
            pool.memset(ones[:, :], 1.0).then_inc(ones_set, 1)
            for t in range(TILES):
                pool.wait_ge(h_sq, TILES + t + 1)
                link(pool.tensor_tensor(sum_h[:, t:t + 1], ss_h[:, 2 * t:2 * t + 1], ss_h[:, 2 * t + 1:2 * t + 2],
                                        ALU.add))
                inverse_rms(r_h[:, t:t + 1], sum_h[:, t:t + 1], 1, D).then_inc(h_rstd, 1)
                pool.wait_ge(h_rstd, t + 1)
            pool.wait_ge(hn_sent, 16 * TILES)
            for t in range(4):
                pool.wait_ge(pj_sent[t], 32)
            pool.sem_inc(left_e, 1)

            pool.wait_ge(routed, 1)
            n = pool.value_load(n_blocks[0:1, 0:1], min_val=1, max_val=NBLK)
            pool.tensor_copy(row_in[:, :], src_row[:, 0:1]).then_inc(in_e, 1)
            pool.wait_ge(in_e, 1)

            def gather():
                pool.indirect_dma_start(xg[:, 0, :], None, hn_rows,
                                        bass.IndirectOffsetOnAxis(ap=row_in[:, :], axis=0)).then_inc(ld_xg, 16)

            gather()
            pool.wait_ge(ld_xg, 16)
            pool.tensor_copy(row_in[:, :], src_row[:, 1:2]).then_inc(in_e, 1)
            pool.wait_ge(in_e, 2)
            pool.wait_ge(t_e, 2)
            gather()
            def pair(i):
                with pool.If(i * 2 + 4 < n):
                    pool.wait_ge(t_e, i * 2 + 4)
                    pool.wait_ge(ld_xg, i * 16 + 32)
                    pool.sem_inc(pool_steps, 1)
                    pool.tensor_copy(row_in[:, :], src_row[:, ds(i + 2, 1)]).then_inc(in_e, 1)
                    pool.wait_ge(in_e, i + 3)
                    pool.sem_inc(pool_steps, 1)
                    gather()
                pool.tensor_copy(row_out[:, :], dst_row[:, ds(i, 1)]).then_inc(own_e, 1)
                pool.wait_ge(own_e, i + 1)
                pool.wait_ge(ya_e, i * 2 + 4)
                pool.wait_ge(yd_e, i * 2 + 4)
                pool.sem_inc(pool_steps, 1)
                pool.indirect_dma_start(y_rows, bass.IndirectOffsetOnAxis(ap=row_out[:, :], axis=0),
                                        ye, None, bounds_check=NASSIGN - 1,
                                        oob_is_err=False).then_inc(sent_e, 16)
                pool.wait_ge(sent_e, i * 16 + 16)
                pool.sem_inc(left_e, 1)

            each_pair(pool, n, pair)
            steps = (n + 1) // 2
            pool.wait_ge(sent_e, steps * 16)
            pool.sem_inc(moe_done, 1)
            for t in range(TILES + 1):
                if t < TILES:
                    rows = ROWS[t]
                    if t == 0:
                        continue
                    pool.wait_ge(ld_y[t % 3], 16 * (t // 3 + 1))
                    pool.tensor_tensor(ysum[0:rows, t % 3, 0, :], ysum[0:rows, t % 3, 0, :],
                                       ysum[0:rows, t % 3, 1, :], ALU.add).then_inc(y_summed, 1)
                    pool.wait_ge(y_summed, t)
                if t:
                    pool.wait_ge(f_sq, t)
                    inverse_rms(r_f[:, t - 1:t], ss_f[:, t - 1:t], 1, D).then_inc(f_rstd, 1)
                    pool.wait_ge(f_rstd, t)
            for t in range(TILES):
                pool.wait_ge(y_done, y_index[(ple_first + 1, t)] + 1)
                dst = o["y_p"][t * P:t * P + P, :] if t < PT else o["y_s"]
                pool.dma_start(dst, h[0:ROWS[t], t, :]).then_inc(st_y, 16)
            pool.wait_ge(st_y, 16 * TILES)

        block = ctx.enter_context(nc.Block())
        last_first = len(first) - 1
        NCONST = 18
        gv = {"mla_qn": 0, "mla_qr": 1, "mla_kn": 2, "diff_q": 3, "diff_k": 4, "diff_sub": 5}

        def load_granule(sp, i, g):
            c, n = items[i], granules[(i, g)]
            if n >= RAW:
                sp.wait_ge(lo_done, n - RAW + 1)
            src = a[c.src].rearrange("(k p) n -> p k n", p=P)[:, 2 * g:2 * g + 2, c.col:c.col + c.width]
            sp.dma_start(raw[:, n % RAW, :, 0:c.width], src).then_inc(ld_raw[n % RAW], 16)

        @block.sync
        def _(sp):
            for t in range(TILES):
                sp.dma_start(gates[0:ROWS[t], t, 0:D], a["x"][t * P:t * P + ROWS[t], :]).then_inc(ld_x[t], 16)
                if t == 0:
                    sp.dma_start(grow[:, :], a["g_mix"].partition_broadcast(P)).then_inc(ld_start, 16)
                    sp.dma_start(ident[:, :], a["c_ident"]).then_inc(ld_start, 16)
            for g in range(2):
                load_granule(sp, 0, g)
            sp.dma_start(rope[:, :, :], a["c_rope"].rearrange("(t p) n -> p t n", p=P)).then_inc(ld_const, 16)
            sp.dma_start(mask[:, :], a["c_mask"]).then_inc(ld_const, 16)
            sp.dma_start(gq_lat[:, :], a["g_q_lat"].partition_broadcast(P)).then_inc(ld_const, 16)
            sp.dma_start(gkv[:, 0:KVL], a["g_kv_lat"].partition_broadcast(P)).then_inc(ld_const, 16)
            sp.dma_start(gkv[:, KVL:KVL + RD], a["g_mla_kr"].partition_broadcast(P)).then_inc(ld_const, 16)
            for name, j in gv.items():
                g = a["g_" + name]
                sp.dma_start(gvec[:, j, 0:g.shape[-1]], g.partition_broadcast(P)).then_inc(ld_const, 16)
            for j, name in enumerate(("lambda_q1", "lambda_k1", "lambda_q2", "lambda_k2")):
                sp.dma_start(zs[:, 5, 64 * j:64 * j + 64], a[name].partition_broadcast(P)).then_inc(ld_const, 16)
            sp.dma_start(gates[:, 0, D:2 * D], a["cache_k"]).then_inc(ld_const, 16)
            sp.dma_start(gates[:, 1, D:D + KVL], a["cache_ckv"]).then_inc(ld_const, 16)
            sp.dma_start(krope[:, CACHE, :], a["cache_krope"]).then_inc(ld_const, 16)
            every = [(i, g) for i in range(len(first)) for g in range(items[i].kt // 2)][2:]
            for n, (i, g) in enumerate(every):
                load_granule(sp, i, g)
                if n == 2:
                    sp.wait_ge(xn_done, TILES)
                    sp.dma_start(grow[:, :], a["g_ffn"].partition_broadcast(P)).then_inc(ld_g, 16)
            sp.wait_ge(z_done, units[(last_first, TILES - 1)] + 1)
            sp.dma_start(w_uq[:, :, :], a["w_uq"].rearrange("(k p) n -> p k n", p=P)).then_inc(ld_wu, 16)
            sp.dma_start(w_uk[:, :, :], a["w_uk"].rearrange("(k p) n -> p k n", p=P)).then_inc(ld_wu, 16)
            sp.dma_start(w_uv[:, :, :], a["w_uv"].rearrange("(k p) n -> p k n", p=P)).then_inc(ld_wu, 16)
            first_dv = next(i for i, c in enumerate(first) if c.name == "dv")
            for hd in range(H):
                cols = slice(hd * VB, hd * VB + VB)
                if hd >= 2:
                    sp.wait_ge(pv_done["b"], TILES * (hd - 1))
                if hd % (H // 2) == 0:
                    for t in range(TILES):
                        sp.wait_ge(outz[t], 16 * out_count(last_first if hd else first_dv, t))
                s = ld_v[hd % 2]
                sp.dma_start(vh[:, hd % 2, 0:PT, :],
                             o["dv_p"].rearrange("(t p) n -> p t n", p=P)[:, :, cols]).then_inc(s, 16)
                sp.dma_start(vh[0:DEC, hd % 2, PT, :], o["dv_s"][:, cols]).then_inc(s, 16)
                sp.dma_start(vh[:, hd % 2, CACHE, :], a["cache_v"][:, cols]).then_inc(s, 16)
            last_latent = start[id(outp)] - 1
            for t in range(TILES + 1):
                sp.wait_ge(outz[t], 16 * out_count(last_latent, t))
            rest = [(i, g) for i in phase_items(outp) for g in range(items[i].kt // 2)]
            for hd in range(H):
                cols = slice(hd * VB, hd * VB + VB)
                if hd >= 2:
                    sp.wait_ge(pv_done["a"], TILES * (hd - 1))
                else:
                    sp.wait_ge(pv_done["b"], TILES * H)
                sp.dma_start(vh[:, hd % 2, :, :],
                             va_rows.rearrange("(t p) n -> p t n", p=P)[:, :, cols]).then_inc(ld_v[hd % 2], 16)
                if hd == 1:
                    for i, g in rest[:RAW]:
                        load_granule(sp, i, g)
            sp.wait_ge(s_done["a"], H * TILES)
            for t in range(TILES):
                sp.dma_start(ptok[0:ROWS[t], t, :], a["p"][t * P:t * P + ROWS[t], :]).then_inc(ld_p, 16)
            sp.wait_ge(t_copied, copied[("merged", TILE_ORDER[-1], 1)] + 1)
            for t in range(TILES):
                sp.dma_start(h[0:ROWS[t], t, :], a["x"][t * P:t * P + ROWS[t], :]).then_inc(ld_h, 16)
            for i, g in rest[RAW:]:
                load_granule(sp, i, g)
            late_sync(sp)

        def key_tiles(t):
            if t < PT:
                return [(j, P, j * P) for j in range(t + 1)]
            return [(CACHE, PAST, SEQ), (PT, DEC, SEQ + PAST)]

        @block.tensor
        def _(pe):
            pe.wait_ge(ld_start, 32)

            def turn(key, blocks, rows=P, cols=P, pitch=P):
                wait_bank_for(pe, key)
                bank = tg[key] % 2
                for j, src in enumerate(blocks):
                    last = pe.transpose(tp[0:cols, bank, j * P:j * P + rows], src, ident[0:rows, 0:rows])
                last.then_inc(t_done, 1)

            def multiply(i, between):
                c = items[i]
                lo_name = {"act": {0: "x", 2: "merged", 3: "hp"}.get(
                    next(n for n, ph in enumerate(phases) if c in ph)), "pe": "pe"}.get(c.lhs)
                steps = c.kt // 2 if c.split else 1
                for g in range(steps):
                    if c.split:
                        pe.wait_ge(lo_done, granules[(i, g)] + 1)
                    for t in range(c.tiles):
                        bank = acc[:, t, 0:c.width]
                        rows = slice(t * P, t * P + P)
                        if g == 0:
                            if lo_name:
                                wait_group_copied(pe, (lo_name, t, 0 if lo_name == "pe" else 1))
                            before = [n for n in range(i) if items[n].tiles > t]
                            if before:
                                pe.wait_ge(z_copied, units[(before[-1], t)] + 1)
                        if c.split:
                            for k in range(2):
                                n = granules[(i, g)] % RING
                                kk = 2 * g + k
                                L, W = {"x": (lhi, llo), "pe": (phi, plo)}.get(lo_name, (lhi2, llo2)), (whi, wlo)
                                for x, w in ((0, 0), (0, 1), (1, 0)):
                                    mm = pe.matmul(bank, L[x][:, kk, rows], W[w][:, n, k, 0:c.width],
                                                   start=(kk == 0 and x + w == 0),
                                                   stop=(kk == c.kt - 1 and x == 1))
                        else:
                            L = {"q_lat": q_latT, "ckv": ckvT}[c.lhs]
                            W = {"w_uq": w_uq, "w_uk": w_uk, "w_uv": w_uv}[c.src]
                            for k in range(c.kt):
                                mm = pe.matmul(bank, L[:, k, rows], W[:, k, c.col:c.col + c.width],
                                               start=(k == 0), stop=(k == c.kt - 1))
                        if g == steps - 1:
                            mm.then_inc(z_done, 1)
                    if c.split and g < steps - 1:
                        mm.then_inc(w_used, 1)
                    between(g)

            def transposes(i, tiles=range(TILES + 1)):
                c = items[i]
                if c.kind != "norm":
                    return
                for t in tiles:
                    if t >= c.tiles:
                        continue
                    pe.wait_ge(y_done, y_index[(i, t)] + 1)
                    z = zs[:, t, :]
                    if c.name == "uq":
                        turn((i, t, 0), [z[:, j * HD:j * HD + HD] for j in range(4)], cols=HD)
                    elif c.name == "uk":
                        for s in range(2):
                            turn((i, t, s), [kas(t)[:, j * HD:j * HD + HD] for j in range(4 * s, 4 * s + 4)], cols=HD)
                    else:
                        n = {"q_lat": 3, "ckv": 2}.get(c.name, 4)
                        turn((i, t, 0), [z[:, j * P:j * P + P] for j in range(n)])

            def turn_cache():
                pe.wait_ge(ld_const, 16 * NCONST)
                for s in range(2):
                    turn(("cache_k", 0, s), [gates[:, 0, D + j * P:D + j * P + P] for j in range(4 * s, 4 * s + 4)])
                turn(("cache_ckv", 0, 0), [gates[:, 1, D + j * P:D + j * P + P] for j in range(2)])

            def run(ph):
                ids = phase_items(ph)
                for i in ids:
                    def between(g):
                        if i - 2 in ids and deferred(i - 2):
                            if items[i].split:
                                transposes(i - 2, DEFERRED[g])
                            else:
                                transposes(i - 2)

                    multiply(i, between)
                    if i == 0:
                        turn_cache()
                    if i - 1 in ids and not deferred(i - 1):
                        transposes(i - 1)
                if ids[-1] != last_uq:
                    transposes(ids[-1])

            def attention(ph, maps):
                name = "attn_" + ph

                def scores(n):
                    hd, t = unit(n)
                    if ph == "a" and n == n_units // 2:
                        pe.wait_ge(t_copied, copied[(last_uq, TILES - 1, 0)] + 1)
                    kt_ = key_tiles(t)
                    k0, nk = kt_[0][2], sum(r for _, r, _ in kt_)
                    if n >= bank_uses(ph):
                        pe.wait_ge(exp_done[ph], maps * (n + 1 - bank_uses(ph)))
                    if ph == "b":
                        pe.wait_ge(qz_done, n + 1)
                    for c in range(maps):
                        bank = score_bank(ph, n, c)
                        lhs = qz[:, n % QZ, c, 0:ROWS[t]] if ph == "b" else qT[:, hd, t * P:t * P + ROWS[t]]
                        mm = pe.matmul(acc[0:ROWS[t], bank, 0:nk], lhs, kT[:, hd, k0:k0 + nk],
                                       start=True, stop=(t == PT))
                        if t < PT:
                            mm = pe.matmul(acc[:, bank, nk - CHUNK:nk], mask[:, 0:P], mask[:, P:P + CHUNK],
                                           start=False, stop=True)
                    mm.then_inc(s_done[ph], 1)

                def turn_probs(n):
                    hd, t = unit(n)
                    if ph == "b":
                        pe.wait_ge(comb_done[ph], n + 1)
                    else:
                        pe.wait_ge(exp_done[ph], n + 1)
                    wait_bank_for(pe, (name, n, 0))
                    bank = tg[(name, n, 0)] % 2
                    at = 0
                    for j, (_, nk, _) in enumerate(key_tiles(t)):
                        last = pe.transpose(tp[0:nk, bank, j * P:j * P + ROWS[t]],
                                            probs(ph, n, 0)[0:ROWS[t], at:at + nk], ident[0:ROWS[t], 0:ROWS[t]])
                        at += nk
                    last.then_inc(t_done, 1)

                def values(n):
                    hd, t = unit(n)
                    pe.wait_ge(pt_copied, pt[(name, n, 0)] + 1)
                    if n % TILES == 0:
                        pe.wait_ge(ld_v[hd % 2], 48 * (hd // 2 + 1) if ph == "b" else 48 * 4 + 16 * (hd // 2 + 1))
                    if n >= 2:
                        pe.wait_ge(o_done[ph], n - 1)
                        if ph == "b":
                            pe.wait_ge(sqo_done, n - 1)
                    kt_ = key_tiles(t)
                    for j, (slot, nk, _) in enumerate(kt_):
                        mm = pe.matmul(acc[0:ROWS[t], 4 + n % 2, 0:VB], prT[0:nk, n % 2, j, 0:ROWS[t]],
                                       vh[0:nk, hd % 2, slot, :], start=(j == 0), stop=(j == len(kt_) - 1))
                    mm.then_inc(pv_done[ph], 1)

                n_units = H * TILES
                lag = LAG[ph]
                for n in range(n_units + lag + 1):
                    if n < n_units:
                        scores(n)
                    if lag <= n < n_units + lag:
                        turn_probs(n - lag)
                    if ph == "a" and n in TURN_AT:
                        transposes(last_uq, [TURN_AT[n]])
                    if n > lag:
                        values(n - lag - 1)

            for t in range(TILES):
                pe.wait_ge(xn_done, t + 1)
                for s in range(2):
                    turn(("x", t, s), [gates[:, t, j * P:j * P + P] for j in range(4 * s, 4 * s + 4)])
            run(first)
            pe.wait_ge(z_copied, units[(last_first, TILES - 1)] + 1)
            pe.wait_ge(t_copied, copied[(last_norm(first), TILES - 1, 0)] + 1)
            attention("b", 2)
            pe.wait_ge(exp_done["b"], 2 * H * TILES)
            pe.wait_ge(o_done["b"], H * TILES)
            pe.wait_ge(sqo_done, H * TILES)
            pe.wait_ge(ld_wu, 48)
            run(latent)
            pe.wait_ge(z_copied, units[(start[id(outp)] - 1, TILES - 1)] + 1)
            pe.wait_ge(t_copied, copied[(last_uq - 2, TILES - 1, 0)] + 1)
            pe.wait_ge(q_zeroed, 1)
            attention("a", 1)
            pe.wait_ge(exp_done["a"], H * TILES)
            pe.wait_ge(o_done["a"], H * TILES)
            for k, t in enumerate(TILE_ORDER):
                pe.wait_ge(merged_done, k + 1)
                for s in range(2):
                    turn(("merged", t, s), [gates[:, t, j * P:j * P + P] for j in range(4 * s, 4 * s + 4)])
            pe.wait_ge(ld_p, 16 * TILES)
            pe.wait_ge(zeroed, 3)
            for t in range(TILES):
                turn(("pe", t, 0), [ptok[:, t, j * P:j * P + P] for j in range(2)])
            run(outp)
            late_tensor(pe, turn, run)

        @block.scalar
        def _(act):
            own = [0]

            def link(ins):
                own[0] += 1
                ins.then_inc(act_own, 1)
                act.wait_ge(act_own, own[0])

            def split_hi(i, g):
                c, n = items[i], granules[(i, g)]
                act.wait_ge(ld_raw[n % RAW], 16 * (n // RAW + 1))
                wait_ring_free(act, n)
                act.activation(whi[:, n % RING, :, 0:c.width], raw[:, n % RAW, :, 0:c.width],
                               ACT.Copy).then_inc(hi_done, 1)

            def copy_out(i, tiles=range(TILES + 1)):
                c = items[i]
                for t in tiles:
                    if t >= c.tiles:
                        continue
                    act.wait_ge(z_done, units[(i, t)] + 1)
                    src = acc[:, t, 0:c.width]
                    if uses_zs(i):
                        wait_slot_free(act, i, t)
                        func = ACT.Sigmoid if c.kind == "ple" else ACT.Copy
                        act.activation(zs[:, t, 0:c.width], src, func).then_inc(z_copied, 1)
                    elif c.name == "uv":
                        act.wait_ge(outz[t], 16 * out_count(i - 1, t))
                        act.activation(uv_tile(t), src, ACT.Copy).then_inc(z_copied, 1)
                    elif c.kind == "gate":
                        at = (0 if c.name == "ga" else D) + 512 * c.half
                        act.activation(gates[:, t, at:at + 512], src, ACT.Sigmoid).then_inc(z_copied, 1)
                    else:
                        act.activation(embed_tile(1, t), src, ACT.Copy).then_inc(z_copied, 1)

            def squares(i):
                c = items[i]
                if c.kind != "norm":
                    return
                for t in range(c.tiles):
                    act.wait_ge(z_copied, units[(i, t)] + 1)
                    if y_norm[(i, t)] >= 1:
                        act.wait_ge(ss_done, y_norm[(i, t)])
                    act.activation(sq[:, 0:c.width], zs[:, t, 0:c.width], ACT.Square).then_inc(sq_done, 1)

            def square_residual(i, t):
                n, half = y_index[(i, t)], items[i].half
                act.wait_ge(y_done, n + 1)
                if t or half:
                    act.wait_ge(h_sq, TILES * half + t)
                act.activation(sq[:, :], h[:, t, 512 * half:512 * half + 512], ACT.Square,
                               accum_out=ss_h[:, 2 * t + half:2 * t + half + 1]).then_inc(h_sq, 1)

            def run(ph, halved=0):
                ids = list(phase_items(ph))
                for i in ids + [ids[-1] + 1]:
                    steps = items[i].kt // 2 if i in ids and items[i].split else 0
                    done = halved if i == ids[0] else 0
                    if steps > 0 >= done:
                        split_hi(i, 0)
                    if i - 1 == residual_last and i - 1 in ids:
                        for t in range(TILES + 1):
                            copy_out(i - 1, [t])
                            if t:
                                square_residual(i - 1, t - 1)
                        continue
                    if i - 1 in ids:
                        copy_out(i - 1)
                    if steps > 1 >= done:
                        split_hi(i, 1)
                    if i - 1 in ids:
                        squares(i - 1)
                    for g in range(2, steps):
                        split_hi(i, g)
                    if i - 1 == start[id(outp)] and i in ids:
                        act.wait_ge(ss_done, y_norm_of_phase(latent))
                        for t in range(TILES):
                            square_residual(i - 1, t)

            def halve_hi(name, s, t, n, hi):
                act.wait_ge(t_done, tg[(name, t, s)] + 1)
                act.activation(hi[:, 4 * s:4 * s + n, t * P:t * P + P],
                               tp[:, tg[(name, t, s)] % 2, 0:n * P].rearrange("p (k r) -> p k r", r=P),
                               ACT.Copy).then_inc(hi_copied, 1)

            for t in range(TILES + 3):
                if t < TILES:
                    act.wait_ge(ld_x[t], 16)
                    if t == 0:
                        act.wait_ge(zeroed, 1)
                    if t:
                        act.wait_ge(x_sq, t)
                    act.activation(zs[:, 0:2, :].rearrange("p a b -> p (a b)"), gates[:, t, 0:D], ACT.Square,
                                   accum_out=ss_x[:, t:t + 1]).then_inc(x_sq, 1)
                if t >= 3:
                    for s in range(2):
                        halve_hi("x", s, t - 3, 4, lhi)
            act.wait_ge(lam_dots, 2)
            act.activation(lamv[:, 2:4], lamv[:, 0:2], ACT.Exp).then_inc(lam_exp, 1)
            run(first)

            def attention(ph, maps):
                name = "attn_" + ph
                n_units = H * TILES

                def exps(n):
                    hd, t = unit(n)
                    rows, nk = ROWS[t], sum(r for _, r, _ in key_tiles(t))
                    act.wait_ge(nm_done[ph], n + 1)
                    if n >= prob_slots(ph):
                        act.wait_ge(t_done, tg[(name, n - prob_slots(ph), 0)] + 1)
                    for c in range(maps):
                        b = score_bank(ph, n, c)
                        act.activation(probs(ph, n, c)[0:rows, 0:nk], acc[0:rows, b, 0:nk], ACT.Exp,
                                       bias=negmax[0:rows, b:b + 1], accum_out=sums[0:rows, b:b + 1]
                                       ).then_inc(exp_done[ph], 1)

                def copy_turned(n):
                    hd, t = unit(n)
                    rows, bank = ROWS[t], tg[(name, n, 0)] % 2
                    act.wait_ge(t_done, tg[(name, n, 0)] + 1)
                    if n >= 2:
                        act.wait_ge(pv_done[ph], n - 1)
                    if t < PT:
                        act.activation(prT[:, n % 2, 0:t + 1, :],
                                       tp[:, bank, 0:(t + 1) * P].rearrange("p (k r) -> p k r", r=P),
                                       ACT.Copy).then_inc(pt_copied, 1)
                    else:
                        act.activation(prT[:, n % 2, 0, 0:rows], tp[:, bank, 0:rows], ACT.Copy)
                        act.activation(prT[0:DEC, n % 2, 1, 0:rows], tp[0:DEC, bank, P:P + rows],
                                       ACT.Copy).then_inc(pt_copied, 1)

                def square_out(n):
                    hd, t = unit(n)
                    rows = ROWS[t]
                    act.wait_ge(pv_done[ph], n + 1)
                    if n:
                        act.wait_ge(sqo_done, n)
                    act.activation(sq[0:rows, 0:VB], acc[0:rows, 4 + n % 2, 0:VB], ACT.Square,
                                   accum_out=ss_o[0:rows, t * H + hd:t * H + hd + 1]).then_inc(sqo_done, 1)

                lag = LAG[ph]
                for n in range(n_units + lag + 1):
                    if lag <= n < n_units + lag:
                        copy_turned(n - lag)
                    if n > lag and ph == "b":
                        square_out(n - lag - 1)
                    if n < n_units:
                        exps(n)

            act.wait_ge(ss_done, y_norm_of_phase(first))
            attention("b", 2)
            act.wait_ge(sqo_done, H * TILES)
            act.wait_ge(t_done, tg[("attn_b", H * TILES - 1, 0)] + 1)
            run(latent)
            act.wait_ge(t_done, tg[(start[id(latent)], TILES, 1)] + 1)
            attention("a", 1)
            for t in TILE_ORDER:
                for s in range(2):
                    halve_hi("merged", s, t, 4, lhi2)
            for t in range(TILES):
                halve_hi("pe", 0, t, 2, phi)
            run(outp)
            late_scalar(act, link, halve_hi, split_hi, run)

        @block.vector
        def _(dve):
            own = [0]

            def link(ins):
                own[0] += 1
                ins.then_inc(dve_own, 1)
                dve.wait_ge(dve_own, own[0])

            def split_lo(i, g):
                c, n = items[i], granules[(i, g)]
                dve.wait_ge(hi_done, n + 1)
                dve.tensor_tensor(wlo[:, n % RING, :, 0:c.width], raw[:, n % RAW, :, 0:c.width],
                                  whi[:, n % RING, :, 0:c.width].bitcast(F32), ALU.subtract).then_inc(lo_done, 1)

            def halve_lo(name, s, t, n, hi, lo):
                dve.wait_ge(hi_copied, hi_index[(name, t, s)] + 1)
                cols = (slice(4 * s, 4 * s + n), slice(t * P, t * P + P))
                dve.tensor_tensor(lo[:, cols[0], cols[1]],
                                  tp[:, tg[(name, t, s)] % 2, 0:n * P].rearrange("p (k r) -> p k r", r=P),
                                  hi[:, cols[0], cols[1]].bitcast(F32), ALU.subtract).then_inc(t_copied, 1)

            def copy_group(key, dst, rows, n, width):
                dve.wait_ge(t_done, tg[key] + 1)
                src = tp[0:rows, tg[key] % 2, 0:n * P].rearrange("p (k r) -> p k r", r=P)[:, :, 0:width]
                dve.tensor_copy(dst, src).then_inc(t_copied, 1)

            def copy_turned(i, tiles=range(TILES + 1)):
                c = items[i]
                if c.kind != "norm":
                    return
                for t in tiles:
                    if t >= c.tiles:
                        continue
                    q = slice(t * P, t * P + ROWS[t]) if t < TILES else None
                    k = slice(KCOL[t], KCOL[t] + (ROWS[t] if t < TILES else P))
                    hs = slice(4 * c.half, 4 * c.half + 4)
                    if c.name == "q_lat":
                        copy_group((i, t, 0), q_latT[:, :, t * P:t * P + P], P, 3, P)
                    elif c.name == "ckv":
                        copy_group((i, t, 0), ckvT[:, :, t * P:t * P + P], P, 2, P)
                    elif c.name == "dq":
                        copy_group((i, t, 0), qT[:, hs, q], P, 4, ROWS[t])
                    elif c.name == "dk":
                        copy_group((i, t, 0), kT[:, hs, k], P, 4, ROWS[t])
                    elif c.name == "uq":
                        copy_group((i, t, 0), qT[0:HD, hs, q], HD, 4, ROWS[t])
                    else:
                        for s in range(2):
                            copy_group((i, t, s), kT[0:HD, 4 * s:4 * s + 4, k], HD, 4, ROWS[t] if t < TILES else P)

            def sums_of(i):
                c = items[i]
                if c.kind != "norm":
                    return
                gs = groups(i)
                total = sum(g[1] for g in gs)
                m = normitems[i]
                if m >= 2:
                    old = list(normitems)[m - 2]
                    dve.wait_ge(rstd_done, y_norm[(old, items[old].tiles - 1)] + 1)
                for t in range(c.tiles):
                    dve.wait_ge(sq_done, y_norm[(i, t)] + 1)
                    at = t * total
                    for n, g in enumerate(gs):
                        ins = dve.tensor_reduce(ss_z[m % 2][:, at:at + g[1]], grouped(sq[:, :], g), AX.X, ALU.add)
                        at += g[1]
                    ins.then_inc(ss_done, 1)

            def rotate(t, z, n, half):
                table = 0 if half == RD // 2 else 2 * RD
                cc = rope[:, t, table:table + 2 * half].unsqueeze(1).broadcast_to([P, n, 2 * half])
                ss = rope[:, t, table + 2 * half:table + 4 * half].unsqueeze(1).broadcast_to([P, n, 2 * half])
                r = [rot[:, j, 0:n * 2 * half].rearrange("p (n s) -> p n s", n=n) for j in range(2)]
                dve.tensor_tensor(r[0], z, cc, ALU.mult)
                dve.tensor_tensor(r[1][:, :, 0:half], z[:, :, half:2 * half], ss[:, :, 0:half], ALU.mult)
                link(dve.tensor_tensor(r[1][:, :, half:2 * half], z[:, :, 0:half], ss[:, :, half:2 * half], ALU.mult))
                return dve.tensor_tensor(z, r[0], r[1], ALU.add)

            def normalise(i, tiles):
                c = items[i]
                if c.kind != "norm":
                    return
                gs = groups(i)
                total = sum(g[1] for g in gs)
                m = normitems[i]
                for t in tiles:
                    dve.wait_ge(rstd_done, y_norm[(i, t)] + 1)
                    z = zs[:, t, :]
                    r = r_z[m % 2][:, t * total:t * total + total]
                    if c.name in ("q_lat", "ckv"):
                        gain = {"q_lat": gq_lat, "ckv": gkv}[c.name]
                        for n, (off, _, size, _, _) in enumerate(gs):
                            ins = dve.scalar_tensor_tensor(z[:, off:off + size], z[:, off:off + size], r[:, n:n + 1],
                                                           gain[:, off:off + size], ALU.mult, ALU.mult)
                        if c.name == "ckv":
                            link(ins)
                            link(rotate(t, z[:, KVL:KVL + RD].unsqueeze(1), 1, RD // 2))
                            ins = dve.tensor_copy(krope[:, t, :], z[:, KVL:KVL + RD])
                        ins.then_inc(y_done, 1)
                        continue
                    names = {"dq": ["diff_q"], "dk": ["diff_k"], "uq": ["mla_qn", "mla_qr"], "uk": ["mla_kn"]}[c.name]
                    at = 0
                    for g, nm in zip(gs, names):
                        ins = dve.tensor_tensor(grouped(z, g), grouped(z, g),
                                                r[:, at:at + g[1]].unsqueeze(2).broadcast_to([P, g[1], g[2]]), ALU.mult)
                        at += g[1]
                    link(ins)
                    if c.name == "uk":
                        keys = kas(t).rearrange("p (h s) -> p h s", s=HD)
                    for g, nm in zip(gs, names):
                        dst = grouped(z, g) if c.name != "uk" else keys[:, :, 0:NOPE]
                        ins = dve.tensor_tensor(dst, grouped(z, g),
                                                gvec[:, gv[nm], 0:g[2]].unsqueeze(1).broadcast_to([P, g[1], g[2]]),
                                                ALU.mult)
                    if c.name == "uk":
                        ins = dve.tensor_copy(keys[:, :, NOPE:HD],
                                              krope[:, t, :].unsqueeze(1).broadcast_to([P, H, RD]))
                    elif c.name == "uq":
                        link(ins)
                        ins = rotate(t, grouped(z, gs[1]), 4, RD // 2)
                    else:
                        link(ins)
                        ins = rotate(t, z.rearrange("p (n s) -> p n s", s=DB)[:, :, 0:ROT], 8, ROT // 2)
                    ins.then_inc(y_done, 1)

            def add_residual(i, t):
                if (i, t) == (start[id(outp)], 0):
                    dve.wait_ge(ld_h, 16 * TILES)
                    dve.wait_ge(zeroed, 3)
                dve.wait_ge(z_copied, units[(i, t)] + 1)
                hh = h[:, t, 512 * items[i].half:512 * items[i].half + 512]
                dve.tensor_tensor(hh, hh, zs[:, t, :], ALU.add).then_inc(y_done, 1)

            def normalise_h():
                dve.wait_ge(ld_g, 16)
                for t in range(TILES + 2):
                    if t < TILES:
                        add_residual(residual_last, t)
                    if t >= 2:
                        dve.wait_ge(h_rstd, t - 1)
                        dve.scalar_tensor_tensor(xn[:, t - 2, :], h[:, t - 2, :], r_h[:, t - 2:t - 1], grow[:, :],
                                                 ALU.mult, ALU.mult).then_inc(hn_done, 1)

            def finish(i, tiles):
                c = items[i]
                normalise(i, tiles)
                if c.kind == "residual" and i != residual_last:
                    for t in tiles:
                        add_residual(i, t)
                if c.kind == "ple":
                    for t in tiles:
                        cols = slice(512 * c.half, 512 * c.half + 512)
                        dve.wait_ge(z_copied, units[(i, t)] + 1)
                        link(dve.tensor_tensor(pj[:, t, cols], pj[:, t, cols], zs[:, t, :], ALU.mult))
                        dve.tensor_tensor(h[:, t, cols], h[:, t, cols], pj[:, t, cols], ALU.add).then_inc(y_done, 1)

            def run(ph, halved=0):
                ids = list(phase_items(ph))
                for i in ids + [ids[-1] + 1, ids[-1] + 2]:
                    done = halved if i == ids[0] else 0
                    steps = items[i].kt // 2 if i in ids and items[i].split else 0
                    spread = steps == 4 and i - 2 in ids and deferred(i - 2)
                    n = items[i - 1].tiles if i - 1 in ids and i - 1 != last_uq else 0
                    if steps > 0 >= done:
                        split_lo(i, 0)
                    if i - 1 == residual_last and i in ids:
                        normalise_h()
                    if i == 1:
                        first_extras()
                    if i - 2 in ids and not spread and i - 2 != last_uq:
                        copy_turned(i - 2)
                    if steps > 1 >= done:
                        split_lo(i, 1)
                    if spread:
                        copy_turned(i - 2, DEFERRED[0])
                    if i - 1 in ids:
                        sums_of(i - 1)
                    if steps > 2:
                        split_lo(i, 2)
                    if spread:
                        copy_turned(i - 2, DEFERRED[1])
                    if n:
                        finish(i - 1, range(0, n // 2 + 1))
                    if steps > 3:
                        split_lo(i, 3)
                    if spread:
                        copy_turned(i - 2, DEFERRED[2])
                    if n:
                        finish(i - 1, range(n // 2 + 1, n))

            dve.wait_ge(zeroed, 1)
            dve.wait_ge(ld_start, 32)
            for t in range(TILES + 1):
                if t < TILES:
                    dve.wait_ge(x_rstd, t + 1)
                    dve.scalar_tensor_tensor(gates[:, t, 0:D], gates[:, t, 0:D], r_x[:, t:t + 1], grow[:, :],
                                             ALU.mult, ALU.mult).then_inc(xn_done, 1)
                if t >= 1:
                    for s in range(2):
                        halve_lo("x", s, t - 1, 4, lhi, llo)
            dve.wait_ge(ld_const, 16 * NCONST)
            lq = zs[:, 5, :]
            for j in range(2):
                dve.tensor_tensor_reduce(rot[:, j, 0:64], lq[:, 128 * j:128 * j + 64], lq[:, 128 * j + 64:128 * j + 128],
                                         1.0, 0.0, ALU.mult, ALU.add, lamv[:, j:j + 1]).then_inc(lam_dots, 1)

            def first_extras():
                for s in range(2):
                    copy_group(("cache_k", 0, s), kT[:, 4 * s:4 * s + 4, SEQ:SEQ + PAST], P, 4, P)
                copy_group(("cache_ckv", 0, 0), ckvT[:, :, TOK:TOK + P], P, 2, P)
                dve.wait_ge(lam_exp, 1)
                link(dve.tensor_tensor(lamv[:, 4:5], lamv[:, 3:4], lamv[:, 2:3], ALU.subtract))
                dve.tensor_scalar(pair[:, 1:2], lamv[:, 4:5], -LAM_INIT, None, ALU.add)
                dve.tensor_scalar(pair[:, 0:1], lamv[:, 4:5], 0.0, 1.0, ALU.mult, ALU.add)
                link(dve.tensor_scalar(gvec[:, gv["diff_sub"], :], gvec[:, gv["diff_sub"], :], 1.0 - LAM_INIT, None,
                                       ALU.mult))

            run(first)

            def last_queries(n):
                if n in NORM_AT:
                    normalise(last_uq, [NORM_AT[n]])
                if n - 1 in TURN_AT:
                    copy_turned(last_uq, [TURN_AT[n - 1]])

            def attention(ph, maps):
                n_units = H * TILES

                def maxima(n):
                    hd, t = unit(n)
                    rows, nk, b = ROWS[t], sum(r for _, r, _ in key_tiles(t)), score_bank(ph, n, 0)
                    dve.wait_ge(s_done[ph], n + 1)
                    if n >= bank_uses(ph):
                        dve.wait_ge(exp_done[ph], maps * (n + 1 - bank_uses(ph)))
                    dve.tensor_reduce(negmax[0:rows, b:b + maps], acc[0:rows, b:b + maps, 0:nk], AX.X, ALU.max,
                                      negate=True).then_inc(nm_done[ph], 1)

                def combine(n):
                    hd, t = unit(n)
                    rows, nk, b = ROWS[t], sum(r for _, r, _ in key_tiles(t)), score_bank(ph, n, 0)
                    q = 2 * (n % RSUM)
                    dve.wait_ge(exp_done[ph], maps * (n + 1))
                    rr = rsum[0:rows, q:q + maps]
                    ins = dve.reciprocal(rr, sums[0:rows, b:b + maps])
                    if ph == "a":
                        ins.then_inc(comb_done[ph], 1)
                        return
                    link(ins)
                    link(dve.tensor_tensor(rr, rr, pair[0:rows, :], ALU.mult))
                    p0, p1 = probs(ph, n, 0)[0:rows, 0:nk], probs(ph, n, 1)[0:rows, 0:nk]
                    link(dve.tensor_scalar(p1, p1, rsum[0:rows, q + 1:q + 2], None, ALU.mult))
                    dve.scalar_tensor_tensor(p0, p0, rsum[0:rows, q:q + 1], p1, ALU.mult,
                                             ALU.add).then_inc(comb_done[ph], 1)

                def merge(n):
                    t = unit(n)[1]
                    dve.wait_ge(o_done["a"], n + 1)
                    dve.wait_ge(sub_done, t + 1)
                    dve.tensor_tensor(gates[:, t, 0:D], gates[:, t, 0:D], gates[:, t, D:2 * D],
                                      ALU.add).then_inc(merged_done, 1)

                def gate_out(n):
                    hd, t = unit(n)
                    rows = ROWS[t]
                    dve.wait_ge(pv_done[ph], n + 1)
                    out = acc[0:rows, 4 + n % 2, 0:VB]
                    if ph == "b":
                        dve.wait_ge(sqo_done, n + 1)
                        g = gates[0:rows, t, D + hd * VB:D + hd * VB + VB]
                        dve.tensor_tensor(g, out, g, ALU.mult).then_inc(o_done[ph], 1)
                    else:
                        g = gates[0:rows, t, hd * VB:hd * VB + VB]
                        dve.wait_ge(comb_done[ph], n + 1)
                        dve.scalar_tensor_tensor(g, out, rsum[0:rows, 2 * (n % RSUM):2 * (n % RSUM) + 1], g, ALU.mult,
                                                 ALU.mult).then_inc(o_done[ph], 1)

                lag = LAG[ph]
                for n in range(n_units + lag + 1):
                    if n < n_units:
                        maxima(n)
                    if 1 <= n <= n_units:
                        combine(n - 1)
                    if n > lag:
                        gate_out(n - lag - 1)
                        if ph == "a" and n - lag - 1 >= n_units - TILES:
                            merge(n - lag - 1)
                    if ph == "a":
                        last_queries(n)

            attention("b", 2)
            run(latent)
            attention("a", 1)
            for t in TILE_ORDER:
                for s in range(2):
                    halve_lo("merged", s, t, 4, lhi2, llo2)
            for t in range(TILES):
                halve_lo("pe", 0, t, 2, phi, plo)
            run(outp)
            late_vector(dve, link, halve_lo, split_lo, run)

        @block.gpsimd
        def _(pool):
            own = [0]

            def link(ins):
                own[0] += 1
                ins.then_inc(pool_own, 1)
                pool.wait_ge(pool_own, own[0])

            def inverse_rms(dst, src, n, size, eps_scale=1.0):
                f = eps_scale
                link(pool.tensor_scalar(src, src, 1.0 / (size * f), EPS / f, ALU.mult, ALU.add))
                return pool.tensor_tensor(dst, src, neghalf[:, 0:n], ALU.pow)

            link(pool.memset(small[:, :], 0.0))
            link(pool.memset(neghalf[:, :], -0.5))
            link(pool.memset(qz[:, :, :, :], 0.0))
            pool.memset(gates[DEC:P, PT, 0:D], 0.0).then_inc(zeroed, 1)
            pool.wait_ge(zeroed, 1)

            for t in range(TILES):
                pool.wait_ge(x_sq, t + 1)
                inverse_rms(r_x[:, t:t + 1], ss_x[:, t:t + 1], 1, D).then_inc(x_rstd, 1)
                pool.wait_ge(x_rstd, t + 1)

            def factors(i):
                c, gs, m = items[i], groups(i), normitems[i]
                total = sum(g[1] for g in gs)
                if m >= 2:
                    before = list(normitems)[m - 2]
                    pool.wait_ge(y_done, y_index[(before, items[before].tiles - 1)] + 1)
                for t in range(c.tiles):
                    pool.wait_ge(ss_done, y_norm[(i, t)] + 1)
                    at = t * total
                    for off, k, size, _, f in gs:
                        part_ = ss_z[m % 2][:, at:at + k]
                        link(pool.tensor_scalar(part_, part_, 1.0 / (size * f), EPS / f, ALU.mult, ALU.add))
                        at += k
                    n = slice(t * total, t * total + total)
                    pool.tensor_tensor(r_z[m % 2][:, n], ss_z[m % 2][:, n], neghalf[:, 0:total],
                                       ALU.pow).then_inc(rstd_done, 1)
                    pool.wait_ge(rstd_done, y_norm[(i, t)] + 1)

            def send(i):
                c = items[i]
                if not dmas_of(i):
                    return
                for t in range(c.tiles):
                    if c.kind == "norm":
                        pool.wait_ge(y_done, y_index[(i, t)] + 1)
                    else:
                        pool.wait_ge(z_copied, units[(i, t)] + 1)
                    cols = slice(512 * c.half, 512 * c.half + 512)
                    if c.name == "uv":
                        pool.dma_start(va_rows[t * P:t * P + P, cols], uv_tile(t)).then_inc(outz[t], 16)
                        continue
                    rows = slice(t * P, t * P + P) if t < PT else slice(0, DEC)
                    who = "_p" if t < PT else "_s"
                    if c.name == "ckv":
                        pool.dma_start(o["ckv" + who][rows, :], zs[0:ROWS[t], t, 0:KVL]).then_inc(outz[t], 16)
                        pool.dma_start(o["kr" + who][rows, :], zs[0:ROWS[t], t, KVL:KVL + RD]).then_inc(outz[t], 16)
                    else:
                        pool.dma_start(o[c.name + who][rows, cols], zs[0:ROWS[t], t, :]).then_inc(outz[t], 16)

            for i in phase_items(first):
                if items[i].kind == "norm":
                    factors(i)
                send(i)
            pool.wait_ge(t_copied, copied[(last_norm(first), TILES - 1, 0)] + 1)
            for n in range(H * TILES):
                hd, t = unit(n)
                if n >= QZ:
                    pool.wait_ge(s_done["b"], n - QZ + 1)
                q = slice(t * P, t * P + ROWS[t])
                link(pool.tensor_copy(qz[0:DB, n % QZ, 0, 0:ROWS[t]], qT[0:DB, hd, q]))
                pool.tensor_copy(qz[DB:P, n % QZ, 1, 0:ROWS[t]], qT[DB:P, hd, q]).then_inc(qz_done, 1)
                pool.wait_ge(qz_done, n + 1)
            pool.wait_ge(sqo_done, H * TILES)
            pool.memset(qT[HD:P, :, :], 0.0).then_inc(q_zeroed, 1)
            pool.wait_ge(q_zeroed, 1)
            for i in phase_items(latent):
                if items[i].kind == "norm":
                    factors(i)
                send(i)
            inverse_rms(r_o, ss_o, H * TILES, VB).then_inc(ro_done, 1)
            pool.wait_ge(ro_done, 1)
            pool.wait_ge(o_done["b"], H * TILES)
            for t in range(TILES):
                heads = gates[:, t, D:2 * D].rearrange("p (h v) -> p h v", v=VB)
                link(pool.tensor_tensor(heads, heads, r_o[:, t * H:t * H + H].unsqueeze(2).broadcast_to([P, H, VB]),
                                        ALU.mult))
                pool.tensor_tensor(heads, heads, gvec[:, gv["diff_sub"], :].unsqueeze(1).broadcast_to([P, H, VB]),
                                   ALU.mult).then_inc(sub_done, 1)
                pool.wait_ge(sub_done, t + 1)
            pool.wait_ge(s_done["a"], H * TILES)
            pool.memset(ptok[DEC:P, PT, :], 0.0).then_inc(zeroed, 1)
            pool.wait_ge(zeroed, 2)
            pool.wait_ge(t_copied, copied[("merged", TILE_ORDER[-1], 1)] + 1)
            pool.memset(h[DEC:P, PT, :], 0.0).then_inc(zeroed, 1)
            pool.wait_ge(zeroed, 3)
            late_gpsimd(pool, link, inverse_rms)


def constants():
    pos = np.concatenate([np.arange(SEQ), PAST + np.arange(DEC), np.zeros(TOK - SEQ - DEC)]).astype(np.float32)
    parts = []
    for r in (RD, ROT):
        half = r // 2
        inv = np.float32(ROPE_THETA) ** (-np.arange(half, dtype=np.float32) * np.float32(2.0 / r))
        ang = pos[:, None] * inv[None, :]
        c, s = np.cos(ang), np.sin(ang)
        parts += [c, c, -s, s]
    iota = np.zeros((1, 320), np.float32)
    iota[0, 0:P] = np.arange(P)
    iota[0, P:P + 32] = P * np.arange(32)
    iota[0, 160:192] = SLOTS * np.arange(32)
    iota[0, 192:192 + NE] = np.arange(NE)
    n = np.arange(TOK)
    valid = (n < SEQ + DEC).astype(np.float32)
    return {
        "c_ident": np.eye(P, dtype=np.float32),
        "c_rope": np.concatenate(parts, axis=1).astype(np.float32),
        "c_mask": np.concatenate([(np.arange(P) < CHUNK).astype(np.float32), np.full(CHUNK, -BIG, np.float32)])[None],
        "c_before": (np.arange(P)[:, None] < np.arange(P)[None, :]).astype(np.float32),
        "c_iota": iota,
        "c_token": np.stack([n + 1.0, valid, valid - 1.0], axis=1).astype(np.float32),
    }


def kernel(**inputs):
    from concourse import bacc
    from concourse.bass_utils import run_bass_kernel_spmd

    def flat(name, *shape):
        return np.ascontiguousarray(inputs[name]).reshape(shape)

    arrays = {
        "x": np.concatenate([flat("x_prompt", SEQ, D), flat("x_sample", DEC, D)]),
        "p": np.concatenate([flat("p_prompt", SEQ, DP), flat("p_sample", DEC, DP)]),
        "cache_ckv": flat("cache_mla_ckv", PAST, KVL), "cache_krope": flat("cache_mla_krope", PAST, RD),
        "cache_k": flat("cache_diff_k", PAST, D), "cache_v": flat("cache_diff_v", PAST, D),
        "w_in": flat("w_in", D, -1), "w_uq": flat("w_uq", QL, H * HD), "w_uk": flat("w_uk", KVL, H * NOPE),
        "w_uv": flat("w_uv", KVL, D), "w_out": flat("w_out", D, D),
        "w_rg": flat("w_router_grp", D, NG), "w_re": flat("w_router_exp", D, NE),
        "w_ei": flat("w_exp_in", NE * D, 2 * DE), "w_eo": flat("w_exp_out", NE * DE, D),
        "w_ple_gate": flat("w_ple_gate", D, D), "w_ple_proj": flat("w_ple_proj", DP, D),
        "b_rg": flat("b_router_grp", NG), "b_re": flat("b_router_exp", NE),
    }
    for g in ("g_mix", "g_q_lat", "g_kv_lat", "g_mla_qn", "g_mla_qr", "g_mla_kn", "g_mla_kr", "g_diff_q", "g_diff_k",
              "lambda_q1", "lambda_k1", "lambda_q2", "lambda_k2", "g_diff_sub", "g_ffn", "g_ple"):
        arrays[g] = flat(g, -1)
    arrays.update(constants())
    outs = {"y_p": (SEQ, D), "y_s": (DEC, D), "ckv_p": (SEQ, KVL), "kr_p": (SEQ, RD), "dk_p": (SEQ, D),
            "dv_p": (SEQ, D), "ckv_s": (DEC, KVL), "kr_s": (DEC, RD), "dk_s": (DEC, D), "dv_s": (DEC, D)}
    nc = bacc.Bacc("TRN2", target_bir_lowering=False, num_devices=1)
    a = {n: nc.dram_tensor("in_" + n, v.shape, mybir.dt.from_np(v.dtype), kind="ExternalInput").ap()
         for n, v in arrays.items()}
    o = {n: nc.dram_tensor("out_" + n, s, F32, kind="ExternalOutput").ap() for n, s in outs.items()}
    trunk(nc, a, o)
    r = run_bass_kernel_spmd(nc, [{"in_" + n: v for n, v in arrays.items()}], core_ids=[0]).results[0]
    g = {n: r["out_" + n] for n in outs}
    res = [g["y_p"].reshape(1, SEQ, D), g["y_s"].reshape(1, DEC, D)]
    for who, n in (("p", SEQ), ("s", DEC)):
        res += [g["ckv_" + who].reshape(1, 1, n, KVL), g["kr_" + who].reshape(1, 1, n, RD),
                g["dk_" + who].reshape(1, 1, n, H, 2, DB), g["dv_" + who].reshape(1, 1, n, H, VB)]
    return tuple(res)
```
